# Optimizing a Trainium2 kernel written in Bass

```python
import math
import jax, jax.numpy as jnp
from jax import lax
import numpy as np

D_MODEL = 2048
BATCH = 1
SEQ = 256
DEPTH = 2

GRID_W = 64
CTX_LEN = 256
N_MIXERS = 4
ROPE_BASE = 10000.0
EPS = 1e-6
NEG_INF = -1e30
BLOCK = 128
HEAD_DIM = 128

SWA_HEADS = D_MODEL // HEAD_DIM
SWA_KV_HEADS = SWA_HEADS // 4
SWA_WINDOW = BLOCK
SWA_WIDTH = SWA_HEADS * HEAD_DIM
SWA_IN = SWA_WIDTH + 2 * SWA_KV_HEADS * HEAD_DIM + SWA_WIDTH

MLA_HEADS = D_MODEL // HEAD_DIM
MLA_Q_RANK = 512
MLA_KV_RANK = 256
MLA_NOPE = 128
MLA_ROPE = 64
MLA_V = 128
MLA_WIDTH = MLA_HEADS * MLA_V
MLA_IN = MLA_Q_RANK + MLA_KV_RANK + MLA_ROPE + MLA_WIDTH

HYENA_WIDTH = D_MODEL
HYENA_ORDER = 2
HYENA_BANDS = 16
HYENA_EMB = 1 + 2 * HYENA_BANDS
HYENA_HIDDEN = 64
HYENA_CONV = 3
HYENA_DECAY_TARGET = 1e-2
HYENA_FAST_DECAY = 0.3
HYENA_SLOW_DECAY = 1.5
HYENA_IN = (HYENA_ORDER + 1) * HYENA_WIDTH + HYENA_WIDTH

DIFF_HEADS = D_MODEL // (2 * HEAD_DIM)
DIFF_WIDTH = DIFF_HEADS * 2 * HEAD_DIM
DIFF_IN = 4 * DIFF_WIDTH


def rmsnorm(x, g):
    xf = x.astype(jnp.float32)
    y = xf * lax.rsqrt(jnp.mean(xf * xf, axis=-1, keepdims=True) + EPS)
    return (y * g.astype(jnp.float32)).astype(x.dtype)

def axial_rope_tables(n_tok, rot_dim):
    rows = n_tok // GRID_W
    row = jnp.repeat(jnp.arange(rows, dtype=jnp.float32), GRID_W)
    col = jnp.tile(jnp.arange(GRID_W, dtype=jnp.float32), rows)
    half = rot_dim // 2
    inv = 1.0 / (ROPE_BASE ** (jnp.arange(0, half, 2, dtype=jnp.float32) / half))
    ar = row[:, None] * inv[None, :]
    ac = col[:, None] * inv[None, :]
    ang = jnp.concatenate([ar, ar, ac, ac], axis=-1)
    return jnp.cos(ang), jnp.sin(ang)

def apply_axial_rope(x, cos, sin):
    half = x.shape[-1] // 2
    qr = half // 2
    a, b = x[..., :half], x[..., half:]
    rot = jnp.concatenate([-a[..., qr:], a[..., :qr], -b[..., qr:], b[..., :qr]], axis=-1)
    return x * cos[:, None].astype(x.dtype) + rot * sin[:, None].astype(x.dtype)

def sweep_query_blocks(fn, *qs):
    B, N = qs[0].shape[:2]
    nb = N // BLOCK
    blocks = tuple(jnp.moveaxis(q.reshape((B, nb, BLOCK) + q.shape[2:]), 1, 0) for q in qs)
    out = lax.map(lambda a: fn(*a), blocks)
    return jnp.moveaxis(out, 0, 1).reshape((B, N) + out.shape[3:])

def swa_mixer(h, hc, w_in, q_g, k_g, sink, w_out, need_ctx):
    B, N, _ = h.shape
    C = hc.shape[1]
    Hq, Hk, d = SWA_HEADS, SWA_KV_HEADS, HEAD_DIM
    G = Hq // Hk
    cuts = [Hq * d, Hq * d + Hk * d, Hq * d + 2 * Hk * d]
    q, k, v, gate = jnp.split(h @ w_in, cuts, axis=-1)
    cos, sin = axial_rope_tables(N, d)
    q = apply_axial_rope(rmsnorm(q.reshape(B, N, Hq, d), q_g), cos, sin)
    k = apply_axial_rope(rmsnorm(k.reshape(B, N, Hk, d), k_g), cos, sin)
    v = v.reshape(B, N, Hk, d)
    if need_ctx:
        cq, ck, cv, cgate = jnp.split(hc @ w_in, cuts, axis=-1)
    else:
        ck, cv = jnp.split(hc @ w_in[:, cuts[0]:cuts[2]], 2, axis=-1)
    ck = rmsnorm(ck.reshape(B, C, Hk, d), k_g)
    cv = cv.reshape(B, C, Hk, d)
    scale = d ** -0.5
    sink_l = sink.astype(jnp.float32).reshape(Hk, G)
    nb = N // BLOCK

    def bands(t):
        tp = jnp.pad(t, ((0, 0), (BLOCK, BLOCK), (0, 0), (0, 0))).reshape(B, nb + 2, BLOCK, Hk, d)
        return jnp.concatenate([tp[:, :-2], tp[:, 1:-1], tp[:, 2:]], axis=2)

    kb, vb = bands(k), bands(v)
    qb = q.reshape(B, nb, BLOCK, Hk, G, d)
    qi = jnp.arange(BLOCK)[:, None]
    kj = jnp.arange(3 * BLOCK)[None, :]
    in_band = (kj >= qi + BLOCK - SWA_WINDOW) & (kj <= qi + BLOCK + SWA_WINDOW)
    kpos = (jnp.arange(nb)[:, None] - 1) * BLOCK + jnp.arange(3 * BLOCK)[None, :]
    mask = in_band[None] & ((kpos >= 0) & (kpos < N))[:, None, :]
    s_loc = jnp.einsum('bnqhgd,bnkhd->bnhgqk', qb, kb).astype(jnp.float32) * scale
    s_loc = jnp.where(mask[None, :, None, None], s_loc, NEG_INF)
    s_ctx = jnp.einsum('bnqhgd,bchd->bnhgqc', qb, ck).astype(jnp.float32) * scale
    s_sink = jnp.broadcast_to(sink_l[None, None, :, :, None, None], s_ctx.shape[:-1] + (1,))
    p = jax.nn.softmax(jnp.concatenate([s_loc, s_ctx, s_sink], axis=-1), axis=-1).astype(v.dtype)
    o = (jnp.einsum('bnhgqk,bnkhd->bnqhgd', p[..., :3 * BLOCK], vb)
         + jnp.einsum('bnhgqc,bchd->bnqhgd', p[..., 3 * BLOCK:3 * BLOCK + C], cv)).reshape(B, N, Hq * d)
    out = (o * jax.nn.silu(gate)) @ w_out
    out_c = None
    if need_ctx:
        cqh = rmsnorm(cq.reshape(B, C, Hq, d), q_g).reshape(B, C, Hk, G, d)
        sc = jnp.einsum('bqhgd,bkhd->bhgqk', cqh, ck).astype(jnp.float32) * scale
        sc_sink = jnp.broadcast_to(sink_l[None, :, :, None, None], sc.shape[:-1] + (1,))
        pc = jax.nn.softmax(jnp.concatenate([sc, sc_sink], axis=-1), axis=-1)[..., :C].astype(cv.dtype)
        oc = jnp.einsum('bhgqk,bkhd->bqhgd', pc, cv).reshape(B, C, Hq * d)
        out_c = (oc * jax.nn.silu(cgate)) @ w_out
    return out, out_c

def mla_attend(qn, qp, kn, kp, v):
    scale = (MLA_NOPE + MLA_ROPE) ** -0.5
    s = (jnp.einsum('bqhd,bkhd->bhqk', qn, kn) + jnp.einsum('bqhr,bkr->bhqk', qp, kp)).astype(jnp.float32) * scale
    p = jax.nn.softmax(s, axis=-1).astype(v.dtype)
    return jnp.einsum('bhqk,bkhd->bqhd', p, v)

def mla_mixer(h, hc, w_in, qa_g, kva_g, w_qb, w_kvb, qn_nope_g, qn_pe_g, kn_nope_g, kn_pe_g, w_out, need_ctx):
    B, N, _ = h.shape
    C = hc.shape[1]
    H = MLA_HEADS
    cuts = [MLA_Q_RANK, MLA_Q_RANK + MLA_KV_RANK, MLA_Q_RANK + MLA_KV_RANK + MLA_ROPE]

    def queries(c_q):
        S = c_q.shape[1]
        qf = (rmsnorm(c_q, qa_g) @ w_qb).reshape(B, S, H, MLA_NOPE + MLA_ROPE)
        return rmsnorm(qf[..., :MLA_NOPE], qn_nope_g), rmsnorm(qf[..., MLA_NOPE:], qn_pe_g)

    def keys_values(c_kv, k_rope):
        S = c_kv.shape[1]
        kv = (rmsnorm(c_kv, kva_g) @ w_kvb).reshape(B, S, H, MLA_NOPE + MLA_V)
        return rmsnorm(kv[..., :MLA_NOPE], kn_nope_g), rmsnorm(k_rope, kn_pe_g), kv[..., MLA_NOPE:]

    lat_cq, lat_ckv, lat_kr, gate = jnp.split(h @ w_in, cuts, axis=-1)
    q_nope, q_pe = queries(lat_cq)
    k_nope, k_pe, v = keys_values(lat_ckv, lat_kr)
    cos, sin = axial_rope_tables(N, MLA_ROPE)
    q_pe = apply_axial_rope(q_pe, cos, sin)
    k_pe = apply_axial_rope(k_pe[:, :, None], cos, sin)[:, :, 0]
    if need_ctx:
        ctx_cq, ctx_ckv, ctx_kr, cgate = jnp.split(hc @ w_in, cuts, axis=-1)
    else:
        ctx_ckv, ctx_kr = jnp.split(hc @ w_in[:, cuts[0]:cuts[2]], [MLA_KV_RANK], axis=-1)
    ck_nope, ck_pe, cv = keys_values(ctx_ckv, ctx_kr)
    kn_all = jnp.concatenate([k_nope, ck_nope], axis=1)
    kp_all = jnp.concatenate([k_pe, ck_pe], axis=1)
    v_all = jnp.concatenate([v, cv], axis=1)
    o = sweep_query_blocks(lambda a, b: mla_attend(a, b, kn_all, kp_all, v_all), q_nope, q_pe)
    out = (o.reshape(B, N, MLA_WIDTH) * jax.nn.silu(gate)) @ w_out
    out_c = None
    if need_ctx:
        cq_nope, cq_pe = queries(ctx_cq)
        oc = mla_attend(cq_nope, cq_pe, ck_nope, ck_pe, cv).reshape(B, C, MLA_WIDTH)
        out_c = (oc * jax.nn.silu(cgate)) @ w_out
    return out, out_c

def centred_conv3(u, w, b):
    up = jnp.pad(u, ((0, 0), (1, 1), (0, 0)))
    return up[:, :-2] * w[0] + up[:, 1:-1] * w[1] + up[:, 2:] * w[2] + b

def hyena_filter_spectrum(L, f_w1, f_b1, f_w2, f_b2, f_freq, f_w3):
    f32 = jnp.float32
    pos = jnp.arange(L, dtype=f32)
    t = pos / max(L - 1, 1)
    bands = jnp.linspace(1e-4, HYENA_BANDS - 1, HYENA_BANDS, dtype=f32)
    ang = (2.0 * math.pi / L) * pos[:, None] * bands[None, :]
    z = jnp.concatenate([t[:, None], jnp.cos(ang), -jnp.sin(ang)], axis=-1)
    freq = f_freq.astype(f32)
    hf = jnp.sin(freq[0] * (z @ f_w1.astype(f32) + f_b1.astype(f32)))
    hf = jnp.sin(freq[1] * (hf @ f_w2.astype(f32) + f_b2.astype(f32)))
    hf = (hf @ f_w3.astype(f32)).reshape(L, HYENA_ORDER, 2, HYENA_WIDTH)
    max_decay = math.log(HYENA_DECAY_TARGET) / HYENA_FAST_DECAY
    min_decay = math.log(HYENA_DECAY_TARGET) / HYENA_SLOW_DECAY
    deltas = jnp.abs(jnp.linspace(min_decay, max_decay, HYENA_WIDTH, dtype=f32))
    hf = hf * jnp.exp(-t[:, None] * deltas[None, :])[:, None, None, :]
    fwd = hf[:, :, 0]
    bwd = hf[:0:-1, :, 1]
    kc = jnp.concatenate([fwd, jnp.zeros((1, HYENA_ORDER, HYENA_WIDTH), f32), bwd], axis=0)
    kc = kc * lax.rsqrt(jnp.sum(kc * kc, axis=0, keepdims=True) + EPS)
    return jnp.fft.rfft(kc, axis=0)

def bidir_fftconv(u, spec, skip):
    L = u.shape[1]
    y = jnp.fft.irfft(jnp.fft.rfft(u, n=2 * L, axis=1) * spec[None], n=2 * L, axis=1)[:, :L]
    return y + u * skip

def hyena_branch(hin, w_in, conv_w, conv_b, f_w1, f_b1, f_w2, f_b2, f_freq, f_w3, skip, w_out):
    L = hin.shape[1]
    proj = hin @ w_in
    u, gate = proj[..., :(HYENA_ORDER + 1) * HYENA_WIDTH], proj[..., (HYENA_ORDER + 1) * HYENA_WIDTH:]
    u = centred_conv3(u, conv_w, conv_b).astype(jnp.float32)
    v, x1, x2 = jnp.split(u, 3, axis=-1)
    spec = hyena_filter_spectrum(L, f_w1, f_b1, f_w2, f_b2, f_freq, f_w3)
    sk = skip.astype(jnp.float32)
    z = x1 * bidir_fftconv(v, spec[:, 0], sk[0])
    z = x2 * bidir_fftconv(z, spec[:, 1], sk[1])
    return (z.astype(hin.dtype) * jax.nn.silu(gate)) @ w_out

def diff_attend(q, k, v, lam):
    s = jnp.einsum('bqhid,bkhid->bihqk', q, k).astype(jnp.float32) * (HEAD_DIM ** -0.5)
    p = jax.nn.softmax(s, axis=-1)
    a = (p[:, 0] - lam * p[:, 1]).astype(v.dtype)
    return jnp.einsum('bhqk,bkhe->bqhe', a, v)

def diff_mixer(h, hc, w_in, q_g, k_g, lq1, lk1, lq2, lk2, subln_g, w_out, lam_init, need_ctx):
    B, N, _ = h.shape
    C = hc.shape[1]
    H, d, W = DIFF_HEADS, HEAD_DIM, DIFF_WIDTH
    f32 = jnp.float32

    def qk(t, g):
        return rmsnorm(t.reshape(B, t.shape[1], H, 2, d), g)

    q, k, v, gate = jnp.split(h @ w_in, 4, axis=-1)
    cos, sin = axial_rope_tables(N, d)

    def rope2(t):
        return apply_axial_rope(t.reshape(B, N, 2 * H, d), cos, sin).reshape(B, N, H, 2, d)

    q = rope2(qk(q, q_g))
    k = rope2(qk(k, k_g))
    v = v.reshape(B, N, H, 2 * d)
    if need_ctx:
        cq, ck, cv, cgate = jnp.split(hc @ w_in, 4, axis=-1)
    else:
        ck, cv = jnp.split(hc @ w_in[:, W:3 * W], 2, axis=-1)
    ck = qk(ck, k_g)
    cv = cv.reshape(B, C, H, 2 * d)
    lam = (jnp.exp(jnp.sum(lq1.astype(f32) * lk1.astype(f32)))
           - jnp.exp(jnp.sum(lq2.astype(f32) * lk2.astype(f32))) + lam_init)
    k_all = jnp.concatenate([k, ck], axis=1)
    v_all = jnp.concatenate([v, cv], axis=1)

    def finish(o, g):
        o = (rmsnorm(o, subln_g) * (1.0 - lam_init)).reshape(B, o.shape[1], W)
        return (o * jax.nn.silu(g)) @ w_out

    o = sweep_query_blocks(lambda qb: diff_attend(qb, k_all, v_all, lam), q)
    out = finish(o, gate)
    out_c = None
    if need_ctx:
        out_c = finish(diff_attend(qk(cq, q_g), ck, cv, lam), cgate)
    return out, out_c

def first_inputs(seed: int = 0) -> dict:
    key = jax.random.key(seed)
    ks = iter(jax.random.split(key, 64))
    f32 = jnp.float32

    def nrm(shape, std):
        return jax.random.normal(next(ks), shape, f32) * std

    def gain(shape):
        return 1.0 + nrm(shape, 0.05)

    nA, nB, nC, nD = (len(range(m, DEPTH, N_MIXERS)) for m in range(N_MIXERS))
    D = D_MODEL
    d = HEAD_DIM
    W = HYENA_WIDTH
    return {
        'x': nrm((BATCH, SEQ, D), 1.0),
        'c': nrm((BATCH, D), 1.0),
        'ctx': nrm((BATCH, CTX_LEN, D), 1.0),
        'c_ctx': nrm((D,), 1.0),
        'norm_g': gain((DEPTH, D)),
        'ada_w': nrm((DEPTH, D, 3 * D), 0.5 * D ** -0.5),
        'ada_b': nrm((DEPTH, 3 * D), 0.02),
        'swa_w_in': nrm((nA, D, SWA_IN), D ** -0.5),
        'swa_q_g': gain((nA, d)),
        'swa_k_g': gain((nA, d)),
        'swa_sink': nrm((nA, SWA_HEADS), 1.0),
        'swa_w_out': nrm((nA, SWA_WIDTH, D), SWA_WIDTH ** -0.5),
        'mla_w_in': nrm((nB, D, MLA_IN), D ** -0.5),
        'mla_qa_g': gain((nB, MLA_Q_RANK)),
        'mla_kva_g': gain((nB, MLA_KV_RANK)),
        'mla_w_qb': nrm((nB, MLA_Q_RANK, MLA_HEADS * (MLA_NOPE + MLA_ROPE)), MLA_Q_RANK ** -0.5),
        'mla_w_kvb': nrm((nB, MLA_KV_RANK, MLA_HEADS * (MLA_NOPE + MLA_V)), MLA_KV_RANK ** -0.5),
        'mla_qn_nope_g': gain((nB, MLA_NOPE)),
        'mla_qn_pe_g': gain((nB, MLA_ROPE)),
        'mla_kn_nope_g': gain((nB, MLA_NOPE)),
        'mla_kn_pe_g': gain((nB, MLA_ROPE)),
        'mla_w_out': nrm((nB, MLA_WIDTH, D), MLA_WIDTH ** -0.5),
        'hyena_w_in': nrm((nC, D, HYENA_IN), D ** -0.5),
        'hyena_conv_w': nrm((nC, HYENA_CONV, (HYENA_ORDER + 1) * W), 0.5),
        'hyena_conv_b': nrm((nC, (HYENA_ORDER + 1) * W), 0.02),
        'hyena_f_w1': nrm((nC, HYENA_EMB, HYENA_HIDDEN), HYENA_EMB ** -0.5),
        'hyena_f_b1': nrm((nC, HYENA_HIDDEN), 0.2),
        'hyena_f_w2': nrm((nC, HYENA_HIDDEN, HYENA_HIDDEN), HYENA_HIDDEN ** -0.5),
        'hyena_f_b2': nrm((nC, HYENA_HIDDEN), 0.2),
        'hyena_f_freq': gain((nC, 2, HYENA_HIDDEN)),
        'hyena_f_w3': nrm((nC, HYENA_HIDDEN, HYENA_ORDER * 2 * W), HYENA_HIDDEN ** -0.5),
        'hyena_skip': nrm((nC, HYENA_ORDER, W), 0.5),
        'hyena_w_out': nrm((nC, W, D), W ** -0.5),
        'diff_w_in': nrm((nD, D, DIFF_IN), D ** -0.5),
        'diff_q_g': gain((nD, d)),
        'diff_k_g': gain((nD, d)),
        'diff_lq1': nrm((nD, d), 0.1),
        'diff_lk1': nrm((nD, d), 0.1),
        'diff_lq2': nrm((nD, d), 0.1),
        'diff_lk2': nrm((nD, d), 0.1),
        'diff_subln_g': gain((nD, 2 * d)),
        'diff_w_out': nrm((nD, DIFF_WIDTH, D), DIFF_WIDTH ** -0.5),
    }

def first_block(x, c, ctx, c_ctx, norm_g, ada_w, ada_b,
              swa_w_in, swa_q_g, swa_k_g, swa_sink, swa_w_out,
              mla_w_in, mla_qa_g, mla_kva_g, mla_w_qb, mla_w_kvb,
              mla_qn_nope_g, mla_qn_pe_g, mla_kn_nope_g, mla_kn_pe_g, mla_w_out,
              hyena_w_in, hyena_conv_w, hyena_conv_b, hyena_f_w1, hyena_f_b1, hyena_f_w2,
              hyena_f_b2, hyena_f_freq, hyena_f_w3, hyena_skip, hyena_w_out,
              diff_w_in, diff_q_g, diff_k_g, diff_lq1, diff_lk1, diff_lq2, diff_lk2,
              diff_subln_g, diff_w_out):
    cond = jax.nn.silu(c)[:, None, :]
    cond_ctx = jax.nn.silu(c_ctx)
    for i in range(DEPTH):
        kind, j = i % N_MIXERS, i // N_MIXERS
        need_ctx = i < DEPTH - 1
        shift, scale, gate = jnp.split(cond @ ada_w[i] + ada_b[i], 3, axis=-1)
        h = rmsnorm(x, norm_g[i]) * (1.0 + scale) + shift
        hc = None
        if need_ctx or kind != 2:
            shift_c, scale_c, gate_c = jnp.split(cond_ctx @ ada_w[i] + ada_b[i], 3, axis=-1)
            hc = rmsnorm(ctx, norm_g[i]) * (1.0 + scale_c) + shift_c
        if kind == 0:
            o, oc = swa_mixer(h, hc, swa_w_in[j], swa_q_g[j], swa_k_g[j], swa_sink[j], swa_w_out[j], need_ctx)
        elif kind == 1:
            o, oc = mla_mixer(h, hc, mla_w_in[j], mla_qa_g[j], mla_kva_g[j], mla_w_qb[j], mla_w_kvb[j],
                              mla_qn_nope_g[j], mla_qn_pe_g[j], mla_kn_nope_g[j], mla_kn_pe_g[j],
                              mla_w_out[j], need_ctx)
        elif kind == 2:
            hy = (hyena_w_in[j], hyena_conv_w[j], hyena_conv_b[j], hyena_f_w1[j], hyena_f_b1[j],
                  hyena_f_w2[j], hyena_f_b2[j], hyena_f_freq[j], hyena_f_w3[j], hyena_skip[j], hyena_w_out[j])
            o = hyena_branch(h, *hy)
            oc = hyena_branch(hc, *hy) if need_ctx else None
        else:
            lam_init = 0.8 - 0.6 * math.exp(-0.3 * i)
            o, oc = diff_mixer(h, hc, diff_w_in[j], diff_q_g[j], diff_k_g[j], diff_lq1[j], diff_lk1[j],
                               diff_lq2[j], diff_lk2[j], diff_subln_g[j], diff_w_out[j], lam_init, need_ctx)
        x = x + gate * o
        if need_ctx:
            ctx = ctx + gate_c * oc
    return x


N_MIXERS_2 = 2
POOL_WINDOWS = (2, 4, 8, 16)
N_POOL_GROUPS = 4
POOL_GROUP_DIM = D_MODEL // N_POOL_GROUPS
ATTN_PATTERNS = ((128, 1), (512, 4), (2048, 16))
N_ATTN_GROUPS = 3
N_SLOTS = 8
GROUP_WIDTH = N_SLOTS * HEAD_DIM
QKV_WIDTH = 3 * N_ATTN_GROUPS * GROUP_WIDTH
N_TOTAL_HEADS = N_ATTN_GROUPS * N_SLOTS
D_FF = 4 * D_MODEL
LN_EPS = 1e-5
DEEPNORM_ALPHA = (2 * DEPTH) ** 0.25
DEEPNORM_BETA = (8 * DEPTH) ** -0.25
N_POOL_LAYERS = (DEPTH + 1) // 2
N_ATTN_LAYERS = DEPTH // 2


def layer_norm(x, g, b):
    xf = x.astype(jnp.float32)
    mu = jnp.mean(xf, axis=-1, keepdims=True)
    xc = xf - mu
    var = jnp.mean(xc * xc, axis=-1, keepdims=True)
    y = xc * lax.rsqrt(var + LN_EPS) * g.astype(jnp.float32) + b.astype(jnp.float32)
    return y.astype(x.dtype)

def alibi_slopes():
    n = N_TOTAL_HEADS
    return jnp.exp2(-8.0 * jnp.arange(1, n + 1, dtype=jnp.float32) / n).reshape(N_ATTN_GROUPS, N_SLOTS)

def pool_mixer(x, w_in, w_group, scale, w_out):
    B, S, D = x.shape
    u = (x @ w_in).reshape(B, S, N_POOL_GROUPS, POOL_GROUP_DIM)
    uf = u.astype(jnp.float32)
    cs = jnp.cumsum(uf, axis=1)
    t = jnp.arange(S)
    outs = []
    for g, w in enumerate(POOL_WINDOWS):
        c = cs[:, :, g]
        lagged = jnp.pad(c, ((0, 0), (w, 0), (0, 0)))[:, :S]
        cnt = jnp.minimum(t + 1, w).astype(jnp.float32)[:, None]
        outs.append((c - lagged) / cnt - uf[:, :, g])
    p = jnp.stack(outs, axis=2).astype(x.dtype)
    y = jnp.einsum('bsgc,gcd->bsgd', p, w_group).reshape(B, S, D) * scale
    return y @ w_out

def strided_window_attention(q, k, v, dil, n_back, slopes):
    B, S, H, E = q.shape
    L = S // dil
    nb = -(-L // BLOCK)
    Lp = nb * BLOCK
    N = B * dil

    def to_blocks(a):
        a = a.reshape(B, L, dil, H, E).transpose(0, 2, 1, 3, 4).reshape(N, L, H, E)
        a = jnp.pad(a, ((0, 0), (0, Lp - L), (0, 0), (0, 0)))
        return a.reshape(N, nb, BLOCK, H, E)

    def with_prev(a):
        prev = jnp.pad(a, ((0, 0), (1, 0), (0, 0), (0, 0), (0, 0)))[:, :nb]
        return jnp.concatenate([prev, a], axis=2)

    def from_blocks(a):
        rest = a.shape[3:]
        a = a.reshape((B, dil, Lp) + rest)[:, :, :L]
        a = jnp.moveaxis(a, 1, 2)
        return a.reshape((B, S) + rest)

    qb = to_blocks(q)
    kw = with_prev(to_blocks(k))
    vw = with_prev(to_blocks(v))
    s = jnp.einsum('nbqhe,nbkhe->nbhqk', qb, kw, preferred_element_type=jnp.float32)
    s = s * (1.0 / math.sqrt(E))
    qi = jnp.arange(BLOCK)[:, None]
    ki = jnp.arange(2 * BLOCK)[None, :]
    dist = qi + BLOCK - ki
    blk = jnp.arange(nb)[:, None, None]
    valid = ((dist >= 0) & (dist <= n_back))[None] & ((blk > 0) | (ki[None] >= BLOCK))
    bias = -slopes[:, None, None] * (dist * dil).astype(jnp.float32)[None]
    s = s + bias[None, None]
    s = jnp.where(valid[None, :, None], s, -jnp.inf)
    m = jnp.max(s, axis=-1, keepdims=True)
    e = jnp.exp(s - m)
    den = jnp.sum(e, axis=-1, keepdims=True)
    p = e / den
    lse = (m + jnp.log(den))[..., 0]
    o = jnp.einsum('nbhqk,nbkhe->nbqhe', p.astype(v.dtype), vw,
                   preferred_element_type=jnp.float32)
    return from_blocks(o), from_blocks(jnp.swapaxes(lse, 2, 3))

def dilated_attention(x, w_qkv, w_out):
    B, S, D = x.shape
    qkv = (x @ w_qkv).reshape(B, S, 3, N_ATTN_GROUPS, N_SLOTS, HEAD_DIM)
    slopes = alibi_slopes()
    outs, lses = [], []
    for g, (w, d) in enumerate(ATTN_PATTERNS):
        o, lse = strided_window_attention(qkv[:, :, 0, g], qkv[:, :, 1, g], qkv[:, :, 2, g],
                                          d, w // d, slopes[g])
        outs.append(o)
        lses.append(lse)
    wts = jax.nn.softmax(jnp.stack(lses, axis=0), axis=0)
    merged = jnp.einsum('gbsh,gbshe->bshe', wts, jnp.stack(outs, axis=0)).astype(x.dtype)
    return merged.reshape(B, S, GROUP_WIDTH) @ w_out

def sqrelu_mlp(x, w_up, w_down):
    h = jax.nn.relu(x @ w_up)
    return (h * h) @ w_down

def second_inputs(seed: int = 0) -> dict:
    key = jax.random.key(seed)
    ks = jax.random.split(key, 14)
    f32 = jnp.float32
    nrm = lambda k, shape, s: jax.random.normal(k, shape, f32) * s
    x = jax.random.normal(ks[0], (BATCH, SEQ, D_MODEL), f32)
    pool_w_in = nrm(ks[1], (N_POOL_LAYERS, D_MODEL, D_MODEL), D_MODEL ** -0.5)
    pool_w_group = nrm(ks[2], (N_POOL_LAYERS, N_POOL_GROUPS, POOL_GROUP_DIM, POOL_GROUP_DIM), POOL_GROUP_DIM ** -0.5)
    pool_scale = 1.0 + nrm(ks[3], (N_POOL_LAYERS, D_MODEL), 0.1)
    pool_w_out = nrm(ks[4], (N_POOL_LAYERS, D_MODEL, D_MODEL), DEEPNORM_BETA * D_MODEL ** -0.5)
    attn_w_qkv = nrm(ks[5], (N_ATTN_LAYERS, D_MODEL, QKV_WIDTH), D_MODEL ** -0.5)
    attn_w_out = nrm(ks[6], (N_ATTN_LAYERS, GROUP_WIDTH, D_MODEL), DEEPNORM_BETA * GROUP_WIDTH ** -0.5)
    mlp_w_up = nrm(ks[7], (DEPTH, D_MODEL, D_FF), D_MODEL ** -0.5)
    mlp_w_down = nrm(ks[8], (DEPTH, D_FF, D_MODEL), DEEPNORM_BETA * D_FF ** -0.5)
    ln_mix_g = 1.0 + nrm(ks[9], (DEPTH, D_MODEL), 0.05)
    ln_mix_b = nrm(ks[10], (DEPTH, D_MODEL), 0.02)
    ln_mlp_g = 1.0 + nrm(ks[11], (DEPTH, D_MODEL), 0.05)
    ln_mlp_b = nrm(ks[12], (DEPTH, D_MODEL), 0.02)
    return {"x": x, "pool_w_in": pool_w_in, "pool_w_group": pool_w_group, "pool_scale": pool_scale,
            "pool_w_out": pool_w_out, "attn_w_qkv": attn_w_qkv, "attn_w_out": attn_w_out,
            "mlp_w_up": mlp_w_up, "mlp_w_down": mlp_w_down, "ln_mix_g": ln_mix_g, "ln_mix_b": ln_mix_b,
            "ln_mlp_g": ln_mlp_g, "ln_mlp_b": ln_mlp_b}

def second_block(x, pool_w_in, pool_w_group, pool_scale, pool_w_out, attn_w_qkv, attn_w_out,
              mlp_w_up, mlp_w_down, ln_mix_g, ln_mix_b, ln_mlp_g, ln_mlp_b):
    for i in range(DEPTH):
        j = i // N_MIXERS_2
        if i % N_MIXERS_2 == 0:
            h = pool_mixer(x, pool_w_in[j], pool_w_group[j], pool_scale[j], pool_w_out[j])
        else:
            h = dilated_attention(x, attn_w_qkv[j], attn_w_out[j])
        x = layer_norm(DEEPNORM_ALPHA * x + h, ln_mix_g[i], ln_mix_b[i])
        x = layer_norm(DEEPNORM_ALPHA * x + sqrelu_mlp(x, mlp_w_up[i], mlp_w_down[i]),
                       ln_mlp_g[i], ln_mlp_b[i])
    return x


def setup_inputs(seed=0):
    out = dict(first_inputs(seed))
    for name, value in second_inputs(seed + 1).items():
        if name != "x":
            out[name + "_2"] = value
    return out


def reference(
    x, c, ctx, c_ctx, norm_g, ada_w, ada_b, swa_w_in, swa_q_g, swa_k_g, swa_sink, swa_w_out,
    mla_w_in, mla_qa_g, mla_kva_g, mla_w_qb, mla_w_kvb, mla_qn_nope_g, mla_qn_pe_g,
    mla_kn_nope_g, mla_kn_pe_g, mla_w_out, hyena_w_in, hyena_conv_w, hyena_conv_b, hyena_f_w1,
    hyena_f_b1, hyena_f_w2, hyena_f_b2, hyena_f_freq, hyena_f_w3, hyena_skip, hyena_w_out,
    diff_w_in, diff_q_g, diff_k_g, diff_lq1, diff_lk1, diff_lq2, diff_lk2, diff_subln_g,
    diff_w_out, pool_w_in_2, pool_w_group_2, pool_scale_2, pool_w_out_2, attn_w_qkv_2,
    attn_w_out_2, mlp_w_up_2, mlp_w_down_2, ln_mix_g_2, ln_mix_b_2, ln_mlp_g_2, ln_mlp_b_2,
):
    x = first_block(
        x, c, ctx, c_ctx, norm_g, ada_w, ada_b, swa_w_in, swa_q_g, swa_k_g, swa_sink, swa_w_out,
        mla_w_in, mla_qa_g, mla_kva_g, mla_w_qb, mla_w_kvb, mla_qn_nope_g, mla_qn_pe_g,
        mla_kn_nope_g, mla_kn_pe_g, mla_w_out, hyena_w_in, hyena_conv_w, hyena_conv_b,
        hyena_f_w1, hyena_f_b1, hyena_f_w2, hyena_f_b2, hyena_f_freq, hyena_f_w3, hyena_skip,
        hyena_w_out, diff_w_in, diff_q_g, diff_k_g, diff_lq1, diff_lk1, diff_lq2, diff_lk2,
        diff_subln_g, diff_w_out,
    )
    return second_block(
        x, pool_w_in_2, pool_w_group_2, pool_scale_2, pool_w_out_2, attn_w_qkv_2, attn_w_out_2,
        mlp_w_up_2, mlp_w_down_2, ln_mix_g_2, ln_mix_b_2, ln_mlp_g_2, ln_mlp_b_2,
    )


_drawn_inputs = setup_inputs


def setup_inputs(seed=0):
    import zlib

    import numpy as np

    out = dict(_drawn_inputs(seed))
    spreads = {}
    factors = {'ctx': 3.417,
     'norm_g': 8.0,
     'ada_b': 7.43,
     'swa_q_g': 8.0,
     'swa_k_g': 8.0,
     'swa_sink': 8.0,
     'mla_qa_g': 8.0,
     'mla_kva_g': 8.0,
     'mla_w_qb': 3.19,
     'mla_qn_nope_g': 8.0,
     'mla_qn_pe_g': 8.0,
     'mla_kn_nope_g': 8.0,
     'mla_kn_pe_g': 8.0}
    for name, (base, spread) in spreads.items():
        noise = np.random.default_rng([zlib.crc32(name.encode()), seed]).standard_normal(out[name].shape)
        drawn = base * np.exp(spread * noise) if base else spread * noise
        out[name] = __import__('jax').numpy.asarray(drawn.astype(out[name].dtype))
    for name, factor in factors.items():
        out[name] = (out[name] * factor).astype(out[name].dtype)
    return out
```

```python
from contextlib import ExitStack
import math

import numpy as np

import concourse.bass as bass
from concourse import mybir

F32 = mybir.dt.float32
F32R = mybir.dt.float32r
I32 = mybir.dt.int32
ACT = mybir.ActivationFunctionType
ALU = mybir.AluOpType
AX = mybir.AxisListType.X

P = 128
D = 2048
KC = D // P
TOK = 256
TT = TOK // P
PW = 512
TW = 2048
HD = 128
EPS = 1e-6
LN_EPS = 1e-5
ALPHA = (2 * 2) ** 0.25
NEG = -1e30
N_SLOTS = 8
N_GROUPS = 3
POOL_WINDOWS = (2, 4, 8, 16)
SWA_SCALE = HD ** -0.5
MLA_SCALE = (128 + 64) ** -0.5
MLA_KVW = 320
QBW = 384


def stages():
    table = [("ada0", 12, 4, 1), ("swa_kv", 2, 4, 4), ("swa_qg", 8, 4, 4), ("swa_out", 4, 4, 4),
             ("ada1", 12, 4, 1), ("mla_cq", 1, 4, 2), ("mla_ckv", 1, 4, 4), ("mla_gate", 4, 4, 2),
             ("mla_pair", 8, 2, 6), ("mla_out", 4, 4, 2), ("pool_in", 4, 4, 2), ("pool_group", 4, 1, 2),
             ("pool_out", 4, 4, 2), ("up00", 8, 4, 2), ("down00", 4, 8, 2), ("up01", 8, 4, 2),
             ("down01", 4, 8, 2), ("qkv", 18, 4, 2), ("attn_out", 4, 2, 2), ("up10", 8, 4, 2),
             ("down10", 4, 8, 2), ("up11", 8, 4, 2), ("down11", 4, 8, 2)]
    out, tile, acc, used = {}, 0, 0, 0
    for name, n, tpp, na in table:
        out[name] = Stage(name, n, tpp, na, tile, acc, used)
        tile += n * tpp
        acc += n * na
        used += 0 if name == "mla_pair" else n * (tpp - 1)
    return out, tile


class Stage:

    def __init__(self, name, n, tpp, na, tile, acc, used):
        self.name, self.n, self.tpp, self.na = name, n, tpp, na
        self.tile, self.acc, self.used = tile, acc, used


def need(eng, sem, value):
    if isinstance(value, int) and value <= 0:
        return
    eng.wait_ge(sem, value)


def each(eng, lo, hi, body):
    with eng.Fori(0, hi - lo) as i:
        body(i + lo)


def col(i, n, w=PW):
    if isinstance(i, int):
        return slice(i * w, i * w + n)
    return bass.ds(i * w, n)


class Chain:

    def __init__(self, eng, sem):
        self.eng, self.sem, self.n, self.off = eng, sem, 0, 0

    def __call__(self, ins):
        self.tick(ins)
        self.wait()

    def tick(self, ins):
        ins.then_inc(self.sem, 1)
        self.n += 1

    def wait(self):
        self.eng.wait_ge(self.sem, self.n + self.off)


def counted_loop(eng, chains, lo, hi, body, per):
    starts = [c.n for c in chains]
    with eng.Fori(0, hi - lo) as i:
        for c, n in zip(chains, per):
            c.off = i * n
        body(i + lo)
    for c, n, start in zip(chains, per, starts):
        assert c.n - start == n, [(c.n - s) for c, s in zip(chains, starts)]
        c.off, c.n = 0, start + n * (hi - lo)


def turns():
    table = [("mod0", 8), ("kT", 2), ("q0", 2), ("swa", 30), ("swa_tail", 8), ("og0", 8), ("gate0", 4),
             ("mod1", 8), ("cq", 1), ("ckv", 1), ("kpe", 1), ("mla0", 2), ("mla", 28), ("mla_tail", 2),
             ("og1", 4), ("gate1", 2), ("pool", 4), ("band", 4), ("py", 4), ("ln0", 4), ("up00", 8),
             ("up01", 8), ("ln1", 4), ("qk0", 6), ("att0", 8), ("qk1", 6), ("att1", 8), ("ao", 2),
             ("ln2", 4), ("up10", 8), ("up11", 8)]
    out, n = {}, 0
    for name, k in table:
        out[name] = n
        n += k
    return out


def halves():
    table = [("mod0", 16), ("og0", 16), ("mod1", 16), ("cq", 2), ("ckv", 2), ("og1", 8), ("pool", 8),
             ("band", 8), ("py", 8), ("ln0", 8), ("up00", 16), ("up01", 16), ("ln1", 8), ("ao", 4),
             ("ln2", 8), ("up10", 16), ("up11", 16)]
    out, n = {}, 0
    for name, k in table:
        out[name] = n
        n += k
    return out


CONSTS = [("ident", P), ("selrow", 2 * P), ("selcol", 2), ("cond", 2 * KC), ("normg", 2 * KC), ("sink", 16)]
KEYS = (P, 2 * P)


def dil_parts(tt):
    if tt == 0:
        return [(0, 0), (1, 0)], [(2, 0)]
    blocks = [(g, kt) for g in range(N_GROUPS) for kt in range(2)]
    return blocks[:3], blocks[3:]


def program(nc, a, out):
    ST, NT = stages()
    TB, HB = turns(), halves()
    with ExitStack() as ctx:
        base = -(-nc.sbuf_base // 64) * 64
        arena = 229344 - base - 64
        ctx.enter_context(nc.sbuf_tensor("arena", [P, arena // 4], F32))

        def at(name, off, shape, dt=F32):
            n = int(np.prod(shape[1:])) * 4
            assert off + n <= arena, (name, off, n, arena)
            return nc.alloc_sbuf_tensor_at(name, shape, dt, offset=base + off)

        R_RAW, R_HI, R_LO = 0, 32768, 49152
        R_1H, R_1L, R_2, R_X, R_M = 65536, 98304, 131072, 163840, 196608
        raw = at("raw", R_RAW, [P, 4, TW])
        whi = at("whi", R_HI, [P, 2, TW], F32R)
        wlo = at("wlo", R_LO, [P, 2, TW], F32R)
        h4 = [at(n, r, [P, KC, 4 * P], F32R) for n, r in (("h4_hi", R_1H), ("h4_lo", R_1L))]
        hw = [at(n, r, [P, 32, TOK], F32R) for n, r in (("hw_hi", R_1H), ("hw_lo", R_1L))]
        x2 = [at(n, r, [P, KC, TOK], F32R) for n, r in (("x2_hi", R_2), ("x2_lo", R_2 + 16384))]
        X = at("X", R_X, [P, 4, D])
        off = [R_M]

        def keep(name, shape, dt=F32):
            t = at(name, off[0], shape, dt)
            off[0] += -(-int(np.prod(shape[1:])) * 4 // 32) * 32
            return t

        ident = keep("ident", [P, P])
        selrow = keep("selrow", [5, 2, P])
        selcol = keep("selcol", [5, 2])
        cond = keep("cond", [P, 2, KC])
        condh = keep("condh", [P, 2, KC], F32R)
        normg = keep("normg", [P, 2, KC])
        modA = keep("modA", [P, 2, KC])
        modB = keep("modB", [P, 2, KC])
        sink = keep("sink", [P, 16])
        nsink = keep("nsink", [P, 16])
        ssq = keep("ssq", [P, 4])
        hss = keep("hss", [P, 16])
        ms = keep("ms", [P, 16])
        nt = keep("nt", [P, 16])
        hrs = keep("hrs", [P, 16])
        mx = keep("mx", [P, 2])
        nm = keep("nm", [P, 2])
        rs = keep("rs", [P, 4])
        es = keep("es", [P, 4])
        den = keep("den", [P, 2])
        rden = keep("rden", [P, 2])
        bn = keep("bn", [P, 4, 6])
        mv = keep("mv", [P, 2])
        nmr = keep("nmr", [P, 1])
        zero = keep("zero", [P, 1])
        waited = keep("waited", [P, 1])
        assert off[0] - R_M <= 4096, off[0] - R_M
        M1, M2 = R_M + 4096, R_M + 4096 + 8192
        gaterow = at("gaterow", M1, [5, D])
        adarow = at("adarow", R_2, [5, 3 * D])
        condL = at("condL", R_2 + 24576, [P, KC, P], F32R)
        tmod = at("tmod", R_2, [P, 2, 512])
        scr = at("scr", R_1L, [P, D])
        XN = at("XN", M2, [P, 2, D])
        G0 = at("G0", R_2, [P, 4, D])
        QS = at("QS", R_X, [P, 4, PW])
        qT = at("qT", R_X + 8192, [P, 4, 4 * P])
        kT = at("kT", R_X + 16384, [P, 4, 4 * P])
        V0 = at("V0", R_X + 24576, [P, 4, PW])
        masks = at("masks", M2, [P, 7 * P])
        tabs = at("tabs", M2 + 3584, [P, 2, TT, 2, HD])
        gqk = at("gqk", M2 + 7680, [P, 2, 2, HD])
        Sb = at("Sb", M2 + 9728, [P, 2, 512])
        PTb = at("PTb", M2 + 13824, [P, 4, P])
        SQ = at("SQ", M2 + 15872, [P, PW])
        gateB = at("gateB", M2, [P, 2, D])
        rtmp = at("rtmp", M2 + 16384, [P, PW])
        G1 = at("G1", R_2, [P, TT, D])
        cqT = [at(n, r, [P, 4, TOK], F32R) for n, r in (("cqT_hi", R_2 + 16384), ("cqT_lo", R_2 + 20480))]
        ckvT = [at(n, r, [P, 2, 512], F32R) for n, r in (("ckvT_hi", R_2 + 24576), ("ckvT_lo", R_2 + 28672))]
        cqS = at("cqS", R_X + 16384, [P, TT, 512])
        ckvS = at("ckvS", R_X + 20480, [P, 4, MLA_KVW])
        sqS = at("sqS", R_X + 26112, [P, 512])
        rtab = at("rtab", M2, [P, 2, TT, 2, 64])
        gpe = at("gpe", M2 + 2048, [P, 2, 2, 64])
        gqa = at("gqa", M2 + 3072, [P, 512])
        gkva = at("gkva", M2 + 5120, [P, 256])
        gnope = at("gnope", M2 + 6144, [P, 2, HD])
        gprod = at("gprod", M2 + 7168, [P, HD])
        kpT = at("kpT", M2 + 7680, [64, 4 * P])
        KV = at("KV", R_1H, [P, 2, 4, 512])
        QP = at("QP", R_1H + 16384, [P, TT, QBW])
        kTp = at("kTp", R_1H + 20480, [P, 2, 4 * P])
        qTp = at("qTp", R_1H + 24576, [P, 2, TOK])
        qpT = at("qpT", R_1H + 26624, [64, 2, TOK])
        Sm = at("Sm", R_1L, [P, 2, 512])
        PTm = at("PTm", R_1L + 4096, [P, 4, P])
        SQm = at("SQm", R_1L + 8192, [P, 1024])
        og1 = [at(n, r, [P, KC, TOK], F32R) for n, r in (("og1_hi", R_1H), ("og1_lo", R_1L))]
        gateB1 = at("gateB1", M2, [P, D])
        U = at("U", M1, [P, TT, D])
        bands = at("bands", R_X + 16384, [P, 4, TT, TOK])
        scaleB = at("scaleB", R_X + 24576, [P, D])
        pT = [at(n, r, [P, KC, TOK], F32R) for n, r in (("pT_hi", R_1H), ("pT_lo", R_1L))]
        yT = [at(n, r, [P, KC, TOK], F32R) for n, r in (("yT_hi", R_1H + 16384), ("yT_lo", R_1L + 16384))]
        lnB = at("lnB", M1, [P, 2, D])
        HS = at("HS", R_X + 16384, [P, TT, PW])
        qA = at("qA", R_1H, [P, N_GROUPS * 4, TOK])
        kA = at("kA", R_1H + 12288, [P, N_GROUPS * 4, TOK])
        SA = at("SA", R_1H + 24576, [P, 2, N_GROUPS * TOK])
        VA = at("VA", R_1L, [P, TT, N_GROUPS * 4 * HD])
        PTa = at("PTa", R_1L + 12288, [P, 6, P])
        OA = at("OA", R_1L + 16384, [P, TT, N_SLOTS * HD])
        ndm = at("ndm", R_X + 20480, [P, N_GROUPS, KEYS[0] + KEYS[1]])
        oT = [at(n, r, [P, 8, TOK], F32R) for n, r in (("oT_hi", R_2), ("oT_lo", R_2 + 8192))]

        PS = ctx.enter_context(nc.psum_tensor("PS", [P, 8, 512], F32))

        def sem(name):
            return ctx.enter_context(nc.semaphore(name))

        raw_landed = [sem(f"raw_landed{j}") for j in range(4)]
        hi_done, lo_done, tile_used = sem("hi_done"), sem("lo_done"), sem("tile_used")
        acc_full, acc_free = sem("acc_full"), sem("acc_free")
        tr_full = [sem("tr_full0"), sem("tr_full1")]
        tr_free = [sem("tr_free0"), sem("tr_free1")]
        split_hi, mod_lo = sem("split_hi"), sem("mod_lo")
        dve_chain, act_chain = sem("dve_chain"), sem("act_chain")
        consts_in, cond_in, x_in, x_again, bias_in = (sem(n) for n in ("consts_in", "cond_in", "x_in", "x_again", "bias_in"))
        swa_in_, mla_in_, pool_in_, ln_in, ndm_in = (sem(n) for n in ("swa_in", "mla_in", "pool_in", "ln_in", "ndm_in"))
        out_done = sem("out_done")
        cond_hi, cond_ready, ss_ready, xn_ready = (sem(n) for n in ("cond_hi", "cond_ready", "ss_ready", "xn_ready"))
        cols_full, mod_ready, gate_kept = sem("cols_full"), sem("mod_ready"), sem("gate_kept")
        x_freed = sem("x_freed")
        qk_ready, lat_ready, pair_ready = sem("qk_ready"), sem("lat_ready"), sem("pair_ready")
        x_ready, sq_ready = sem("x_ready"), sem("sq_ready")
        final = sem("final")
        names = ("s_full", "s_free", "m_ready", "p_ready", "o_full", "o_free")
        swa, mla, dil = ({n: sem(f"{k}_{n}") for n in names} for k in ("swa", "mla", "dil"))

        def tile_at(st, b, q, k):
            n = q * st.tpp + k
            span = max(4, st.tpp) // 4
            return st.tile // 4 + b * span + n // 4, n % 4

        def panel(st, b, q):
            return b if st.tpp >= 4 else b * (4 // st.tpp) + q

        def width(I, j, default=TW):
            if not isinstance(I, int):
                return default
            T = 4 * I + j
            if 0 <= T - ST["mla_ckv"].tile < 4:
                return 4 * MLA_KVW
            if 0 <= T - ST["mla_pair"].tile < 16:
                return (4 * QBW, 2 * PW)[T % 2]
            return TW

        def consumed(st, b, q, k):
            n = panel(st, b, q)
            if st.name == "mla_pair":
                return acc_full, st.acc + n * st.na + (2, 6)[k]
            if k == st.tpp - 1:
                return acc_full, st.acc + (n + 1) * st.na
            return tile_used, st.used + n * (st.tpp - 1) + k + 1

        block = ctx.enter_context(nc.Block())

        @block.sync
        def _(sp):
            sp.dma_start(cond[:], a["cond"]).then_inc(cond_in, 16)
            for j in range(4):
                sp.dma_start(raw[:, j, :], a["weights"][j]).then_inc(raw_landed[j], 16)
                if j == 0:
                    sp.dma_start(adarow[4:5, :], a["ada_b"][0]).then_inc(bias_in, 16)
                    sp.dma_start(X[:], a["x"]).then_inc(x_in, 16)
            w = a["weights"].rearrange("(i j) p n -> i j p n", j=4)

            def refill(i):
                for j in range(4):
                    sp.wait_ge(lo_done, 4 * i + j + 1)
                    sp.dma_start(raw[:, j, :], w[bass.ds(i + 1, 1), j].rearrange("a p n -> (a p) n")).then_inc(raw_landed[j], 16)

            each(sp, 0, NT // 4 - 1, refill)
            sp.wait_ge(final, TT)
            sp.dma_start(out, X[:, 0:TT, :]).then_inc(out_done, 16)
            sp.wait_ge(out_done, 16)

        @block.tensor
        def _(pe):
            mm, tr = nc.tensor.matmul, nc.tensor.transpose

            def tile_mm(st, b, q, k, lhs, banks, nch, w, tts, K, kc0, n0, slot=None):
                I, j = tile_at(st, b, q, k)
                pe.wait_ge(lo_done, 4 * I + j + 1)
                for tt in tts:
                    bank = PS[:, banks[tt], 0:w]
                    if kc0 == 0:
                        need(pe, acc_free, n0 + tt - len(set(banks)) + 1)
                    for c in range(nch):
                        kc = kc0 + c
                        wh = whi[:, j % 2, c * w:(c + 1) * w]
                        wl = wlo[:, j % 2, c * w:(c + 1) * w]
                        if st.name.startswith("ada"):
                            mm(bank, condL[:, kc, :], wh, start=(kc == 0), stop=False)
                            last = mm(bank, condL[:, kc, :], wl, start=False, stop=(kc == K - 1))
                            continue
                        xh, xl = (x[:, kc, tt * P:(tt + 1) * P] for x in lhs)
                        mm(bank, xh, wh, start=(kc == 0), stop=False)
                        mm(bank, xl, wh, start=False, stop=False)
                        last = mm(bank, xh, wl, start=False, stop=(kc == K - 1))
                    if kc0 + nch == K:
                        last.then_inc(acc_full, 1)
                    elif tt == tts[-1]:
                        last.then_inc(tile_used, 1)
                    if slot:
                        slot(k, tt)

            def gemm(st, b, lhs, q=0, w=PW, kc=0, slot=None):
                K = 4 * st.tpp
                n = panel(st, b, q)
                view = [x[:, kc:kc + K, :] for x in lhs] if lhs else None
                for k in range(st.tpp):
                    tile_mm(st, b, q, k, view, list(range(st.na)), 4, w, list(range(st.na)), K, 4 * k,
                            st.acc + n * st.na, slot)

            def bank_free(K, j):
                need(pe, tr_free[j], K)

            def turn(K, j, blocks, rows=P, waited=False):
                if not waited:
                    bank_free(K, j)
                for n, blk in enumerate(blocks):
                    last = tr(PS[0:rows, 4 + j, n * P:(n + 1) * P], blk, ident[:])
                last.then_inc(tr_full[j], 1)

            def turned(K):
                for j in range(2):
                    pe.wait_ge(tr_free[j], K)

            def modulation(layer):
                st = ST[f"ada{layer}"]
                pe.wait_ge(acc_free, st.acc + st.n)
                pe.wait_ge(bias_in, 16 * (layer + 1))
                for c in range(2 * KC):
                    last = mm(PS[:, 7, 2 * c:2 * c + 2], adarow[:, c * P:(c + 1) * P], selcol[:],
                              start=True, stop=True)
                last.then_inc(cols_full, 1)

            def turn_rows(part, src):
                for c in range(KC):
                    turn(TB[part] + c // 2, c % 2, [src(tt, c) for tt in range(4)])

            def turn_pairs(part, src, chunks=KC, first=0):
                for u in range(chunks // 2):
                    turn(TB[part] + first + u // 2, u % 2,
                         [src(tt, 2 * u + c) for c in range(2) for tt in range(TT)])

            def gate_rows(part, which):
                u = 0
                pe.wait_ge(gate_kept, 1 if part == "gate0" else 2)
                for s in which:
                    for p in range(4):
                        K, j = TB[part] + u // 2, u % 2
                        bank_free(K, j)
                        mm(PS[:, 4 + j, :], selrow[:, s, :], gaterow[:, p * PW:(p + 1) * PW],
                           start=True, stop=True).then_inc(tr_full[j], 1)
                        u += 1

            pe.wait_ge(cond_ready, 1)
            gemm(ST["ada0"], 0, None)
            each(pe, 1, 12, lambda i: gemm(ST["ada0"], i, None))
            pe.wait_ge(consts_in, 16 * (len(CONSTS) - 1))
            modulation(0)
            pe.wait_ge(xn_ready, 4)
            turn_rows("mod0", lambda tt, c: X[:, tt, c * P:(c + 1) * P])
            pe.wait_ge(mod_lo, 16)

            st = ST["swa_kv"]
            pe.wait_ge(acc_free, st.acc)
            for i in range(2):
                gemm(st, i, h4)
            pe.wait_ge(qk_ready, 4)

            def turn_heads(K):
                for h in range(4):
                    turn(K + h // 2, h % 2, [QS[:, tt, h * HD:(h + 1) * HD] for tt in range(4)])

            turn_heads(TB["kT"])

            def swa_scores(g, u):
                h, tt = u // 4, u % 4
                n = 16 * g + u
                if u == 0:
                    turned(TB["q0"] + 2 + 10 * g)
                need(pe, swa["s_free"], n)
                kg = kT[:, col(g, 1, 1), :].rearrange("p a n -> p (a n)")
                keys = kg[:, 0:512] if tt < TT else kg[:, 256:512]
                mm(PS[:, 6, 0:keys.shape[-1]], qT[:, h, tt * P:(tt + 1) * P], keys,
                   start=True, stop=True).then_inc(swa["s_full"], 1)

            def swa_turn(g, u, K):
                tt = u % 4
                pe.wait_ge(swa["p_ready"], 16 * g + u + 1)
                turn(K + u // 2, u % 2, [Sb[:, u % 2, c * P:(c + 1) * P] for c in range(4 if tt < TT else 2)])

            def swa_pv(g, u, K):
                tt = u % 4
                n = 16 * g + u
                pe.wait_ge(tr_free[u % 2], K + u // 2 + 1)
                need(pe, swa["o_free"], n)
                tiles = range(4) if tt < TT else range(TT, 4)
                for c, kt in enumerate(tiles):
                    last = mm(PS[:, 7, 0:HD], PTb[:, c, :], V0[:, kt, col(g, HD, HD)],
                              start=(c == 0), stop=(c == len(tiles) - 1))
                last.then_inc(swa["o_full"], 1)

            def swa_step(g, n, K):
                if n < 16:
                    swa_scores(g, n)
                if 1 <= n < 17:
                    swa_turn(g, n - 1, K)
                if 2 <= n:
                    swa_pv(g, n - 2, K)

            st = ST["swa_qg"]
            gemm(st, 0, h4)
            gemm(st, 1, h4)
            pe.wait_ge(qk_ready, 8)
            turn_heads(TB["q0"])

            def swa_group(i):
                K = TB["swa"] + 10 * (i - 1)
                gemm(st, 2 * i, h4, slot=lambda k, tt: swa_step(i - 1, 4 * k + tt, K))
                swa_step(i - 1, 16, K)
                swa_step(i - 1, 17, K)
                gemm(st, 2 * i + 1, h4)
                pe.wait_ge(qk_ready, 8 + 4 * i)
                turn_heads(K + 8)

            each(pe, 1, 4, swa_group)
            for n in range(18):
                swa_step(3, n, TB["swa_tail"])
            pe.wait_ge(swa["o_free"], 64)
            turn_rows("og0", lambda tt, c: G0[:, tt, c * P:(c + 1) * P])
            gate_rows("gate0", (0, 1))
            turned(TB["og0"] + 8)
            st = ST["swa_out"]
            pe.wait_ge(acc_free, st.acc)
            each(pe, 0, 4, lambda i: gemm(st, i, h4))

            st = ST["ada1"]
            pe.wait_ge(cond_ready, 2)
            pe.wait_ge(acc_free, st.acc)
            each(pe, 0, 12, lambda i: gemm(st, i, None))
            modulation(1)
            pe.wait_ge(xn_ready, 8)
            turn_rows("mod1", lambda tt, c: (XN if tt < TT else X)[:, tt, c * P:(c + 1) * P])
            pe.wait_ge(mod_lo, 32)

            pe.wait_ge(acc_free, ST["mla_cq"].acc)
            gemm(ST["mla_cq"], 0, h4)
            pe.wait_ge(acc_free, ST["mla_ckv"].acc)
            gemm(ST["mla_ckv"], 0, h4, w=MLA_KVW)
            pe.wait_ge(acc_free, ST["mla_gate"].acc)
            gemm(ST["mla_gate"], 0, h4)
            pe.wait_ge(lat_ready, 3)
            turn_pairs("cq", lambda tt, c: cqS[:, tt, c * P:(c + 1) * P], 4)
            for c in range(2):
                turn(TB["ckv"], c, [ckvS[:, tt, c * P:(c + 1) * P] for tt in range(4)])
            for c in range(2):
                turn(TB["kpe"], c, [ckvS[:, 2 * c + t, 256:320] for t in range(2)], rows=64)
            each(pe, 1, 4, lambda i: gemm(ST["mla_gate"], i, h4))
            turned(TB["mla0"])

            st = ST["mla_pair"]
            pe.wait_ge(acc_free, st.acc)

            def pair_mm(b, q):
                n0 = st.acc + panel(st, b, q) * 6
                bank = lambda m: (6 * q + m) % 4
                for k, (m0, tts, lhs, w) in enumerate(((0, 2, cqT, QBW), (2, 4, ckvT, PW))):
                    I, j = tile_at(st, b, q, k)
                    pe.wait_ge(lo_done, 4 * I + j + 1)
                    nch = 4 if k == 0 else 2
                    for tt in range(tts):
                        pe.wait_ge(acc_free, n0 + m0 + tt - 3)
                        o = PS[:, bank(m0 + tt), 0:w]
                        for c in range(nch):
                            wh, wl = (t[:, j % 2, c * w:(c + 1) * w] for t in (whi, wlo))
                            xh, xl = (x[:, c, tt * P:(tt + 1) * P] for x in lhs)
                            mm(o, xh, wh, start=(c == 0), stop=False)
                            mm(o, xl, wh, start=False, stop=False)
                            last = mm(o, xh, wl, start=False, stop=(c == nch - 1))
                        last.then_inc(acc_full, 1)

            def pair_turn(p, q, K):
                pe.wait_ge(pair_ready, p + 1)
                for h in range(2):
                    turn(K, h, [KV[:, q, tt, h * 256:h * 256 + P] for tt in range(4)])
                bank_free(K + 1, 1)
                turn(K + 1, 0, [QP[:, tt, h * 192:h * 192 + P] for h in range(2) for tt in range(TT)])
                turn(K + 1, 1, [QP[:, tt, h * 192 + P:(h + 1) * 192] for h in range(2) for tt in range(TT)], rows=64, waited=True)

            def mla_step(p, q, m, K):
                if m < 4:
                    h, tt = m // 2, m % 2
                    if m == 0:
                        turned(K)
                    need(pe, mla["s_free"], 4 * p + m)
                    mm(PS[:, 6, :], qTp[:, h, tt * P:(tt + 1) * P], kTp[:, h, :], start=True, stop=False)
                    mm(PS[:, 6, :], qpT[:, h, tt * P:(tt + 1) * P], kpT[:], start=False,
                       stop=True).then_inc(mla["s_full"], 1)
                if 1 <= m < 5:
                    u = m - 1
                    pe.wait_ge(mla["p_ready"], 4 * p + u + 1)
                    turn(K + u // 2, u % 2, [Sm[:, u % 2, c * P:(c + 1) * P] for c in range(4)])
                if 2 <= m:
                    u = m - 2
                    h = u // 2
                    pe.wait_ge(tr_free[u % 2], K + u // 2 + 1)
                    need(pe, mla["o_free"], 4 * p + u)
                    for c in range(4):
                        last = mm(PS[:, 7, 0:HD], PTm[:, c, :], KV[:, q, c, h * 256 + P:(h + 1) * 256],
                                  start=(c == 0), stop=(c == 3))
                    last.then_inc(mla["o_full"], 1)

            def mla_att(p, q, K):
                for m in range(6):
                    mla_step(p, q, m, K)

            def mla_body(b):
                for q in range(2):
                    p = 2 * b + q
                    K = TB["mla"] + 4 * (p - 1)
                    pair_mm(b, q)
                    mla_att(p - 1, 1 - q, K)
                    pair_turn(p, q, K + 2)

            pair_mm(0, 0)
            pair_turn(0, 0, TB["mla0"])
            pair_mm(0, 1)
            mla_att(0, 0, TB["mla"])
            pair_turn(1, 1, TB["mla"] + 2)
            each(pe, 1, 4, mla_body)
            mla_att(7, 1, TB["mla_tail"])
            pe.wait_ge(mla["o_free"], 32)
            turn_pairs("og1", lambda tt, c: G1[:, tt, c * P:(c + 1) * P])
            gate_rows("gate1", (0,))
            turned(TB["og1"] + 4)
            st = ST["mla_out"]
            pe.wait_ge(acc_free, st.acc)
            each(pe, 0, 4, lambda i: gemm(st, i, og1))

            def turn_x(part, number):
                need(pe, x_ready, number)
                turn_pairs(part, lambda tt, c: X[:, tt, c * P:(c + 1) * P])
                turned(TB[part] + 4)

            st = ST["pool_in"]
            pe.wait_ge(acc_free, st.acc)
            turn_x("pool", 0)

            def pooled(g):
                pe.wait_ge(acc_free, ST["pool_in"].acc + 2 * (g + 1))
                for u in range(2):
                    K, j = TB["band"] + g, u
                    bank_free(K, j)
                    for c in range(2):
                        f = g * PW + (2 * u + c) * P
                        o = PS[:, 4 + j, c * TOK:(c + 1) * TOK]
                        mm(o, U[:, 0, f:f + P], bands[:, g, 0, :], start=True, stop=False, skip_group_check=True)
                        last = mm(o[:, P:], U[:, 1, f:f + P], bands[:, g, 1, P:], start=False, stop=True,
                                  skip_group_check=True)
                    last.then_inc(tr_full[j], 1)

            for g in range(4):
                gemm(st, g, x2)
                if g == 0:
                    pe.wait_ge(pool_in_, 32)
                if g:
                    pooled(g - 1)
            pooled(3)
            st = ST["pool_group"]
            pe.wait_ge(acc_free, st.acc)
            for g in range(4):
                turned(TB["band"] + g + 1)
                gemm(st, g // 4, pT, q=g, kc=4 * g)
                if g:
                    pe.wait_ge(acc_free, st.acc + 2 * g)
                    turn_pairs("py", lambda tt, c: U[:, tt, (g - 1) * PW + c * P:(g - 1) * PW + (c + 1) * P], 4, g - 1)
            pe.wait_ge(acc_free, st.acc + 8)
            turn_pairs("py", lambda tt, c: U[:, tt, 3 * PW + c * P:3 * PW + (c + 1) * P], 4, 3)
            turned(TB["py"] + 4)
            st = ST["pool_out"]
            pe.wait_ge(acc_free, st.acc)
            each(pe, 0, 4, lambda i: gemm(st, i, yT))

            def mlp(layer, sq0):
                for half in range(2):
                    up, down = ST[f"up{layer}{half}"], ST[f"down{layer}{half}"]
                    K0, s0 = TB[up.name], sq0 + 16 * half

                    def turn_panel(i, k=1, tt=1):
                        if (k, tt) == (1, 1):
                            pe.wait_ge(sq_ready, s0 + 2 * i + 2)
                            for u in range(2):
                                turn(K0 + i, u, [HS[:, t, (2 * u + c) * P:(2 * u + c + 1) * P]
                                                 for c in range(2) for t in range(TT)])

                    pe.wait_ge(acc_free, up.acc)
                    gemm(up, 0, x2)
                    each(pe, 1, 8, lambda i: gemm(up, i, x2, slot=lambda k, tt: turn_panel(i - 1, k, tt)))
                    pe.wait_ge(acc_free, down.acc)
                    turned(K0 + 7)

                    def last_turned(k, tt):
                        turn_panel(7, k, tt)
                        if (k, tt) == (6, 1):
                            turned(K0 + 8)

                    gemm(down, 0, hw, slot=last_turned)
                    each(pe, 1, 4, lambda i: gemm(down, i, hw))

            turn_x("ln0", TT)
            mlp(0, 0)
            turn_x("ln1", 2 * TT)
            st = ST["qkv"]
            pe.wait_ge(acc_free, st.acc)

            def dil_step(hf, m, K):
                n = 8 * hf + m
                if m < 8:
                    s, tt = m // 2, m % 2
                    nk = KEYS[tt]
                    need(pe, dil["s_free"], n)
                    for g in range(N_GROUPS):
                        last = mm(PS[:, 2 + g // 2, (g % 2) * TOK:(g % 2) * TOK + nk], qA[:, 4 * g + s, tt * P:(tt + 1) * P],
                                  kA[:, 4 * g + s, 0:nk], start=True, stop=True, skip_group_check=True)
                    last.then_inc(dil["s_full"], 1)
                if 1 <= m < 9:
                    u = m - 1
                    tt = u % 2
                    pe.wait_ge(dil["p_ready"], 8 * hf + u + 1)
                    for j, part in enumerate(dil_parts(tt)):
                        turn(K + u, j, [SA[:, u % 2, g * TOK + kt * P:g * TOK + (kt + 1) * P] for g, kt in part])
                if 2 <= m:
                    u = m - 2
                    s, tt = u // 2, u % 2
                    for j in range(2):
                        pe.wait_ge(tr_free[j], K + u + 1)
                    need(pe, dil["o_free"], 8 * hf + u)
                    blocks = [x for part in dil_parts(tt) for x in part]
                    for c, (g, kt) in enumerate(blocks):
                        last = mm(PS[:, 7, 0:HD], PTa[:, c, :], VA[:, kt, (4 * g + s) * HD:(4 * g + s + 1) * HD],
                                  start=(c == 0), stop=(c == len(blocks) - 1))
                    last.then_inc(dil["o_full"], 1)

            for hf in range(2):
                def turn_qk(K, n):
                    pe.wait_ge(acc_free, n)
                    for u in range(2):
                        turn(K, u, [HS[:, t, (2 * u + c) * HD:(2 * u + c + 1) * HD] for c in range(2) for t in range(TT)])

                def group(g):
                    i = 9 * hf + 3 * g
                    K = TB[f"qk{hf}"] + 2 * g
                    gemm(st, i, x2)
                    gemm(st, i + 1, x2, slot=lambda k, tt: turn_qk(K, st.acc + 2 * i + 2) if (k, tt) == (0, 1) else None)
                    gemm(st, i + 2, x2, slot=lambda k, tt: turn_qk(K + 1, st.acc + 2 * i + 4) if (k, tt) == (0, 1) else None)

                each(pe, 0, N_GROUPS, group)
                turned(TB[f"att{hf}"])
                pe.wait_ge(acc_free, st.acc + 18 * (hf + 1))
                for m in range(10):
                    dil_step(hf, m, TB[f"att{hf}"])
            pe.wait_ge(dil["o_free"], 16)
            turn_pairs("ao", lambda tt, c: OA[:, tt, c * P:(c + 1) * P], 8)
            turned(TB["ao"] + 2)
            st = ST["attn_out"]
            pe.wait_ge(acc_free, st.acc)

            def out_body(b):
                for q in range(2):
                    gemm(st, b, oT, q=q)

            each(pe, 0, 2, out_body)
            turn_x("ln2", 3 * TT)
            mlp(1, 32)

        @block.scalar
        def _(act):
            f = nc.scalar.activation

            def copy(dst, src):
                return f(dst, src, ACT.Copy)

            def upper(I, j, b=None, st=None, q=0, k=0, w=TW):
                act.wait_ge(raw_landed[j], 16 * (I + 1))
                if st is not None:
                    act.wait_ge(*consumed(st, b, q, k))
                w = width(I, j, w)
                copy(whi[:, j % 2, 0:w], raw[:, j, 0:w]).then_inc(hi_done, 1)

            def panel_act(st, b, q=0, evac=None, slot=None, tail=None, final=False):
                n = panel(st, b, q)
                for k in range(st.tpp):
                    if slot:
                        slot(k)
                    if evac and st.name == "mla_pair":
                        for m in ((0, 1), (2, 3, 4, 5))[k]:
                            act.wait_ge(acc_full, st.acc + n * st.na + m + 1)
                            evac(m).then_inc(acc_free, 1)
                    elif evac and k == st.tpp - 1:
                        for tt in range(st.na):
                            act.wait_ge(acc_full, st.acc + n * st.na + tt + 1)
                            evac(tt).then_inc(acc_free, 1)
                    if tail and k == st.tpp - 1:
                        tail()
                    I, j = tile_at(st, b, q, k)
                    j += 2
                    w = TW
                    if st.name == "mla_pair":
                        w = (4 * QBW, 2 * PW)[k]
                    if not (final and k >= st.tpp - 2):
                        upper(I + j // 4, j % 4, b, st, q, k, w)

            def split(K, j, hi):
                act.wait_ge(tr_full[j], K + 1)
                width_ = hi.shape[-1] * (hi.shape[1] if len(hi.shape) == 3 else 1)
                src = PS[:, 4 + j, 0:width_]
                if len(hi.shape) == 3:
                    src = src.rearrange("p (c t) -> p c t", c=hi.shape[1])
                copy(hi, src).then_inc(split_hi, 1)

            def take(K, j, dst, src):
                act.wait_ge(tr_full[j], K + 1)
                copy(dst, src).then_inc(tr_free[j], 1)

            def load(dst, src, s):
                act.dma_start(dst, src).then_inc(s, 16)

            for (name, _), t in zip(CONSTS, (ident, selrow, selcol, cond, normg, sink)):
                if name != "cond":
                    load(t[:], a[name], consts_in)
            load(masks[:], a["masks"], swa_in_)
            for w in range(2):
                load(tabs[:, w], a["rope128"], swa_in_)
            load(gqk[:], a["gqk"], swa_in_)

            act.wait_ge(cond_in, 16)
            f(cond[:], cond[:], ACT.Silu).then_inc(act_chain, 1)
            act.wait_ge(act_chain, 1)
            copy(condh[:], cond[:]).then_inc(cond_hi, 1)
            upper(0, 0)
            upper(0, 1)

            def squares(tt, done=0):
                need(act, ss_ready, done + tt)
                f(scr[:], X[:, tt, :], ACT.Square, accum_out=ssq[:, tt:tt + 1]).then_inc(ss_ready, 1)

            def row_evac(i):
                return lambda tt: copy(adarow[0:4, col(i, PW)], PS[0:4, 0, :])

            def stats0(k):
                if k == 0:
                    act.wait_ge(x_in, 16)
                squares(k)

            panel_act(ST["ada0"], 0, evac=row_evac(0), slot=stats0)
            each(act, 1, 12, lambda i: panel_act(ST["ada0"], i, evac=row_evac(i)))

            def mod_split(part):
                for c in range(KC):
                    K, j = TB[part] + c // 2, c % 2
                    act.wait_ge(tr_free[j], K + 1)
                    copy(h4[0][:, c, :], tmod[:, j, :]).then_inc(split_hi, 1)

            mod_split("mod0")
            st = ST["swa_kv"]
            panel_act(st, 0, evac=lambda tt: copy(QS[:, tt, :], PS[:, tt, :]))
            panel_act(st, 1, evac=lambda tt: copy(V0[:, tt, :], PS[:, tt, :]))

            def take_heads(K, dst):
                for h in range(4):
                    take(K + h // 2, h % 2, dst[:, h, :], PS[:, 4 + h % 2, :])

            take_heads(TB["kT"], kT)

            def q_evac(tt):
                return copy(QS[:, tt, :], PS[:, tt, :])

            def g_evac(i):
                return lambda tt: f(G0[:, tt, col(i, PW)], PS[:, tt, :], ACT.Silu)

            def swa_step(g, n, K):
                if n < 16:
                    b, nk = n % 2, (512 if n % 4 < TT else 256)
                    act.wait_ge(swa["m_ready"], 16 * g + n + 1)
                    f(Sb[:, b, 0:nk], Sb[:, b, 0:nk], ACT.Exp, bias=nm[:, b:b + 1], scale=SWA_SCALE,
                      accum_out=rs[:, n % 4:n % 4 + 1])
                    f(es[:, n % 4:n % 4 + 1], sink[:, col(4 * g + n // 4, 1, 1)], ACT.Exp,
                      bias=nm[:, b:b + 1]).then_inc(swa["p_ready"], 1)
                if 1 <= n < 17:
                    u = n - 1
                    nk = 512 if u % 4 < TT else 256
                    need(act, swa["o_full"], 16 * g + u)
                    take(K + u // 2, u % 2, PTb[:, 0:nk // P, :],
                         PS[:, 4 + u % 2, 0:nk].rearrange("p (c t) -> p c t", c=nk // P))

            st = ST["swa_qg"]
            panel_act(st, 0, evac=q_evac)
            panel_act(st, 1, evac=g_evac(0))
            take_heads(TB["q0"], qT)

            def swa_group(i):
                K = TB["swa"] + 10 * (i - 1)

                def slot(k):
                    for tt in range(4):
                        swa_step(i - 1, 4 * k + tt, K)

                panel_act(st, 2 * i, evac=q_evac, slot=slot, tail=lambda: swa_step(i - 1, 16, K))
                panel_act(st, 2 * i + 1, evac=g_evac(i))
                take_heads(K + 8, qT)

            each(act, 1, 4, swa_group)
            for n in range(17):
                swa_step(3, n, TB["swa_tail"])

            def og_split(part, u0, u1, hi):
                for u in range(u0, u1):
                    split(TB[part] + u // 2, u % 2, hi(u))

            og_split("og0", 0, 1, lambda u: h4[0][:, u, :])
            load(X[:], a["x"], x_again)
            og_split("og0", 1, KC, lambda u: h4[0][:, u, :])
            load(adarow[4:5, :], a["ada_b"][1], bias_in)
            for u in range(8):
                take(TB["gate0"] + u // 2, u % 2, gateB[:, u // 4, u % 4 * PW:(u % 4 + 1) * PW], PS[:, 4 + u % 2, :])
            each(act, 0, 4, lambda i: panel_act(ST["swa_out"], i))

            def stats1(k):
                if k == 0:
                    act.wait_ge(acc_free, ST["ada1"].acc)
                squares(k, 4)

            panel_act(ST["ada1"], 0, evac=row_evac(0), slot=stats1)
            each(act, 1, 12, lambda i: panel_act(ST["ada1"], i, evac=row_evac(i)))
            mod_split("mod1")
            load(gpe[:], a["gpe"], mla_in_)
            for w in range(2):
                load(rtab[:, w], a["rope64"], mla_in_)
            load(gqa[:], a["gqa"], mla_in_)
            load(gkva[:], a["gkva"], mla_in_)
            load(gnope[:], a["gnope"], mla_in_)
            panel_act(ST["mla_cq"], 0, evac=lambda tt: copy(cqS[:, tt, :], PS[:, tt, :]))
            panel_act(ST["mla_ckv"], 0, evac=lambda tt: copy(ckvS[:, tt, :], PS[:, tt, 0:MLA_KVW]))

            def g1_evac(i):
                return lambda tt: f(G1[:, tt, col(i, PW)], PS[:, tt, :], ACT.Silu)

            st = ST["mla_gate"]
            panel_act(st, 0, evac=g1_evac(0))
            for u in range(2):
                split(TB["cq"], u, cqT[0][:, 2 * u:2 * u + 2, :])
            for u in range(2):
                split(TB["ckv"], u, ckvT[0][:, u, :])
            for u in range(2):
                take(TB["kpe"], u, kpT[:, u * TOK:(u + 1) * TOK], PS[0:64, 4 + u, 0:TOK])
            each(act, 1, 3, lambda i: panel_act(st, i, evac=g1_evac(i)))
            panel_act(st, 3, evac=g1_evac(3))

            st = ST["mla_pair"]

            def pair_evac(q):
                def evac(m):
                    bank = (6 * q + m) % 4
                    if m < 2:
                        return copy(QP[:, m, :], PS[:, bank, 0:QBW])
                    return copy(KV[:, q, m - 2, :], PS[:, bank, :])
                return evac

            def pair_take(K):
                for h in range(2):
                    take(K, h, kTp[:, h, :], PS[:, 4 + h, :])
                take(K + 1, 0, qTp[:].rearrange("p h t -> p (h t)"), PS[:, 4, :])
                take(K + 1, 1, qpT[:].rearrange("p h t -> p (h t)"), PS[0:64, 5, :])

            def mla_att(p, K):
                for m in range(5):
                    if m < 4:
                        b = m % 2
                        act.wait_ge(mla["m_ready"], 4 * p + m + 1)
                        f(Sm[:, b, :], Sm[:, b, :], ACT.Exp, bias=nm[:, b:b + 1], scale=MLA_SCALE,
                          accum_out=rs[:, m:m + 1]).then_inc(mla["p_ready"], 1)
                    if m:
                        u = m - 1
                        need(act, mla["o_full"], 4 * p + u)
                        take(K + u // 2, u % 2, PTm[:], PS[:, 4 + u % 2, :].rearrange("p (c t) -> p c t", c=4))

            def mla_body(b):
                for q in range(2):
                    K = TB["mla"] + 4 * (2 * b + q - 1)
                    panel_act(st, b, q, evac=pair_evac(q))
                    mla_att(2 * b + q - 1, K)
                    pair_take(K + 2)

            panel_act(st, 0, 0, evac=pair_evac(0))
            pair_take(TB["mla0"])
            panel_act(st, 0, 1, evac=pair_evac(1))
            mla_att(0, TB["mla"])
            pair_take(TB["mla"] + 2)
            each(act, 1, 3, mla_body)
            mla_body(3)
            mla_att(7, TB["mla_tail"])
            load(bands[:], a["bands"], pool_in_)
            load(scaleB[:], a["pool_scale"], pool_in_)
            og_split("og1", 0, 8, lambda u: og1[0][:, 2 * u:2 * u + 2, :])
            for u in range(4):
                take(TB["gate1"] + u // 2, u % 2, gateB1[:, u * PW:(u + 1) * PW], PS[:, 4 + u % 2, :])
            each(act, 0, 4, lambda i: panel_act(ST["mla_out"], i))

            def split_x(part):
                og_split(part, 0, 8, lambda u: x2[0][:, 2 * u:2 * u + 2, :])

            split_x("pool")

            def u_evac(g):
                return lambda tt: copy(U[:, tt, g * PW:(g + 1) * PW], PS[:, tt, :])

            for g in range(4):
                panel_act(ST["pool_in"], g, evac=u_evac(g))
                if g:
                    og_split("band", 2 * g - 2, 2 * g, lambda u: pT[0][:, 2 * u:2 * u + 2, :])
            og_split("band", 6, 8, lambda u: pT[0][:, 2 * u:2 * u + 2, :])
            for g in range(4):
                panel_act(ST["pool_group"], 0, q=g)
                if g:
                    og_split("py", 2 * g - 2, 2 * g, lambda u: yT[0][:, 2 * u:2 * u + 2, :])
            og_split("py", 6, 8, lambda u: yT[0][:, 2 * u:2 * u + 2, :])
            load(lnB[:], a["ln"][0], ln_in)
            load(ndm[:], a["ndm"], ndm_in)
            each(act, 0, 4, lambda i: panel_act(ST["pool_out"], i))

            def mlp(layer):
                for half in range(2):
                    up, down = ST[f"up{layer}{half}"], ST[f"down{layer}{half}"]

                    def relu(tt):
                        return f(HS[:, tt, :], PS[:, tt, :], ACT.Relu)

                    def split_panel(i, k):
                        if k == 2:
                            for u in range(2):
                                split(TB[up.name] + i, u, hw[0][:, bass.ds(4 * i + 2 * u, 2), :] if not isinstance(i, int)
                                      else hw[0][:, 4 * i + 2 * u:4 * i + 2 * u + 2, :])

                    panel_act(up, 0, evac=relu)
                    each(act, 1, 8, lambda i: panel_act(up, i, evac=relu, slot=lambda k: split_panel(i - 1, k)))
                    if half == 0:
                        act.wait_ge(x_ready, (2 * layer + 1) * TT)
                        load(lnB[:], a["ln"][2 * layer + 1], ln_in)
                    panel_act(down, 0, slot=lambda k: split_panel(7, k))
                    last = layer == 1 and half == 1
                    each(act, 1, 3 if last else 4, lambda i: panel_act(down, i))
                    if last:
                        panel_act(down, 3, final=True)

            split_x("ln0")
            mlp(0)
            split_x("ln1")

            act.wait_ge(x_ready, 2 * TT)
            load(lnB[:], a["ln"][2], ln_in)
            st = ST["qkv"]
            for hf in range(2):
                def take_qk(K, dst, g):
                    for u in range(2):
                        take(K, u, dst[:, bass.ds(4 * g + 2 * u, 2), :], PS[:, 4 + u, :].rearrange("p (h t) -> p h t", h=2))

                def stage(tt):
                    return copy(HS[:, tt, :], PS[:, tt, :])

                def group(g):
                    i = 9 * hf + 3 * g
                    K = TB[f"qk{hf}"] + 2 * g
                    panel_act(st, i, evac=stage)
                    panel_act(st, i + 1, evac=stage, slot=lambda k: take_qk(K, qA, g) if k == 1 else None)
                    panel_act(st, i + 2, evac=lambda tt: copy(VA[:, tt, col(g, PW)], PS[:, tt, :]),
                              slot=lambda k: take_qk(K + 1, kA, g) if k == 1 else None)

                each(act, 0, N_GROUPS, group)
                K = TB[f"att{hf}"]
                for m in range(9):
                    n = 8 * hf + m
                    if m < 8:
                        b, nk = m % 2, KEYS[m % 2]
                        s = SA[:, b, :].rearrange("p (g t) -> p g t", g=N_GROUPS)[:, :, 0:nk]
                        act.wait_ge(dil["m_ready"], n + 1)
                        f(s, s, ACT.Exp, bias=nm[:, b:b + 1], scale=SWA_SCALE,
                          accum_out=rs[:, m % 4:m % 4 + 1]).then_inc(dil["p_ready"], 1)
                    if m:
                        u = m - 1
                        need(act, dil["o_full"], n - 1)
                        at_ = 0
                        for j, part in enumerate(dil_parts(u % 2)):
                            nb = len(part)
                            take(K + u, j, PTa[:, at_:at_ + nb, :],
                                 PS[:, 4 + j, 0:nb * P].rearrange("p (c t) -> p c t", c=nb))
                            at_ += nb
            og_split("ao", 0, 4, lambda u: oT[0][:, 2 * u:2 * u + 2, :])

            def out_body(b):
                for q in range(2):
                    panel_act(ST["attn_out"], b, q)

            each(act, 0, 2, out_body)
            split_x("ln2")
            mlp(1)

        @block.vector
        def _(dve):
            v = nc.vector
            C = Chain(dve, dve_chain)

            def rest(I, j, w=TW):
                dve.wait_ge(hi_done, 4 * I + j + 1)
                w = width(I, j, w)
                v.tensor_tensor(wlo[:, j % 2, 0:w], raw[:, j, 0:w], whi[:, j % 2, 0:w],
                                ALU.subtract).then_inc(lo_done, 1)

            def panel_dve(st, b, q=0, evac=None, slot=None, final=False):
                n = panel(st, b, q)
                for k in range(st.tpp):
                    if slot:
                        slot(k)
                    if evac and k == st.tpp - 1:
                        for tt in range(st.na):
                            dve.wait_ge(acc_full, st.acc + n * st.na + tt + 1)
                            evac(tt).then_inc(acc_free, 1)
                    I, j = tile_at(st, b, q, k)
                    j += 2
                    w = (4 * QBW, 2 * PW)[k] if st.name == "mla_pair" else TW
                    if not (final and k >= st.tpp - 2):
                        rest(I + j // 4, j % 4, w)

            def lower(part, u, hi, lo, first=None):
                K, j = TB[part] + u // 2, u % 2
                dve.wait_ge(split_hi, HB[part] + u + 1)
                n = hi.shape[-1] * (hi.shape[1] if len(hi.shape) == 3 else 1)
                src = PS[:, 4 + j, 0:n]
                if len(hi.shape) == 3:
                    src = src.rearrange("p (c t) -> p c t", c=hi.shape[1])
                v.tensor_tensor(lo, src, hi, ALU.subtract).then_inc(tr_free[j], 1)

            def rsqrt(*terms):
                for c, src, n, eps in terms:
                    C(v.tensor_scalar(ms[:, c], src, 1.0 / n, eps, ALU.mult, ALU.add))
                c = slice(terms[0][0].start, terms[-1][0].stop)
                x, y, t = ms[:, c], hrs[:, c], nt[:, c]
                C(v.tensor_scalar(t.bitcast(I32), x.bitcast(I32), 1, None, ALU.logical_shift_right))
                C(v.tensor_scalar(y.bitcast(I32), t.bitcast(I32), -1.0, float(0x5F3759DF), ALU.mult, ALU.add))
                for _ in range(3):
                    C(v.scalar_tensor_tensor(t, x, -0.5, y, ALU.mult, ALU.mult))
                    C(v.tensor_tensor(t, t, y, ALU.mult))
                    C(v.scalar_tensor_tensor(y, t, 1.5, y, ALU.add, ALU.mult))

            def place_cond():
                c4 = condL[:, :, 0:4].rearrange("p k (j s) -> p j k s", s=2)
                C(v.memset(condL[:].bitcast(F32), 0.0))
                C.tick(v.tensor_copy(c4[:, :, :, 0], condh[:]))
                v.tensor_tensor(c4[:, :, :, 1], cond[:], condh[:], ALU.subtract).then_inc(cond_ready, 1)

            dve.wait_ge(cond_hi, 1)
            C(v.memset(ms[:], 1.0))
            place_cond()
            C.wait()
            rest(0, 0)
            rest(0, 1)
            dve.wait_ge(consts_in, 16 * (len(CONSTS) - 1))
            C(v.memset(zero[:], 0.0))
            C(v.tensor_scalar(nsink[:], sink[:], -1.0, None, ALU.mult))

            def normed(layer, dst):
                dve.wait_ge(ss_ready, 4 * (layer + 1))
                rsqrt((slice(0, 4), ssq[:], D, EPS))
                for tt in range(4):
                    v.tensor_scalar(dst(tt), X[:, tt, :], hrs[:, tt:tt + 1], None, ALU.mult).then_inc(xn_ready, 1)

            def modulated(layer, part):
                dve.wait_ge(cols_full, layer + 1)
                cols = PS[:, 7, 0:4 * KC].rearrange("p (s c j) -> p s j c", s=2, j=2)
                g = normg[:, layer:layer + 1, :].broadcast_to([P, 2, KC])
                C(v.tensor_scalar(modA[:], cols[:, 1], 1.0, None, ALU.add))
                C.tick(v.tensor_tensor(modA[:], modA[:], g, ALU.mult))
                C(v.tensor_copy(modB[:], cols[:, 0]))
                v.tensor_copy(gaterow[:], adarow[:, 2 * D:3 * D]).then_inc(gate_kept, 1)
                dve.wait_ge(gate_kept, layer + 1)
                for c in range(KC + 1):
                    if c < KC:
                        K, j = TB[part] + c // 2, c % 2
                        dve.wait_ge(tr_full[j], K + 1)
                        need(dve, mod_lo, KC * layer + c - 1)
                        for s in range(2):
                            last = v.tensor_scalar(tmod[:, j, s * TOK:(s + 1) * TOK], PS[:, 4 + j, s * TOK:(s + 1) * TOK],
                                                   modA[:, s, c:c + 1], modB[:, s, c:c + 1], ALU.mult, ALU.add)
                        last.then_inc(tr_free[j], 1)
                    if c:
                        dve.wait_ge(split_hi, HB[part] + c)
                        v.tensor_tensor(h4[1][:, c - 1, :], tmod[:, (c - 1) % 2, :], h4[0][:, c - 1, :],
                                        ALU.subtract).then_inc(mod_lo, 1)

            panel_dve(ST["ada0"], 0)
            normed(0, lambda tt: X[:, tt, :])
            each(dve, 1, 12, lambda i: panel_dve(ST["ada0"], i))
            modulated(0, "mod0")
            dve.wait_ge(swa_in_, 16 * 4)
            for w in range(2):
                for s in range(2):
                    C.tick(v.tensor_tensor(tabs[:, w, :, s, :], tabs[:, w, :, s, :],
                                           gqk[:, w, s:s + 1, :].broadcast_to([P, TT, HD]), ALU.mult))
            C.wait()

            def heads(t):
                return t.rearrange("p (h e) -> p h e", h=4)

            def head_norm(acc, w, tt, done):
                x = heads(QS[:, tt, :])
                q4 = heads(SQ[:])
                dve.wait_ge(acc_free, acc + tt + 1)
                need(dve, qk_ready, done + tt)
                C(v.tensor_tensor(SQ[:], QS[:, tt, :], QS[:, tt, :], ALU.mult))
                C(v.tensor_reduce(hss[:, 0:4], q4, AX, ALU.add))
                rsqrt((slice(0, 4), hss[:, 0:4], HD, EPS))
                C(v.tensor_tensor(x, x, hrs[:, 0:4].unsqueeze(2).broadcast_to([P, 4, HD]), ALU.mult))
                if tt < TT:
                    xs = QS[:, tt, :].rearrange("p (h s e) -> p h s e", s=2, e=32)
                    qs = SQ[:].rearrange("p (h s e) -> p h s e", s=2, e=32)
                    sn = tabs[:, w, tt, 1, :].rearrange("p (a s e) -> p a s e", s=2, e=32)
                    for s in range(2):
                        for h in range(4):
                            C.tick(v.tensor_tensor(qs[:, 2 * h:2 * h + 2, s, :], xs[:, 2 * h:2 * h + 2, 1 - s, :],
                                                   sn[:, :, s, :], ALU.mult))
                    C.wait()
                    C(v.tensor_tensor(x, x, tabs[:, w, tt, 0:1, :].broadcast_to([P, 4, HD]), ALU.mult))
                    last = v.tensor_tensor(QS[:, tt, :], QS[:, tt, :], SQ[:], ALU.add)
                else:
                    last = v.tensor_tensor(x, x, gqk[:, w, 0:1, :].broadcast_to([P, 4, HD]), ALU.mult)
                last.then_inc(qk_ready, 1)

            st = ST["swa_kv"]
            panel_dve(st, 0)
            panel_dve(st, 1, slot=lambda k: head_norm(st.acc, 1, k, 0))
            st = ST["swa_qg"]

            def swa_step(g, n):
                if n < 16:
                    h, tt, b = n // 4, n % 4, n % 2
                    nk = 512 if tt < TT else 256
                    m0 = (3 * P, 0, P, P)[tt]
                    dve.wait_ge(swa["s_full"], 16 * g + n + 1)
                    v.memset(waited[:], 0.0)
                    v.tensor_tensor_reduce(Sb[:, b, 0:nk], PS[:, 6, 0:nk], masks[:, m0:m0 + nk], 1.0, -3e38,
                                           ALU.add, ALU.max, mx[:, b:b + 1]).then_inc(swa["s_free"], 1)
                    dve.wait_ge(swa["s_free"], 16 * g + n + 1)
                    v.tensor_scalar(nm[:, b:b + 1], mx[:, b:b + 1], -SWA_SCALE, nsink[:, col(4 * g + h, 1, 1)],
                                    ALU.mult, ALU.min).then_inc(swa["m_ready"], 1)
                if n >= 2:
                    u = n - 2
                    h, tt, b = u // 4, u % 4, u % 2
                    dve.wait_ge(swa["p_ready"], 16 * g + u + 1)
                    C(v.tensor_tensor(den[:, b:b + 1], rs[:, u % 4:u % 4 + 1], es[:, u % 4:u % 4 + 1], ALU.add))
                    C(v.reciprocal(rden[:, b:b + 1], den[:, b:b + 1]))
                    dve.wait_ge(swa["o_full"], 16 * g + u + 1)
                    gate = G0[:, tt, col(4 * g + h, HD, HD)]
                    v.scalar_tensor_tensor(gate, PS[:, 7, 0:HD], rden[:, b:b + 1], gate, ALU.mult,
                                           ALU.mult).then_inc(swa["o_free"], 1)

            panel_dve(st, 0)
            panel_dve(st, 1, slot=lambda k: head_norm(st.acc, 0, k, 4))

            def swa_group(i):
                def slot(k):
                    for tt in range(4):
                        swa_step(i - 1, 4 * k + tt)

                panel_dve(st, 2 * i, slot=slot)
                swa_step(i - 1, 16)
                swa_step(i - 1, 17)
                panel_dve(st, 2 * i + 1, slot=lambda k: head_norm(st.acc + 8 * i, 0, k, 4 + 4 * i))

            counted_loop(dve, (C,), 1, 4, swa_group, (110,))
            for n in range(18):
                swa_step(3, n)
            for u in range(KC):
                lower("og0", u, h4[0][:, u, :], h4[1][:, u, :])

            def residual(st, i, gate, tts):
                def evac(tt):
                    dve.wait_ge(acc_free, st.acc + st.na * i + tt)
                    C(v.tensor_tensor(rtmp[:], PS[:, tt, :], gate(tt, col(i, PW)), ALU.mult))
                    return v.tensor_tensor(X[:, tt, col(i, PW)], X[:, tt, col(i, PW)], rtmp[:], ALU.add)
                panel_dve(st, i, evac=evac)

            place_cond()
            for j in range(2):
                dve.wait_ge(tr_free[j], TB["gate0"] + 4)
            dve.wait_ge(x_again, 16)
            counted_loop(dve, (C,), 0, 4, lambda i: residual(ST["swa_out"], i, lambda tt, c: gateB[:, tt // TT, c], 4), (4,))

            panel_dve(ST["ada1"], 0)
            normed(1, lambda tt: (XN if tt < TT else X)[:, tt, :])
            each(dve, 1, 12, lambda i: panel_dve(ST["ada1"], i))
            modulated(1, "mod1")
            panel_dve(ST["mla_cq"], 0)

            def latents(k):
                if k == 0:
                    dve.wait_ge(mla_in_, 16 * 6)
                    for w in range(2):
                        for s in range(2):
                            C.tick(v.tensor_tensor(rtab[:, w, :, s, :], rtab[:, w, :, s, :],
                                                   gpe[:, w, s:s + 1, :].broadcast_to([P, TT, 64]), ALU.mult))
                    C(v.tensor_tensor(gprod[:], gnope[:, 0, :], gnope[:, 1, :], ALU.mult))
                    dve.wait_ge(acc_free, ST["mla_cq"].acc + 2)
                if k < TT:
                    x = cqS[:, k, :]
                    C(v.tensor_tensor(sqS[:], x, x, ALU.mult))
                    C(v.tensor_reduce(hss[:, 0:1], sqS[:], AX, ALU.add))
                    rsqrt((slice(0, 1), hss[:, 0:1], 512, EPS))
                    v.scalar_tensor_tensor(x, x, hrs[:, 0:1], gqa[:], ALU.mult, ALU.mult).then_inc(lat_ready, 1)

            panel_dve(ST["mla_ckv"], 0, slot=latents)

            def rope64(x, w, tts, heads_, sq):
                xs = x.rearrange("p t h (a s e) -> p t h a s e", s=2, e=16)
                qs = sq.rearrange("p t h (a s e) -> p t h a s e", s=2, e=16)
                for tt in tts:
                    sn = rtab[:, w, tt, 1, :].rearrange("p (a s e) -> p a s e", s=2, e=16)
                    for h in range(heads_):
                        for s in range(2):
                            C.tick(v.tensor_tensor(qs[:, tt, h, :, s, :], xs[:, tt, h, :, 1 - s, :], sn[:, :, s, :], ALU.mult))
                C.wait()
                for tt in tts:
                    C.tick(v.tensor_tensor(x[:, tt], x[:, tt], rtab[:, w, tt, 0:1, :].broadcast_to([P, heads_, 64]), ALU.mult))
                C.wait()

            def latents_kv(k):
                if k != 0:
                    return
                dve.wait_ge(acc_free, ST["mla_ckv"].acc + 4)
                for tt in range(4):
                    x, y = ckvS[:, tt, 0:256], ckvS[:, tt, 256:320]
                    C.tick(v.tensor_tensor(sqS[:, 0:MLA_KVW], ckvS[:, tt, :], ckvS[:, tt, :], ALU.mult))
                    C.wait()
                    C.tick(v.tensor_reduce(hss[:, 0:1], sqS[:, 0:256], AX, ALU.add))
                    C(v.tensor_reduce(hss[:, 1:2], sqS[:, 256:320], AX, ALU.add))
                    rsqrt((slice(0, 1), hss[:, 0:1], 256, EPS), (slice(1, 2), hss[:, 1:2], 64, EPS))
                    C(v.scalar_tensor_tensor(x, x, hrs[:, 0:1], gkva[:], ALU.mult, ALU.mult))
                    if tt < TT:
                        C(v.tensor_scalar(y, y, hrs[:, 1:2], None, ALU.mult))
                    else:
                        C(v.scalar_tensor_tensor(y, y, hrs[:, 1:2], gpe[:, 1, 0, :], ALU.mult, ALU.mult))
                y = ckvS[:, 0:TT, 256:320].unsqueeze(2)
                s = sqS[:, 0:TT * 64].rearrange("p (t h e) -> p t h e", t=TT, h=1)
                rope64(y, 1, range(TT), 1, s)
                v.tensor_tensor(y, y, s, ALU.add).then_inc(lat_ready, 1)

            st = ST["mla_gate"]
            panel_dve(st, 0, slot=latents_kv)
            for u in range(2):
                lower("cq", u, *(t[:, 2 * u:2 * u + 2, :] for t in cqT))
            for u in range(2):
                lower("ckv", u, *(t[:, u, :] for t in ckvT))
            each(dve, 1, 3, lambda i: panel_dve(st, i))
            panel_dve(st, 3)
            st = ST["mla_pair"]

            def pair_norm(p, q):
                kn = KV[:, q].rearrange("p t (h e) -> p t h e", h=2)[:, :, :, 0:P]
                s8 = SQm[:].rearrange("p (t h e) -> p t h e", t=4, h=2)
                dve.wait_ge(acc_free, st.acc + 6 * p + 6)
                C(v.tensor_tensor(s8, kn, kn, ALU.mult))
                C(v.tensor_reduce(hss[:, 0:8], SQm[:].rearrange("p (n e) -> p n e", e=P), AX, ALU.add))
                rsqrt((slice(0, 8), hss[:, 0:8], HD, EPS))
                r8 = hrs[:, 0:8].rearrange("p (t h) -> p t h", h=2).unsqueeze(3).broadcast_to([P, 4, 2, P])
                C.tick(v.tensor_tensor(kn, kn, r8, ALU.mult))
                x = QP[:].rearrange("p t (h e) -> p t h e", h=2)
                sx = SQm[:, 0:TT * QBW].rearrange("p (t h e) -> p t h e", t=TT, h=2)
                C(v.tensor_tensor(SQm[:, 0:TT * QBW], QP[:].rearrange("p t e -> p (t e)"),
                                  QP[:].rearrange("p t e -> p (t e)"), ALU.mult))
                C.tick(v.tensor_reduce(hss[:, 0:4], sx[:, :, :, 0:P], AX, ALU.add))
                C(v.tensor_reduce(hss[:, 8:12], sx[:, :, :, P:192], AX, ALU.add))
                rsqrt((slice(0, 4), hss[:, 0:4], HD, EPS), (slice(8, 12), hss[:, 8:12], 64, EPS))
                xn, xp = x[:, :, :, 0:P], x[:, :, :, P:192]
                r4 = hrs[:, 0:4].rearrange("p (t h) -> p t h", h=2).unsqueeze(3).broadcast_to([P, TT, 2, P])
                C.tick(v.tensor_tensor(xn, xn, r4, ALU.mult))
                rp = hrs[:, 8:12].rearrange("p (t h) -> p t h", h=2).unsqueeze(3).broadcast_to([P, TT, 2, 64])
                C(v.tensor_tensor(xp, xp, rp, ALU.mult))
                C.tick(v.tensor_tensor(xn, xn, gprod[:].unsqueeze(1).unsqueeze(1).broadcast_to([P, TT, 2, P]), ALU.mult))
                s4 = SQm[:, 0:TT * 2 * 64].rearrange("p (t h e) -> p t h e", t=TT, h=2)
                rope64(xp, 0, range(TT), 2, s4)
                v.tensor_tensor(xp, xp, s4, ALU.add).then_inc(pair_ready, 1)

            def mla_att(p):
                for m in range(6):
                    if m < 4:
                        b = m % 2
                        dve.wait_ge(mla["s_full"], 4 * p + m + 1)
                        v.memset(waited[:], 0.0)
                        v.tensor_tensor_reduce(Sm[:, b, :], PS[:, 6, :], zero[:].broadcast_to([P, 512]), 1.0, -3e38,
                                               ALU.add, ALU.max, mx[:, b:b + 1]).then_inc(mla["s_free"], 1)
                        dve.wait_ge(mla["s_free"], 4 * p + m + 1)
                        v.tensor_scalar(nm[:, b:b + 1], mx[:, b:b + 1], -MLA_SCALE, None,
                                        ALU.mult).then_inc(mla["m_ready"], 1)
                    if m >= 2:
                        u = m - 2
                        h, tt, b = u // 2, u % 2, u % 2
                        dve.wait_ge(mla["p_ready"], 4 * p + u + 1)
                        C(v.reciprocal(rden[:, b:b + 1], rs[:, u % 4:u % 4 + 1]))
                        dve.wait_ge(mla["o_full"], 4 * p + u + 1)
                        gate = G1[:, tt, col(2 * p + h, HD, HD)]
                        v.scalar_tensor_tensor(gate, PS[:, 7, 0:HD], rden[:, b:b + 1], gate, ALU.mult,
                                               ALU.mult).then_inc(mla["o_free"], 1)

            def mla_body(b):
                for q in range(2):
                    p = 2 * b + q
                    panel_dve(st, b, q)
                    pair_norm(p, q)
                    mla_att(p - 1)

            panel_dve(st, 0, 0)
            pair_norm(0, 0)
            panel_dve(st, 0, 1)
            pair_norm(1, 1)
            mla_att(0)
            counted_loop(dve, (C,), 1, 3, mla_body, (96,))
            mla_body(3)
            mla_att(7)
            for u in range(8):
                lower("og1", u, *(t[:, 2 * u:2 * u + 2, :] for t in og1))
            for j in range(2):
                dve.wait_ge(tr_free[j], TB["gate1"] + 2)
            counted_loop(dve, (C,), 0, 4, lambda i: residual(ST["mla_out"], i, lambda tt, c: gateB1[:, c], 2), (2,))

            def lower_x(part):
                for u in range(8):
                    lower(part, u, *(t[:, 2 * u:2 * u + 2, :] for t in x2))

            lower_x("pool")
            for g in range(4):
                panel_dve(ST["pool_in"], g)
                if g:
                    for u in range(2 * g - 2, 2 * g):
                        lower("band", u, *(t[:, 2 * u:2 * u + 2, :] for t in pT))
            for u in range(6, 8):
                lower("band", u, *(t[:, 2 * u:2 * u + 2, :] for t in pT))
            dve.wait_ge(pool_in_, 32)
            for g in range(4):
                c = slice(g * PW, (g + 1) * PW)
                panel_dve(ST["pool_group"], 0, q=g, evac=lambda tt: v.tensor_tensor(U[:, tt, c], PS[:, tt, :], scaleB[:, c], ALU.mult))
                if g:
                    for u in range(2 * g - 2, 2 * g):
                        lower("py", u, *(t[:, 2 * u:2 * u + 2, :] for t in yT))
            for u in range(6, 8):
                lower("py", u, *(t[:, 2 * u:2 * u + 2, :] for t in yT))

            def add_to_x(st, b, factor, q=0, final=False):
                n = panel(st, b, q)

                def evac(tt):
                    x = X[:, tt, col(n, PW)]
                    return v.scalar_tensor_tensor(x, x, factor, PS[:, tt, :], ALU.mult, ALU.add)

                panel_dve(st, b, q, evac=evac, final=final)

            def layer_norm(number, acc, signal):
                dve.wait_ge(acc_free, acc)
                for tt in range(TT):
                    for c in range(4):
                        C.tick(v.bn_stats(bn[:, c, :], X[:, tt, c * 512:(c + 1) * 512]))
                    C.wait()
                    C(v.bn_aggr(mv[:], bn[:]))
                    rsqrt((slice(0, 1), mv[:, 1:2], 1, LN_EPS))
                    C(v.scalar_tensor_tensor(nmr[:], mv[:, 0:1], -1.0, hrs[:, 0:1], ALU.mult, ALU.mult))
                    x = X[:, tt, :]
                    C(v.tensor_scalar(x, x, hrs[:, 0:1], nmr[:], ALU.mult, ALU.add))
                    dve.wait_ge(ln_in, 16 * (number + 1))
                    C(v.tensor_tensor(x, x, lnB[:, 0, :], ALU.mult))
                    v.tensor_tensor(x, x, lnB[:, 1, :], ALU.add).then_inc(signal, 1)

            each(dve, 0, 4, lambda i: add_to_x(ST["pool_out"], i, ALPHA))
            layer_norm(0, ST["up00"].acc, x_ready)

            def mlp(layer, number, last, sq0):
                for half in range(2):
                    up, down = ST[f"up{layer}{half}"], ST[f"down{layer}{half}"]

                    def square(i, k):
                        if k == 0:
                            for tt in range(TT):
                                dve.wait_ge(acc_free, up.acc + 2 * i + tt + 1)
                                v.tensor_tensor(HS[:, tt, :], HS[:, tt, :], HS[:, tt, :], ALU.mult).then_inc(sq_ready, 1)
                        if k == 2:
                            for u in range(2):
                                K = TB[up.name] + i
                                dve.wait_ge(split_hi, HB[up.name] + 2 * i + u + 1)
                                c = slice(4 * i + 2 * u, 4 * i + 2 * u + 2) if isinstance(i, int) else bass.ds(4 * i + 2 * u, 2)
                                v.tensor_tensor(hw[1][:, c, :], PS[:, 4 + u, :].rearrange("p (c t) -> p c t", c=2),
                                                hw[0][:, c, :], ALU.subtract).then_inc(tr_free[u], 1)

                    panel_dve(up, 0)
                    each(dve, 1, 8, lambda i: panel_dve(up, i, slot=lambda k: square(i - 1, k)))
                    factor = ALPHA if half == 0 else 1.0
                    end = last and half == 1

                    def down_panel(i, slot=None, final=False):
                        def evac(tt):
                            x = X[:, tt, col(i, PW)]
                            return v.scalar_tensor_tensor(x, x, factor, PS[:, tt, :], ALU.mult, ALU.add)
                        panel_dve(down, i, evac=evac, slot=slot, final=final)

                    down_panel(0, slot=lambda k: square(7, k))
                    each(dve, 1, 3 if end else 4, down_panel)
                    if end:
                        down_panel(3, final=True)

            lower_x("ln0")
            mlp(0, 1, False, 0)
            layer_norm(1, ST["qkv"].acc, x_ready)
            lower_x("ln1")
            st = ST["qkv"]
            dve.wait_ge(ndm_in, 16)
            for hf in range(2):
                each(dve, 9 * hf, 9 * hf + 9, lambda i: panel_dve(st, i))
                for m in range(10):
                    n = 8 * hf + m
                    if m < 8:
                        s, tt, b = m // 2, m % 2, m % 2
                        nk, k0 = KEYS[tt], (0, KEYS[0])[tt]
                        dve.wait_ge(dil["s_full"], n + 1)
                        for g in range(N_GROUPS):
                            slope = 2.0 ** (-8.0 * (g * N_SLOTS + 4 * hf + s + 1) / (N_GROUPS * N_SLOTS))
                            last = v.scalar_tensor_tensor(
                                SA[:, b, g * TOK:g * TOK + nk], ndm[:, g, k0:k0 + nk], slope / SWA_SCALE,
                                PS[:, 2 + g // 2, g % 2 * TOK:g % 2 * TOK + nk], ALU.mult, ALU.add)
                            if g < 2:
                                C.tick(last)
                        last.then_inc(dil["s_free"], 1)
                        dve.wait_ge(dil["s_free"], n + 1)
                        C.wait()
                        sv = SA[:, b, :].rearrange("p (g t) -> p g t", g=N_GROUPS)[:, :, 0:nk]
                        C(v.tensor_reduce(mx[:, b:b + 1], sv, mybir.AxisListType.XY, ALU.max))
                        v.tensor_scalar(nm[:, b:b + 1], mx[:, b:b + 1], -SWA_SCALE, None, ALU.mult).then_inc(dil["m_ready"], 1)
                    if m >= 2:
                        u = m - 2
                        s, tt, b = u // 2, u % 2, u % 2
                        dve.wait_ge(dil["p_ready"], 8 * hf + u + 1)
                        C(v.reciprocal(rden[:, b:b + 1], rs[:, u % 4:u % 4 + 1]))
                        dve.wait_ge(dil["o_full"], 8 * hf + u + 1)
                        f0 = (4 * hf + s) * HD
                        v.tensor_scalar(OA[:, tt, f0:f0 + HD], PS[:, 7, 0:HD], rden[:, b:b + 1], None,
                                        ALU.mult).then_inc(dil["o_free"], 1)
            for u in range(4):
                lower("ao", u, *(t[:, 2 * u:2 * u + 2, :] for t in oT))

            def out_body(b):
                for q in range(2):
                    add_to_x(ST["attn_out"], b, ALPHA, q)

            each(dve, 0, 2, out_body)
            layer_norm(2, ST["up10"].acc, x_ready)
            lower_x("ln2")
            mlp(1, 3, True, 32)
            end = ST["down11"]
            layer_norm(3, end.acc + end.n * end.na, final)


def tiles(w):
    k, n = w.shape
    return w.reshape(k // 512, 4, P, n // PW, PW).transpose(3, 0, 2, 1, 4).reshape(-1, P, TW)


def padded(t):
    out = np.zeros((t.shape[0], P, TW), t.dtype)
    out[:, :, :t.shape[2] * t.shape[3]] = t.reshape(t.shape[0], P, -1)
    return out


def weight_stream(i):
    q, kv, hd = D, 512, PW
    w = i["swa_w_in"][0]
    parts = [tiles(i["ada_w"][0]), tiles(w[:, q:q + 2 * kv])]
    for g in range(4):
        parts += [tiles(w[:, g * PW:(g + 1) * PW]), tiles(w[:, q + 2 * kv + g * PW:q + 2 * kv + (g + 1) * PW])]
    parts += [tiles(i["swa_w_out"][0]), tiles(i["ada_w"][1])]
    w = i["mla_w_in"][0]
    parts.append(tiles(w[:, 0:512]))
    parts.append(padded(w[:, 512:832].reshape(4, 4, P, MLA_KVW).transpose(0, 2, 1, 3)))
    parts.append(tiles(w[:, 832:]))
    qb, kvb = i["mla_w_qb"][0], i["mla_w_kvb"][0]
    for p in range(8):
        parts.append(padded(qb[:, p * QBW:(p + 1) * QBW].reshape(1, 4, P, QBW).transpose(0, 2, 1, 3)))
        parts.append(padded(kvb[:, p * PW:(p + 1) * PW].reshape(1, 2, P, PW).transpose(0, 2, 1, 3)))
    parts.append(tiles(i["mla_w_out"][0]))
    parts.append(tiles(i["pool_w_in_2"][0]))
    parts += [tiles(i["pool_w_group_2"][0, g]) for g in range(4)]
    parts.append(tiles(i["pool_w_out_2"][0]))

    def mlp(l):
        up, down = i["mlp_w_up_2"][l], i["mlp_w_down_2"][l]
        return [tiles(up[:, :4096]), tiles(down[:4096]), tiles(up[:, 4096:]), tiles(down[4096:])]

    parts += mlp(0)
    w = i["attn_w_qkv_2"][0].reshape(D, 3, N_GROUPS, 2, PW)
    parts += [tiles(w[:, k, g, hf]) for hf in range(2) for g in range(N_GROUPS) for k in range(3)]
    parts.append(tiles(i["attn_w_out_2"][0]))
    parts += mlp(1)
    return np.concatenate(parts)


def rope(rot):
    half = rot // 2
    pos = np.arange(TOK)
    inv = (1.0 / (np.float32(10000.0) ** (np.arange(0, half, 2, dtype=np.float32) / np.float32(half)))).astype(np.float32)
    ar, ac = ((x.astype(np.float32)[:, None] * inv).astype(np.float32) for x in (pos // 64, pos % 64))
    ang = np.concatenate([ar, ar, ac, ac], -1).astype(np.float64)
    sign = np.repeat(np.array([-1.0, 1.0, -1.0, 1.0]), half // 2)
    t = np.stack([np.cos(ang), np.sin(ang) * sign], 1).astype(np.float32)
    return t.reshape(TT, P, 2, rot).transpose(1, 0, 2, 3).copy()


def swap(g):
    n = g.shape[-1] // 4
    return np.concatenate([g[..., n:2 * n], g[..., :n], g[..., 3 * n:], g[..., 2 * n:3 * n]], -1)


def over(v):
    return np.broadcast_to(v, (P,) + v.shape).copy()


def constants():
    f = np.float32
    qi, ki = np.arange(P)[:, None], np.arange(P)[None, :]
    zero = np.zeros((P, P), f)
    upper = np.where(ki >= qi, 0, NEG).astype(f)
    lower = np.where(ki <= qi, 0, NEG).astype(f)
    masks = np.concatenate([upper, zero, zero, zero, lower, zero, zero], 1)
    s, t = np.arange(TOK)[:, None], np.arange(TOK)[None, :]
    bands = np.zeros((TOK, 4, TOK), f)
    for g, w in enumerate(POOL_WINDOWS):
        inside = (s <= t) & (s > t - w)
        bands[:, g] = np.where(inside, 1.0 / np.minimum(t + 1, w), 0.0) - (s == t)
    bands = bands.reshape(TT, P, 4, TOK).transpose(1, 2, 0, 3).copy()
    ndm = np.zeros((P, N_GROUPS, 3 * P), f)
    for g, (w, d) in enumerate(((128, 1), (512, 4), (2048, 16))):
        dist = np.arange(TOK)[:, None] - np.arange(TOK)[None, :]
        ok = (dist >= 0) & (dist % d == 0) & (dist // d <= w // d)
        m = np.where(ok, -dist, NEG).astype(f)
        ndm[:, g, :P] = m[:P, :P]
        ndm[:, g, P:] = m[P:]
    selrow = np.zeros((5, 2, P), f)
    selrow[0:2, 0] = selrow[2:4, 1] = selrow[4] = 1
    return {"ident": np.eye(P, dtype=f), "masks": masks, "bands": bands, "ndm": ndm, "selrow": selrow,
            "selcol": selrow[:, :, 0].copy(), "rope128": rope(HD), "rope64": rope(64)}


def kernel(**inputs):
    import concourse.bacc as bacc
    from concourse.bass_utils import run_bass_kernel_spmd

    i = {k: np.asarray(v) for k, v in inputs.items()}
    pair = lambda q, k: over(np.stack([np.stack([q, swap(q)]), np.stack([k, swap(k)])]))
    cols = lambda v: v.reshape(KC, P).T
    tok = lambda v: v.reshape(TT, P, D).transpose(1, 0, 2)
    ln = np.stack([i["ln_mix_g_2"], i["ln_mix_b_2"], i["ln_mlp_g_2"], i["ln_mlp_b_2"]], 1).reshape(2, 2, 2, D).reshape(4, 1, 2, D)
    arrays = {
        "weights": weight_stream(i),
        "x": np.concatenate([tok(i["x"][0]), tok(i["ctx"][0])], 1),
        "cond": np.stack([cols(i["c"][0]), cols(i["c_ctx"])], 1),
        "normg": np.stack([cols(i["norm_g"][0]), cols(i["norm_g"][1])], 1),
        "ada_b": i["ada_b"][:, None, :],
        "sink": over(i["swa_sink"][0]),
        "gqk": pair(i["swa_q_g"][0], i["swa_k_g"][0]),
        "gpe": pair(i["mla_qn_pe_g"][0], i["mla_kn_pe_g"][0]),
        "gqa": over(i["mla_qa_g"][0]),
        "gkva": over(i["mla_kva_g"][0]),
        "gnope": over(np.stack([i["mla_qn_nope_g"][0], i["mla_kn_nope_g"][0]])),
        "pool_scale": over(i["pool_scale_2"][0]),
        "ln": np.broadcast_to(ln, (4, P, 2, D)),
        **constants(),
    }
    nc = bacc.Bacc("TRN2", target_bir_lowering=False, num_devices=1, dynamic_dma_scratch_size=1024)
    sent, a = {}, {}
    for name, x in arrays.items():
        x = np.ascontiguousarray(x)
        sent[f"in_{name}"] = x
        a[name] = nc.dram_tensor(f"in_{name}", x.shape, mybir.dt.from_np(x.dtype), kind="ExternalInput").ap()
    out = nc.dram_tensor("out_x", (P, TT, D), F32, kind="ExternalOutput").ap()
    program(nc, a, out)
    r = run_bass_kernel_spmd(nc, [sent], core_ids=[0])
    return r.results[0]["out_x"].transpose(1, 0, 2).reshape(1, TOK, D)
```

```python
from contextlib import ExitStack
import math

import numpy as np

import concourse.bass as bass
from concourse import mybir

F32 = mybir.dt.float32
F32R = mybir.dt.float32r
I32 = mybir.dt.int32
ACT = mybir.ActivationFunctionType
ALU = mybir.AluOpType
AX = mybir.AxisListType.X

P = 128
D = 2048
KC = D // P
TOK = 256
TT = TOK // P
PW = 512
TW = 2048
HD = 128
EPS = 1e-6
LN_EPS = 1e-5
ALPHA = (2 * 2) ** 0.25
NEG = -1e30
N_SLOTS = 8
N_GROUPS = 3
POOL_WINDOWS = (2, 4, 8, 16)
SWA_SCALE = HD ** -0.5
MLA_SCALE = (128 + 64) ** -0.5
MLA_KVW = 320
QBW = 384


def stages():
    table = [(("ada0_0", 4, 4, 0), ("ada0_1", 4, 4, 0), ("ada0_2", 4, 4, 0)),
             ("swa_kv", 2, 4, 4), ("swa_qg", 8, 4, 4),
             [("swa_out", 4, 4, 4), ("ada1_0", 4, 4, 0), ("ada1_1", 4, 4, 0), ("ada1_2", 4, 4, 0)],
             ("mla_cq", 1, 4, 2), ("mla_ckv", 1, 4, 4), ("mla_gate", 4, 4, 2),
             ("mla_pair", 8, 2, 6), ("mla_out", 4, 4, 2), ("pool_in", 4, 4, 2), ("pool_group", 4, 1, 2),
             ("pool_out", 4, 4, 2), ("up00", 8, 4, 2), ("down00", 4, 8, 2), ("up01", 8, 4, 2),
             ("down01", 4, 8, 2), ("qkv", 18, 4, 2), ("attn_out", 4, 2, 2), ("up10", 8, 4, 2),
             ("down10", 4, 8, 2), ("up11", 8, 4, 2), ("down11", 4, 8, 2)]
    out, tile, acc, used, direct = {}, 0, 0, 0, 0
    for run in table:
        mixed = isinstance(run, list)
        run = run if isinstance(run[0], tuple) else (run,)
        uses = {name: 0 if name == "mla_pair" else tpp - 1 for name, _, tpp, _ in run}
        tstep, ustep = sum(tpp for _, _, tpp, _ in run), sum(uses.values())
        at, used_at = tile, used
        for name, n, tpp, na in run:
            out[name] = Stage(name, n, tpp, na, at, acc, used_at, tstep, ustep, len(run) if mixed else 1, direct, tile // 4)
            at += 1 if mixed else tpp
            used_at += 1 if mixed else uses[name]
            acc += n * na
        tile += run[0][1] * tstep
        used += run[0][1] * ustep
        if run[0][0] in ("ada0_0", "swa_out"):
            direct += run[0][1] * tstep // 2
    return out, tile


class Stage:

    def __init__(self, name, n, tpp, na, tile, acc, used, tstep, ustep, kstep, before, first):
        self.kstep, self.before, self.first = kstep, before, first
        self.name, self.n, self.tpp, self.na = name, n, tpp, na
        self.tile, self.acc, self.used, self.tstep, self.ustep = tile, acc, used, tstep, ustep
        self.ada = name.startswith("ada")
        if self.ada:
            self.layer, self.sub = int(name[3]), int(name[5])

    def direct(self, k):
        return self.ada and (self.tile % 4 + k * self.kstep) % 4 >= 2

    def split(self, I, j):
        if self.ada or self.name == "swa_out":
            return 2 * I + 2 * self.first + j + 1 - self.before
        return 4 * I + j + 1 - self.before

    def row(self, b):
        return 12 * self.layer + self.sub + b * 3


def need(eng, sem, value):
    if isinstance(value, int) and value <= 0:
        return
    eng.wait_ge(sem, value)


def each(eng, lo, hi, body):
    with eng.Fori(0, hi - lo) as i:
        body(i + lo)


def col(i, n, w=PW):
    if isinstance(i, int):
        return slice(i * w, i * w + n)
    return bass.ds(i * w, n)


class Chain:

    def __init__(self, eng, sem):
        self.eng, self.sem, self.n, self.off = eng, sem, 0, 0

    def __call__(self, ins):
        self.tick(ins)
        self.wait()

    def tick(self, ins):
        ins.then_inc(self.sem, 1)
        self.n += 1

    def wait(self):
        self.eng.wait_ge(self.sem, self.n + self.off)


def counted_loop(eng, chains, lo, hi, body, per):
    starts = [c.n for c in chains]
    with eng.Fori(0, hi - lo) as i:
        for c, n in zip(chains, per):
            c.off = i * n
        body(i + lo)
    for c, n, start in zip(chains, per, starts):
        assert c.n - start == n, [(c.n - s) for c, s in zip(chains, starts)]
        c.off, c.n = 0, start + n * (hi - lo)


def turns():
    table = [("mod0", 8), ("kT", 2), ("q0", 2), ("swa", 30), ("swa_tail", 8), ("og0", 8), ("gate0", 4),
             ("mod1", 8), ("cq", 1), ("ckv", 1), ("kpe", 1), ("mla", 32),
             ("og1", 4), ("gate1", 2), ("pool", 4), ("band", 4), ("py", 4), ("ln0", 4), ("up00", 8),
             ("up01", 8), ("ln1", 4), ("qk0", 6), ("att0", 8), ("qk1", 6), ("att1", 8), ("ao", 2),
             ("ln2", 4), ("up10", 8), ("up11", 8)]
    out, n = {}, 0
    for name, k in table:
        out[name] = n
        n += k
    return out


def halves():
    table = [("mod0", 16), ("og0", 16), ("mod1", 16), ("cq", 2), ("ckv", 2), ("og1", 8), ("pool", 8),
             ("band", 8), ("py", 8), ("ln0", 8), ("up00", 16), ("up01", 16), ("ln1", 8), ("ao", 4),
             ("ln2", 8), ("up10", 16), ("up11", 16)]
    out, n = {}, 0
    for name, k in table:
        out[name] = n
        n += k
    return out


CONSTS = [("ident", P), ("selrow", 2 * P), ("selcol", 2), ("cond", 2 * KC), ("normg", 2 * KC), ("sink", 16)]
KEYS = (P, 2 * P)


def dil_parts(tt):
    if tt == 0:
        return [(0, 0), (1, 0)], [(2, 0)]
    blocks = [(g, kt) for g in range(N_GROUPS) for kt in range(2)]
    return blocks[:3], blocks[3:]


def program(nc, a, out):
    ST, NT = stages()
    ADA = [[ST[f"ada{layer}_{s}"] for s in range(3)] for layer in range(2)]
    ROW_BANKS = (5, 6, 7)
    TB, HB = turns(), halves()
    with ExitStack() as ctx:
        base = -(-nc.sbuf_base // 64) * 64
        arena = 229344 - base - 64
        ctx.enter_context(nc.sbuf_tensor("arena", [P, arena // 4], F32))

        def at(name, off, shape, dt=F32):
            n = int(np.prod(shape[1:])) * 4
            assert off + n <= arena, (name, off, n, arena)
            return nc.alloc_sbuf_tensor_at(name, shape, dt, offset=base + off)

        R_RAW, R_HI, R_LO = 0, 32768, 49152
        R_1H, R_1L, R_2, R_X, R_M = 65536, 98304, 131072, 163840, 196608
        raw = at("raw", R_RAW, [P, 4, TW])
        whi = at("whi", R_HI, [P, 2, TW], F32R)
        wlo = at("wlo", R_LO, [P, 2, TW], F32R)
        h4 = [at(n, r, [P, KC, 4 * P], F32R) for n, r in (("h4_hi", R_1H), ("h4_lo", R_1L))]
        hw = [at(n, r, [P, 32, TOK], F32R) for n, r in (("hw_hi", R_1H), ("hw_lo", R_1L))]
        x2 = [at(n, r, [P, KC, TOK], F32R) for n, r in (("x2_hi", R_2), ("x2_lo", R_2 + 16384))]
        X = at("X", R_X, [P, 4, D])
        off = [R_M]

        def keep(name, shape, dt=F32):
            t = at(name, off[0], shape, dt)
            off[0] += -(-int(np.prod(shape[1:])) * 4 // 32) * 32
            return t

        ident = keep("ident", [P, P])
        selrow = keep("selrow", [5, 2, P])
        selcol = keep("selcol", [5, 2])
        cond = keep("cond", [P, 2, KC])
        condh = keep("condh", [P, 2, KC], F32R)
        normg = keep("normg", [P, 2, KC])
        modA = keep("modA", [P, 2, KC])
        modB = keep("modB", [P, 2, KC])
        sink = keep("sink", [P, 16])
        nsink = keep("nsink", [P, 16])
        ssq = keep("ssq", [P, 4])
        ssq1 = keep("ssq1", [P, 4, 4])
        hss = keep("hss", [P, 16])
        ms = keep("ms", [P, 16])
        nt = keep("nt", [P, 16])
        hrs = keep("hrs", [P, 16])
        mx = keep("mx", [P, 2])
        nm = keep("nm", [P, 2])
        rs = keep("rs", [P, 4])
        es = keep("es", [P, 4])
        den = keep("den", [P, 2])
        rden = keep("rden", [P, 2])
        bn = keep("bn", [P, TT, 4, 6])
        mv = keep("mv", [P, TT, 2])
        nmr = keep("nmr", [P, TT])
        zero = keep("zero", [P, 1])
        waited = keep("waited", [P, 1])
        assert off[0] - R_M <= 4096, off[0] - R_M
        M1, M2 = R_M + 4096, R_M + 4096 + 8192
        gaterow = at("gaterow", M1, [5, D])
        adarow = at("adarow", R_2, [5, 3 * D])
        condL = at("condL", R_2 + 24576, [P, KC, P], F32R)
        tmod = at("tmod", R_2, [P, 2, 512])
        scr = at("scr", R_1L, [P, D])
        scr1 = at("scr1", M1, [P, PW])
        XN = at("XN", M2, [P, 2, D])
        G0 = at("G0", R_2, [P, 4, D])
        QS = at("QS", R_X, [P, 4, PW])
        qT = at("qT", R_X + 8192, [P, 4, 4 * P])
        kT = at("kT", R_X + 16384, [P, 4, 4 * P])
        V0 = at("V0", R_X + 24576, [P, 4, PW])
        masks = at("masks", M2, [P, 7 * P])
        tabs = at("tabs", M2 + 3584, [P, 2, TT, 2, HD])
        gqk = at("gqk", M2 + 7680, [P, 2, 2, HD])
        Sb = at("Sb", M2 + 9728, [P, 2, 512])
        PTb = at("PTb", M2 + 13824, [P, 4, P])
        SQ = at("SQ", M2 + 15872, [P, PW])
        gateB = at("gateB", M2, [P, 2, D])
        rtmp = at("rtmp", M2 + 16384, [P, PW])
        G1 = at("G1", R_2, [P, TT, D])
        cqT = [at(n, r, [P, 4, TOK], F32R) for n, r in (("cqT_hi", R_2 + 16384), ("cqT_lo", R_2 + 20480))]
        ckvT = [at(n, r, [P, 2, 512], F32R) for n, r in (("ckvT_hi", R_2 + 24576), ("ckvT_lo", R_2 + 28672))]
        cqS = at("cqS", R_X + 16384, [P, TT, 512])
        ckvS = at("ckvS", R_X + 20480, [P, 4, MLA_KVW])
        sqS = at("sqS", R_X + 26112, [P, 512])
        rtab = at("rtab", M2, [P, 2, TT, 2, 64])
        gpe = at("gpe", M2 + 2048, [P, 2, 2, 64])
        gqa = at("gqa", M2 + 3072, [P, 512])
        gkva = at("gkva", M2 + 5120, [P, 256])
        gnope = at("gnope", M2 + 6144, [P, 2, HD])
        gprod = at("gprod", M2 + 7168, [P, HD])
        kpT = at("kpT", M2 + 7680, [64, 4 * P])
        VL = at("VL", R_1H, [P, 4, D])
        KL = at("KL", R_1L, [P, 2, 4, 2 * HD])
        QP = at("QP", R_1L + 8192, [P, 2, TT, QBW])
        kTp = at("kTp", R_1L + 14336, [P, 2, 4 * P])
        qTp = at("qTp", R_1L + 18432, [P, 2, TOK])
        qpT = at("qpT", R_1L + 20480, [64, 2, TOK])
        Sm = at("Sm", R_1L + 22528, [P, 2, 512])
        PTm = at("PTm", R_1L + 26624, [P, 4, P])
        SQm = at("SQm", R_1L + 28672, [P, 1024])
        og1 = [at(n, r, [P, KC, TOK], F32R) for n, r in (("og1_hi", R_1H), ("og1_lo", R_1L))]
        gateB1 = at("gateB1", M2, [P, D])
        U = at("U", M1, [P, TT, D])
        bands = at("bands", R_X + 16384, [P, 4, TT, TOK])
        scaleB = at("scaleB", R_X + 24576, [P, D])
        pT = [at(n, r, [P, KC, TOK], F32R) for n, r in (("pT_hi", R_1H), ("pT_lo", R_1L))]
        yT = [at(n, r, [P, KC, TOK], F32R) for n, r in (("yT_hi", R_1H + 16384), ("yT_lo", R_1L + 16384))]
        lnB = at("lnB", M1, [P, 2, D])
        HS = at("HS", R_X + 16384, [P, TT, PW])
        qA = at("qA", R_1H, [P, N_GROUPS * 4, TOK])
        kA = at("kA", R_1H + 12288, [P, N_GROUPS * 4, TOK])
        SA = at("SA", R_1H + 24576, [P, 2, N_GROUPS * TOK])
        VA = at("VA", R_1L, [P, TT, N_GROUPS * 4 * HD])
        PTa = at("PTa", R_1L + 12288, [P, 6, P])
        OA = at("OA", R_1L + 16384, [P, TT, N_SLOTS * HD])
        ndm = at("ndm", R_X + 20480, [P, N_GROUPS, KEYS[0] + KEYS[1]])
        oT = [at(n, r, [P, 8, TOK], F32R) for n, r in (("oT_hi", R_2), ("oT_lo", R_2 + 8192))]

        PS = ctx.enter_context(nc.psum_tensor("PS", [P, 8, 512], F32))

        def sem(name):
            return ctx.enter_context(nc.semaphore(name))

        raw_landed = [sem(f"raw_landed{j}") for j in range(4)]
        hi_done, lo_done, tile_used = sem("hi_done"), sem("lo_done"), sem("tile_used")
        acc_full, acc_free = sem("acc_full"), sem("acc_free")
        rows_full, rows_free = sem("rows_full"), sem("rows_free")
        tr_full = [sem("tr_full0"), sem("tr_full1")]
        tr_free = [sem("tr_free0"), sem("tr_free1")]
        split_hi, mod_lo = sem("split_hi"), sem("mod_lo")
        dve_chain, act_chain = sem("dve_chain"), sem("act_chain")
        consts_in, cond_in, x_in, x_again, bias_in = (sem(n) for n in ("consts_in", "cond_in", "x_in", "x_again", "bias_in"))
        swa_in_, mla_in_, pool_in_, ln_in, ndm_in = (sem(n) for n in ("swa_in", "mla_in", "pool_in", "ln_in", "ndm_in"))
        out_done = sem("out_done")
        cond_hi, cond_ready, ss_ready, xn_ready = (sem(n) for n in ("cond_hi", "cond_ready", "ss_ready", "xn_ready"))
        cols_full, gate_kept = sem("cols_full"), sem("gate_kept")
        qk_ready, lat_ready, pair_ready = sem("qk_ready"), sem("lat_ready"), sem("pair_ready")
        part_stats, row_stats, hat = sem("part_stats"), sem("row_stats"), sem("hat")
        x_ready = [sem("x_ready0"), sem("x_ready1")]
        scaled = [sem("scaled0"), sem("scaled1")]
        sq_ready = sem("sq_ready")
        names = ("s_full", "s_free", "m_ready", "p_ready", "o_full", "o_free")
        swa, mla, dil = ({n: sem(f"{k}_{n}") for n in names} for k in ("swa", "mla", "dil"))

        def tile_at(st, b, q, k):
            n = q * st.tpp + k * st.kstep + st.tile % 4
            span = max(4, st.tstep) // 4
            return st.tile // 4 + b * span + n // 4, n % 4

        def two_ahead(st, b, q, k):
            I, j = tile_at(st, b, q, k)
            if st.ada or st.name == "swa_out":
                return I + 1, j
            return I + (j + 2) // 4, (j + 2) % 4

        def panel(st, b, q):
            return b if st.tpp >= 4 else b * (4 // st.tpp) + q

        def width(I, j, default=TW):
            if not isinstance(I, int):
                return default
            T = 4 * I + j
            if 0 <= T - ST["mla_ckv"].tile < 4:
                return 4 * MLA_KVW
            if 0 <= T - ST["mla_pair"].tile < 16:
                return (4 * QBW, 2 * PW)[T % 2]
            return TW

        def consumed(st, b, q, k):
            n = panel(st, b, q)
            if st.ada and k == st.tpp - 1:
                return rows_full, st.row(b) + 1
            if st.name == "mla_pair":
                return acc_full, st.acc + n * st.na + (2, 6)[k]
            if k == st.tpp - 1:
                return acc_full, st.acc + (n + 1) * st.na
            return tile_used, st.used + n * st.ustep + k * st.kstep + 1

        def gain_bias(eng, v, tt, number, c):
            n = 4 * number + c
            x = X[:, tt, c * PW:(c + 1) * PW]
            eng.wait_ge(hat, 2 * n + tt + 1)
            if c == 0:
                eng.wait_ge(ln_in, 16 * (number + 1))
            v.tensor_tensor(x, x, lnB[:, 0, c * PW:(c + 1) * PW], ALU.mult).then_inc(scaled[tt], 1)
            eng.wait_ge(scaled[tt], n + 1)
            v.tensor_tensor(x, x, lnB[:, 1, c * PW:(c + 1) * PW], ALU.add).then_inc(x_ready[tt], 1)

        block = ctx.enter_context(nc.Block())

        @block.gpsimd
        def _(pool):
            for number in range(4):
                for c in range(4):
                    gain_bias(pool, nc.gpsimd, 1, number, c)

        @block.sync
        def _(sp):
            sp.dma_start(cond[:], a["cond"]).then_inc(cond_in, 16)
            for j in range(4):
                sp.dma_start(raw[:, j, :], a["weights"][j]).then_inc(raw_landed[j], 16)
                if j == 3:
                    sp.dma_start(adarow[4:5, :], a["ada_b"][0]).then_inc(bias_in, 16)
                    sp.dma_start(X[:], a["x"]).then_inc(x_in, 16)
            w = a["weights"].rearrange("(i j) p n -> i j p n", j=4)

            def refill(i, waits):
                for j, (done, value) in enumerate(waits):
                    sp.wait_ge(done, value)
                    sp.dma_start(raw[:, j, :], w[bass.ds(i + 1, 1), j].rearrange("a p n -> (a p) n")).then_inc(raw_landed[j], 16)

            def refill_split(st):
                return lambda i: refill(i, [(lo_done, st.split(i, j)) for j in range(4)])

            def refill_ada(i):
                st = ADA[0][0]
                refill(i, [(lo_done, st.split(i, 0)), (lo_done, st.split(i, 1)),
                           (tile_used, 3 * i + 3), (rows_full, i + 1)])

            def refill_out_ada(b):
                st = ST["swa_out"]
                for k in range(4):
                    i = st.tile // 4 + 4 * b + k
                    refill(i, [(lo_done, st.split(i, 0)), (lo_done, st.split(i, 1)),
                               consumed(ADA[1][1], b, 0, k), consumed(ADA[1][2], b, 0, k)])

            first = [ST[n].tile // 4 for n in ("swa_kv", "swa_out", "mla_cq")]
            each(sp, 0, first[0], refill_ada)
            each(sp, first[0], first[1], refill_split(ST["swa_kv"]))
            each(sp, 0, 4, refill_out_ada)
            each(sp, first[2], NT // 4 - 1, refill_split(ST["mla_cq"]))
            for c in range(4):
                for tt in range(TT):
                    sp.wait_ge(x_ready[tt], 12 + c + 1)
                sp.dma_start(out[:, :, c * PW:(c + 1) * PW], X[:, 0:TT, c * PW:(c + 1) * PW]).then_inc(out_done, 16)
            sp.wait_ge(out_done, 16 * 4)

        @block.tensor
        def _(pe):
            mm, tr = nc.tensor.matmul, nc.tensor.transpose

            def tile_mm(st, b, q, k, lhs, banks, nch, w, tts, K, kc0, n0, slot=None):
                I, j = tile_at(st, b, q, k)
                pe.wait_ge(lo_done, st.split(I, j))
                for tt in tts:
                    bank = PS[:, banks[tt], 0:w]
                    if kc0 == 0:
                        need(pe, acc_free, n0 + tt - len(set(banks)) + 1)
                    for c in range(nch):
                        kc = kc0 + c
                        wh = whi[:, j % 2, c * w:(c + 1) * w]
                        wl = wlo[:, j % 2, c * w:(c + 1) * w]
                        xh, xl = (x[:, kc, tt * P:(tt + 1) * P] for x in lhs)
                        mm(bank, xh, wh, start=(kc == 0), stop=False)
                        mm(bank, xl, wh, start=False, stop=False)
                        last = mm(bank, xh, wl, start=False, stop=(kc == K - 1))
                    if kc0 + nch == K:
                        last.then_inc(acc_full, 1)
                    elif tt == tts[-1]:
                        last.then_inc(tile_used, 1)
                    if slot:
                        slot(k, tt)

            def gemm(st, b, lhs, q=0, w=PW, kc=0, slot=None, ks=None, before=None):
                K = 4 * st.tpp
                n = panel(st, b, q)
                view = [x[:, kc:kc + K, :] for x in lhs] if lhs else None
                for k in ks or range(st.tpp):
                    if before:
                        before(k)
                    tile_mm(st, b, q, k, view, list(range(st.na)), 4, w, list(range(st.na)), K, 4 * k,
                            st.acc + n * st.na, slot)

            def row_panel(st, b, ks=range(4)):
                o = PS[:, ROW_BANKS[st.sub], :]
                for k in ks:
                    I, j = tile_at(st, b, 0, k)
                    if st.direct(k):
                        pe.wait_ge(raw_landed[j], 16 * (I + 1))
                    else:
                        pe.wait_ge(lo_done, st.split(I, j))
                    if k == 0:
                        need(pe, rows_free, st.row(b) - 2)
                    for c in range(4):
                        kc = 4 * k + c
                        if st.direct(k):
                            last = mm(o, condL[:, kc, :].bitcast(F32), raw[:, j, c * PW:(c + 1) * PW],
                                      start=(kc == 0), stop=(kc == KC - 1))
                            continue
                        mm(o, condL[:, kc, :], whi[:, j % 2, c * PW:(c + 1) * PW], start=(kc == 0), stop=False)
                        last = mm(o, condL[:, kc, :], wlo[:, j % 2, c * PW:(c + 1) * PW], start=False, stop=(kc == KC - 1))
                    last.then_inc(rows_full if k == st.tpp - 1 else tile_used, 1)

            def bank_free(K, j):
                need(pe, tr_free[j], K)

            def turn(K, j, blocks, rows=P, waited=False):
                if not waited:
                    bank_free(K, j)
                for n, blk in enumerate(blocks):
                    last = tr(PS[0:rows, 4 + j, n * P:(n + 1) * P], blk, ident[:])
                last.then_inc(tr_full[j], 1)

            def turned(K):
                for j in range(2):
                    pe.wait_ge(tr_free[j], K)

            def modulation(layer):
                pe.wait_ge(rows_free, 12 * (layer + 1))
                pe.wait_ge(bias_in, 16 * (layer + 1))
                for c in range(2 * KC):
                    last = mm(PS[:, 7, 2 * c:2 * c + 2], adarow[:, c * P:(c + 1) * P], selcol[:],
                              start=True, stop=True)
                last.then_inc(cols_full, 1)

            def turn_rows(part, src, c0=0, c1=KC):
                for c in range(c0, c1):
                    turn(TB[part] + c // 2, c % 2, [src(tt, c) for tt in range(4)])

            def mod_panel(st, layer, src, first):
                turn_rows(f"mod{layer}", src, 0, first)

                def two_more(k, tt):
                    c = first + 2 * (st.na * k + tt)
                    if c < KC:
                        turn_rows(f"mod{layer}", src, c, c + 2)

                gemm(st, 0, h4, before=lambda k: pe.wait_ge(mod_lo, KC * layer + 4 * (k + 1)), slot=two_more)

            def turn_pairs(part, src, chunks=KC, first=0):
                for u in range(chunks // 2):
                    turn(TB[part] + first + u // 2, u % 2,
                         [src(tt, 2 * u + c) for c in range(2) for tt in range(TT)])

            def gate_rows(part, which):
                u = 0
                pe.wait_ge(gate_kept, 1 if part == "gate0" else 2)
                for s in which:
                    for p in range(4):
                        K, j = TB[part] + u // 2, u % 2
                        bank_free(K, j)
                        mm(PS[:, 4 + j, :], selrow[:, s, :], gaterow[:, p * PW:(p + 1) * PW],
                           start=True, stop=True).then_inc(tr_full[j], 1)
                        u += 1

            pe.wait_ge(cond_ready, 1)

            def ada(layer, b, ks=range(4)):
                for st in ADA[layer]:
                    row_panel(st, b, ks)

            ada(0, 0)
            each(pe, 1, 4, lambda b: ada(0, b))
            pe.wait_ge(consts_in, 16 * (len(CONSTS) - 1))
            modulation(0)
            pe.wait_ge(xn_ready, 4)
            st = ST["swa_kv"]
            mod_panel(st, 0, lambda tt, c: X[:, tt, c * P:(c + 1) * P], 6)

            def beside_heads(st, i, K, n, begin=None):
                def turn_head(k, h):
                    if k == 0 and begin:
                        begin(h)
                    if k == 3:
                        if h == 0:
                            pe.wait_ge(qk_ready, n)
                        turn(K + h // 2, h % 2, [QS[:, tt, h * HD:(h + 1) * HD] for tt in range(4)])

                gemm(st, i, h4, slot=turn_head)

            beside_heads(st, 1, TB["kT"], 4)

            def swa_scores(g, u):
                h, tt = u // 4, u % 4
                n = 16 * g + u
                if u == 0:
                    turned(TB["q0"] + 2 + 10 * g)
                need(pe, swa["s_free"], n)
                kg = kT[:, col(g, 1, 1), :].rearrange("p a n -> p (a n)")
                keys = kg[:, 0:512] if tt < TT else kg[:, 256:512]
                mm(PS[:, 6, 0:keys.shape[-1]], qT[:, h, tt * P:(tt + 1) * P], keys,
                   start=True, stop=True).then_inc(swa["s_full"], 1)

            def swa_turn(g, u, K):
                tt = u % 4
                pe.wait_ge(swa["p_ready"], 16 * g + u + 1)
                turn(K + u // 2, u % 2, [Sb[:, u % 2, c * P:(c + 1) * P] for c in range(4 if tt < TT else 2)])

            def swa_pv(g, u, K):
                tt = u % 4
                n = 16 * g + u
                pe.wait_ge(tr_free[u % 2], K + u // 2 + 1)
                need(pe, swa["o_free"], n)
                tiles = range(4) if tt < TT else range(TT, 4)
                for c, kt in enumerate(tiles):
                    last = mm(PS[:, 7, 0:HD], PTb[:, c, :], V0[:, kt, col(g, HD, HD)],
                              start=(c == 0), stop=(c == len(tiles) - 1))
                last.then_inc(swa["o_full"], 1)

            def swa_step(g, n, K):
                if n < 16:
                    swa_scores(g, n)
                if 1 <= n < 17:
                    swa_turn(g, n - 1, K)
                if 2 <= n:
                    swa_pv(g, n - 2, K)

            st = ST["swa_qg"]
            gemm(st, 0, h4)
            beside_heads(st, 1, TB["q0"], 8)

            def swa_group(i):
                K = TB["swa"] + 10 * (i - 1)
                gemm(st, 2 * i, h4, slot=lambda k, tt: swa_step(i - 1, 4 * k + tt, K))
                beside_heads(st, 2 * i + 1, K + 8, 8 + 4 * i, lambda h: swa_step(i - 1, 16 + h, K) if h < 2 else None)

            each(pe, 1, 4, swa_group)
            for n in range(18):
                swa_step(3, n, TB["swa_tail"])
            pe.wait_ge(swa["o_free"], 64)
            turn_rows("og0", lambda tt, c: G0[:, tt, c * P:(c + 1) * P])
            gate_rows("gate0", (0, 1))
            turned(TB["gate0"] + 4)
            st = ST["swa_out"]
            pe.wait_ge(acc_free, st.acc)
            pe.wait_ge(cond_ready, 2)

            def out_ada(i):
                for k in range(4):
                    gemm(st, i, h4, ks=(k,))
                    ada(1, i, (k,))

            each(pe, 0, 4, out_ada)

            modulation(1)
            pe.wait_ge(xn_ready, 8)

            pe.wait_ge(acc_free, ST["mla_cq"].acc)
            mod_panel(ST["mla_cq"], 1, lambda tt, c: (XN if tt < TT else X)[:, tt, c * P:(c + 1) * P], 8)
            pe.wait_ge(acc_free, ST["mla_ckv"].acc)
            gemm(ST["mla_ckv"], 0, h4, w=MLA_KVW)
            pe.wait_ge(acc_free, ST["mla_gate"].acc)
            for i in range(2):
                gemm(ST["mla_gate"], i, h4)
            pe.wait_ge(lat_ready, 3)
            turn_pairs("cq", lambda tt, c: cqS[:, tt, c * P:(c + 1) * P], 4)
            for c in range(2):
                turn(TB["ckv"], c, [ckvS[:, tt, c * P:(c + 1) * P] for tt in range(4)])
            for c in range(2):
                turn(TB["kpe"], c, [ckvS[:, 2 * c + t, 256:320] for t in range(2)], rows=64)
            each(pe, 2, 4, lambda i: gemm(ST["mla_gate"], i, h4))
            turned(TB["mla"])

            st = ST["mla_pair"]
            pe.wait_ge(acc_free, st.acc)

            def pair_mm(b, q, m):
                k, tt, lhs, w, nch = (0, m, cqT, QBW, 4) if m < 2 else (1, m - 2, ckvT, PW, 2)
                if tt == 0:
                    I, j = tile_at(st, b, q, k)
                    pe.wait_ge(lo_done, st.split(I, j))
                j = 2 * q + k
                pe.wait_ge(acc_free, st.acc + panel(st, b, q) * 6 + m - 3)
                o = PS[:, (6 * q + m) % 4, 0:w]
                for c in range(nch):
                    wh, wl = (t[:, j % 2, c * w:(c + 1) * w] for t in (whi, wlo))
                    xh, xl = (x[:, c, tt * P:(tt + 1) * P] for x in lhs)
                    mm(o, xh, wh, start=(c == 0), stop=False)
                    mm(o, xl, wh, start=False, stop=False)
                    last = mm(o, xh, wl, start=False, stop=(c == nch - 1))
                last.then_inc(acc_full, 1)

            def pair_turn(p, q, K):
                pe.wait_ge(pair_ready, p + 1)
                for h in range(2):
                    turn(K, h, [KL[:, q, tt, h * HD:(h + 1) * HD] for tt in range(4)])
                bank_free(K + 1, 1)
                turn(K + 1, 0, [QP[:, q, tt, h * 192:h * 192 + P] for h in range(2) for tt in range(TT)])
                turn(K + 1, 1, [QP[:, q, tt, h * 192 + P:(h + 1) * 192] for h in range(2) for tt in range(TT)], rows=64, waited=True)

            def mla_step(p, m, K):
                if m < 4:
                    h, tt = m // 2, m % 2
                    if m == 0:
                        turned(K)
                    need(pe, mla["s_free"], 4 * p + m)
                    mm(PS[:, 6, :], qTp[:, h, tt * P:(tt + 1) * P], kTp[:, h, :], start=True, stop=False)
                    mm(PS[:, 6, :], qpT[:, h, tt * P:(tt + 1) * P], kpT[:], start=False,
                       stop=True).then_inc(mla["s_full"], 1)
                if 1 <= m < 5:
                    u = m - 1
                    pe.wait_ge(mla["p_ready"], 4 * p + u + 1)
                    turn(K + u // 2, u % 2, [Sm[:, u % 2, c * P:(c + 1) * P] for c in range(4)])
                if 2 <= m:
                    u = m - 2
                    h = u // 2
                    pe.wait_ge(tr_free[u % 2], K + u // 2 + 1)
                    need(pe, mla["o_free"], 4 * p + u)
                    for c in range(4):
                        last = mm(PS[:, 7, 0:HD], PTm[:, c, :], VL[:, c, col(2 * p + h, HD, HD)],
                                  start=(c == 0), stop=(c == 3))
                    last.then_inc(mla["o_full"], 1)

            def mla_turn_att(p, q, product):
                K = TB["mla"] + 4 * p
                product(0)
                product(1)
                pair_turn(p, q, K)
                for m in range(6):
                    if m:
                        product(m + 1)
                    mla_step(p, m, K + 2)

            def mla_body(b):
                for q in range(2):
                    mla_turn_att(2 * b + q - 2, q, lambda m: pair_mm(b, q, m) if m < 6 else None)

            for q in range(2):
                for m in range(6):
                    pair_mm(0, q, m)
            each(pe, 1, 4, mla_body)
            for q in range(2):
                mla_turn_att(6 + q, q, lambda m: None)
            pe.wait_ge(mla["o_free"], 32)
            turn_pairs("og1", lambda tt, c: G1[:, tt, c * P:(c + 1) * P])
            gate_rows("gate1", (0,))
            turned(TB["og1"] + 4)
            st = ST["mla_out"]
            pe.wait_ge(acc_free, st.acc)
            each(pe, 0, 4, lambda i: gemm(st, i, og1))

            def turn_x(part):
                turn_pairs(part, lambda tt, c: X[:, tt, c * P:(c + 1) * P])
                turned(TB[part] + 4)

            st = ST["pool_in"]
            pe.wait_ge(acc_free, st.acc)
            turn_x("pool")

            def pooled(g):
                pe.wait_ge(acc_free, ST["pool_in"].acc + 2 * (g + 1))
                for u in range(2):
                    K, j = TB["band"] + g, u
                    bank_free(K, j)
                    for c in range(2):
                        f = g * PW + (2 * u + c) * P
                        o = PS[:, 4 + j, c * TOK:(c + 1) * TOK]
                        mm(o, U[:, 0, f:f + P], bands[:, g, 0, :], start=True, stop=False, skip_group_check=True)
                        last = mm(o[:, P:], U[:, 1, f:f + P], bands[:, g, 1, P:], start=False, stop=True,
                                  skip_group_check=True)
                    last.then_inc(tr_full[j], 1)

            for g in range(4):
                gemm(st, g, x2)
                if g == 0:
                    pe.wait_ge(pool_in_, 32)
                if g:
                    pooled(g - 1)
            pooled(3)
            st = ST["pool_group"]
            pe.wait_ge(acc_free, st.acc)
            for g in range(4):
                turned(TB["band"] + g + 1)
                gemm(st, g // 4, pT, q=g, kc=4 * g)
                if g:
                    pe.wait_ge(acc_free, st.acc + 2 * g)
                    turn_pairs("py", lambda tt, c: U[:, tt, (g - 1) * PW + c * P:(g - 1) * PW + (c + 1) * P], 4, g - 1)
            pe.wait_ge(acc_free, st.acc + 8)
            turn_pairs("py", lambda tt, c: U[:, tt, 3 * PW + c * P:3 * PW + (c + 1) * P], 4, 3)
            turned(TB["py"] + 4)
            st = ST["pool_out"]
            pe.wait_ge(acc_free, st.acc)
            each(pe, 0, 4, lambda i: gemm(st, i, yT))

            def normed_panel(st, part, number):
                def piece(c):
                    for tt in range(TT):
                        pe.wait_ge(x_ready[tt], 4 * number + c + 1)
                    for u in range(2):
                        turn(TB[part] + c, u, [X[:, tt, f * P:(f + 1) * P] for f in (4 * c + 2 * u, 4 * c + 2 * u + 1)
                                               for tt in range(TT)])

                piece(0)
                piece(1)
                gemm(st, 0, x2, before=lambda k: turned(TB[part] + k + 1),
                     slot=lambda k, tt: piece(k + 2) if tt == 1 and k < 2 else None)

            def mlp(layer, sq0):
                for half in range(2):
                    up, down = ST[f"up{layer}{half}"], ST[f"down{layer}{half}"]
                    K0, s0 = TB[up.name], sq0 + 16 * half

                    def turn_panel(i, k=1, tt=1):
                        if (k, tt) == (1, 1):
                            pe.wait_ge(sq_ready, s0 + 2 * i + 2)
                            for u in range(2):
                                turn(K0 + i, u, [HS[:, t, (2 * u + c) * P:(2 * u + c + 1) * P]
                                                 for c in range(2) for t in range(TT)])

                    pe.wait_ge(acc_free, up.acc)
                    if half == 0:
                        normed_panel(up, f"ln{2 * layer}", 2 * layer)
                    else:
                        gemm(up, 0, x2)
                    each(pe, 1, 8, lambda i: gemm(up, i, x2, slot=lambda k, tt: turn_panel(i - 1, k, tt)))
                    pe.wait_ge(acc_free, down.acc)
                    turned(K0 + 7)

                    def last_turned(k, tt):
                        turn_panel(7, k, tt)
                        if (k, tt) == (6, 1):
                            turned(K0 + 8)

                    gemm(down, 0, hw, slot=last_turned)
                    each(pe, 1, 4, lambda i: gemm(down, i, hw))

            mlp(0, 0)
            st = ST["qkv"]
            pe.wait_ge(acc_free, st.acc)

            def dil_step(hf, m, K):
                n = 8 * hf + m
                if m < 8:
                    s, tt = m // 2, m % 2
                    nk = KEYS[tt]
                    need(pe, dil["s_free"], n)
                    for g in range(N_GROUPS):
                        last = mm(PS[:, 2 + g // 2, (g % 2) * TOK:(g % 2) * TOK + nk], qA[:, 4 * g + s, tt * P:(tt + 1) * P],
                                  kA[:, 4 * g + s, 0:nk], start=True, stop=True, skip_group_check=True)
                    last.then_inc(dil["s_full"], 1)
                if 1 <= m < 9:
                    u = m - 1
                    tt = u % 2
                    pe.wait_ge(dil["p_ready"], 8 * hf + u + 1)
                    for j, part in enumerate(dil_parts(tt)):
                        turn(K + u, j, [SA[:, u % 2, g * TOK + kt * P:g * TOK + (kt + 1) * P] for g, kt in part])
                if 2 <= m:
                    u = m - 2
                    s, tt = u // 2, u % 2
                    for j in range(2):
                        pe.wait_ge(tr_free[j], K + u + 1)
                    need(pe, dil["o_free"], 8 * hf + u)
                    blocks = [x for part in dil_parts(tt) for x in part]
                    for c, (g, kt) in enumerate(blocks):
                        last = mm(PS[:, 7, 0:HD], PTa[:, c, :], VA[:, kt, (4 * g + s) * HD:(4 * g + s + 1) * HD],
                                  start=(c == 0), stop=(c == len(blocks) - 1))
                    last.then_inc(dil["o_full"], 1)

            for hf in range(2):
                def turn_qk(K, n):
                    pe.wait_ge(acc_free, n)
                    for u in range(2):
                        turn(K, u, [HS[:, t, (2 * u + c) * HD:(2 * u + c + 1) * HD] for c in range(2) for t in range(TT)])

                def group(g, first=False):
                    i = 9 * hf + 3 * g
                    K = TB[f"qk{hf}"] + 2 * g
                    if first:
                        normed_panel(st, "ln1", 1)
                    else:
                        gemm(st, i, x2)
                    gemm(st, i + 1, x2, slot=lambda k, tt: turn_qk(K, st.acc + 2 * i + 2) if (k, tt) == (0, 1) else None)
                    gemm(st, i + 2, x2, slot=lambda k, tt: turn_qk(K + 1, st.acc + 2 * i + 4) if (k, tt) == (0, 1) else None)

                if hf == 0:
                    group(0, True)
                each(pe, 1 - hf, N_GROUPS, group)
                turned(TB[f"att{hf}"])
                pe.wait_ge(acc_free, st.acc + 18 * (hf + 1))
                for m in range(10):
                    dil_step(hf, m, TB[f"att{hf}"])
            pe.wait_ge(dil["o_free"], 16)
            turn_pairs("ao", lambda tt, c: OA[:, tt, c * P:(c + 1) * P], 8)
            turned(TB["ao"] + 2)
            st = ST["attn_out"]
            pe.wait_ge(acc_free, st.acc)

            def out_body(b):
                for q in range(2):
                    gemm(st, b, oT, q=q)

            each(pe, 0, 2, out_body)
            mlp(1, 32)

        @block.scalar
        def _(act):
            f = nc.scalar.activation

            def copy(dst, src):
                return f(dst, src, ACT.Copy)

            def upper(I, j, b=None, st=None, q=0, k=0, w=TW):
                act.wait_ge(raw_landed[j], 16 * (I + 1))
                if st is not None:
                    act.wait_ge(*consumed(st, b, q, k))
                w = width(I, j, w)
                copy(whi[:, j % 2, 0:w], raw[:, j, 0:w]).then_inc(hi_done, 1)

            def panel_act(st, b, q=0, evac=None, slot=None, final=False, ks=None):
                n = panel(st, b, q)
                for k in ks or range(st.tpp):
                    if slot:
                        slot(k)
                    if evac and st.name == "mla_pair":
                        for m in ((0, 1), (2, 3, 4, 5))[k]:
                            act.wait_ge(acc_full, st.acc + n * st.na + m + 1)
                            evac(m).then_inc(acc_free, 1)
                    elif st.ada and k == st.tpp - 1:
                        act.wait_ge(rows_full, st.row(b) + 1)
                        evac(b).then_inc(rows_free, 1)
                    elif evac and k == st.tpp - 1:
                        for tt in range(st.na):
                            act.wait_ge(acc_full, st.acc + n * st.na + tt + 1)
                            evac(tt).then_inc(acc_free, 1)
                    if st.direct(k):
                        continue
                    I, j = two_ahead(st, b, q, k)
                    w = TW
                    if st.name == "mla_pair":
                        w = (4 * QBW, 2 * PW)[k]
                    if not (final and k >= st.tpp - 2):
                        upper(I, j, b, st, q, k, w)

            def split(K, j, hi):
                act.wait_ge(tr_full[j], K + 1)
                width_ = hi.shape[-1] * (hi.shape[1] if len(hi.shape) == 3 else 1)
                src = PS[:, 4 + j, 0:width_]
                if len(hi.shape) == 3:
                    src = src.rearrange("p (c t) -> p c t", c=hi.shape[1])
                copy(hi, src).then_inc(split_hi, 1)

            def take(K, j, dst, src):
                act.wait_ge(tr_full[j], K + 1)
                copy(dst, src).then_inc(tr_free[j], 1)

            def load(dst, src, s):
                act.dma_start(dst, src).then_inc(s, 16)

            for (name, _), t in zip(CONSTS, (ident, selrow, selcol, cond, normg, sink)):
                if name != "cond":
                    load(t[:], a[name], consts_in)
            load(masks[:], a["masks"], swa_in_)
            for w in range(2):
                load(tabs[:, w], a["rope128"], swa_in_)
            load(gqk[:], a["gqk"], swa_in_)

            act.wait_ge(cond_in, 16)
            f(cond[:], cond[:], ACT.Silu).then_inc(act_chain, 1)
            act.wait_ge(act_chain, 1)
            copy(condh[:], cond[:]).then_inc(cond_hi, 1)
            upper(0, 0)
            upper(0, 1)

            def squares(tt, done=0):
                need(act, ss_ready, done + tt)
                f(scr[:], X[:, tt, :], ACT.Square, accum_out=ssq[:, tt:tt + 1]).then_inc(ss_ready, 1)

            def ada(layer, b, slot=None, ks=None):
                for st in ADA[layer]:
                    dst = lambda b: adarow[0:4, st.sub * PW:(st.sub + 1) * PW] if isinstance(b, int) and b == 0 \
                        else adarow[0:4, bass.ds(b * 3 * PW + st.sub * PW, PW)]
                    panel_act(st, b, evac=lambda b: copy(dst(b), PS[0:4, ROW_BANKS[st.sub], :]),
                              slot=slot if st.sub == 0 else None, ks=ks)

            def stats0(k):
                if k == 0:
                    act.wait_ge(x_in, 16)
                squares(k)

            ada(0, 0, stats0)
            each(act, 1, 4, lambda b: ada(0, b))

            def mod_split(part):
                for c in range(KC):
                    K, j = TB[part] + c // 2, c % 2
                    act.wait_ge(tr_free[j], K + 1)
                    copy(h4[0][:, c, :], tmod[:, j, :]).then_inc(split_hi, 1)

            mod_split("mod0")
            st = ST["swa_kv"]
            panel_act(st, 0, evac=lambda tt: copy(QS[:, tt, :], PS[:, tt, :]))

            def take_heads(K, dst, k):
                for h in range(4 if k == 3 else 0):
                    take(K + h // 2, h % 2, dst[:, h, :], PS[:, 4 + h % 2, :])

            panel_act(st, 1, evac=lambda tt: copy(V0[:, tt, :], PS[:, tt, :]), slot=lambda k: take_heads(TB["kT"], kT, k))

            def q_evac(tt):
                return copy(QS[:, tt, :], PS[:, tt, :])

            def g_evac(i):
                return lambda tt: f(G0[:, tt, col(i, PW)], PS[:, tt, :], ACT.Silu)

            def swa_step(g, n, K):
                if n < 16:
                    b, nk = n % 2, (512 if n % 4 < TT else 256)
                    act.wait_ge(swa["m_ready"], 16 * g + n + 1)
                    f(Sb[:, b, 0:nk], Sb[:, b, 0:nk], ACT.Exp, bias=nm[:, b:b + 1], scale=SWA_SCALE,
                      accum_out=rs[:, n % 4:n % 4 + 1])
                    f(es[:, n % 4:n % 4 + 1], sink[:, col(4 * g + n // 4, 1, 1)], ACT.Exp,
                      bias=nm[:, b:b + 1]).then_inc(swa["p_ready"], 1)
                if 1 <= n < 17:
                    u = n - 1
                    nk = 512 if u % 4 < TT else 256
                    need(act, swa["o_full"], 16 * g + u)
                    take(K + u // 2, u % 2, PTb[:, 0:nk // P, :],
                         PS[:, 4 + u % 2, 0:nk].rearrange("p (c t) -> p c t", c=nk // P))

            st = ST["swa_qg"]
            panel_act(st, 0, evac=q_evac)
            panel_act(st, 1, evac=g_evac(0), slot=lambda k: take_heads(TB["q0"], qT, k))

            def swa_group(i):
                K = TB["swa"] + 10 * (i - 1)

                def slot(k):
                    for tt in range(4):
                        swa_step(i - 1, 4 * k + tt, K)

                panel_act(st, 2 * i, evac=q_evac, slot=slot)
                panel_act(st, 2 * i + 1, evac=g_evac(i),
                          slot=lambda k: swa_step(i - 1, 16, K) if k == 0 else take_heads(K + 8, qT, k))

            each(act, 1, 4, swa_group)
            for n in range(17):
                swa_step(3, n, TB["swa_tail"])

            def og_split(part, u0, u1, hi):
                for u in range(u0, u1):
                    split(TB[part] + u // 2, u % 2, hi(u))

            og_split("og0", 0, 1, lambda u: h4[0][:, u, :])
            load(X[:], a["x"], x_again)
            og_split("og0", 1, KC, lambda u: h4[0][:, u, :])
            load(adarow[4:5, :], a["ada_b"][1], bias_in)
            for u in range(8):
                take(TB["gate0"] + u // 2, u % 2, gateB[:, u // 4, u % 4 * PW:(u % 4 + 1) * PW], PS[:, 4 + u % 2, :])
            def stats1(i, tt):
                act.wait_ge(acc_free, ST["swa_out"].acc + 4 * i + tt + 1)
                act.wait_ge(ss_ready, 4 + 4 * i + tt)
                f(scr1[:], X[:, tt, col(i, PW)], ACT.Square, accum_out=ssq1[:, tt, col(i, 1, 1)]).then_inc(ss_ready, 1)

            def out_ada(i, stats=True):
                for k in range(4):
                    panel_act(ST["swa_out"], i, ks=(k,))
                    ada(1, i, slot=(lambda tt: stats1(i - 1, tt)) if stats else None, ks=(k,))

            out_ada(0, False)
            each(act, 1, 4, out_ada)
            for tt in range(4):
                stats1(3, tt)
            mod_split("mod1")
            load(gpe[:], a["gpe"], mla_in_)
            for w in range(2):
                load(rtab[:, w], a["rope64"], mla_in_)
            load(gqa[:], a["gqa"], mla_in_)
            load(gkva[:], a["gkva"], mla_in_)
            load(gnope[:], a["gnope"], mla_in_)
            panel_act(ST["mla_cq"], 0, evac=lambda tt: copy(cqS[:, tt, :], PS[:, tt, :]))
            panel_act(ST["mla_ckv"], 0, evac=lambda tt: copy(ckvS[:, tt, :], PS[:, tt, 0:MLA_KVW]))

            def g1_evac(i):
                return lambda tt: f(G1[:, tt, col(i, PW)], PS[:, tt, :], ACT.Silu)

            st = ST["mla_gate"]
            for i in range(2):
                panel_act(st, i, evac=g1_evac(i))
            for u in range(2):
                split(TB["cq"], u, cqT[0][:, 2 * u:2 * u + 2, :])
            for u in range(2):
                split(TB["ckv"], u, ckvT[0][:, u, :])
            for u in range(2):
                take(TB["kpe"], u, kpT[:, u * TOK:(u + 1) * TOK], PS[0:64, 4 + u, 0:TOK])
            panel_act(st, 2, evac=g1_evac(2))
            panel_act(st, 3, evac=g1_evac(3))

            st = ST["mla_pair"]

            def pair_evac(p, q, m):
                act.wait_ge(acc_full, st.acc + 6 * p + m + 1)
                o = PS[:, (6 * q + m) % 4, :]
                if m < 2:
                    return copy(QP[:, q, m, :], o[:, 0:QBW]).then_inc(acc_free, 1)
                h = o.rearrange("p (h s e) -> p h s e", h=2, s=2)
                copy(KL[:, q, m - 2, :].rearrange("p (h e) -> p h e", h=2), h[:, :, 0])
                copy(VL[:, m - 2, col(p, 2 * HD, 2 * HD)].rearrange("p (h e) -> p h e", h=2), h[:, :, 1]).then_inc(acc_free, 1)

            def pair_take(K):
                for h in range(2):
                    take(K, h, kTp[:, h, :], PS[:, 4 + h, :])
                take(K + 1, 0, qTp[:].rearrange("p h t -> p (h t)"), PS[:, 4, :])
                take(K + 1, 1, qpT[:].rearrange("p h t -> p (h t)"), PS[0:64, 5, :])

            def mla_step(p, m, K):
                if m < 4:
                    b = m % 2
                    act.wait_ge(mla["m_ready"], 4 * p + m + 1)
                    f(Sm[:, b, :], Sm[:, b, :], ACT.Exp, bias=nm[:, b:b + 1], scale=MLA_SCALE,
                      accum_out=rs[:, m:m + 1]).then_inc(mla["p_ready"], 1)
                if m:
                    u = m - 1
                    need(act, mla["o_full"], 4 * p + u)
                    take(K + u // 2, u % 2, PTm[:], PS[:, 4 + u % 2, :].rearrange("p (c t) -> p c t", c=4))

            def pair_part(b, q, m):
                pair_evac(2 * b + q, q, m)
                if m in (1, 5):
                    k = m // 5
                    I, j = two_ahead(st, b, q, k)
                    upper(I, j, b, st, q, k, (4 * QBW, 2 * PW)[k])

            def mla_turn_att(p, q, part):
                K = TB["mla"] + 4 * p
                pair_take(K)
                part(0)
                part(1)
                for m in range(5):
                    if m:
                        part(m + 1)
                    mla_step(p, m, K + 2)

            def mla_body(b):
                for q in range(2):
                    mla_turn_att(2 * b + q - 2, q, lambda m: pair_part(b, q, m) if m < 6 else None)

            for q in range(2):
                for m in range(6):
                    pair_part(0, q, m)
            each(act, 1, 3, mla_body)
            mla_body(3)
            for q in range(2):
                mla_turn_att(6 + q, q, lambda m: None)
            load(bands[:], a["bands"], pool_in_)
            load(scaleB[:], a["pool_scale"], pool_in_)
            og_split("og1", 0, 8, lambda u: og1[0][:, 2 * u:2 * u + 2, :])
            for u in range(4):
                take(TB["gate1"] + u // 2, u % 2, gateB1[:, u * PW:(u + 1) * PW], PS[:, 4 + u % 2, :])
            each(act, 0, 4, lambda i: panel_act(ST["mla_out"], i))

            def split_x(part):
                og_split(part, 0, 8, lambda u: x2[0][:, 2 * u:2 * u + 2, :])

            split_x("pool")

            def normed_x(part, number):
                act.wait_ge(row_stats, number + 1)
                for c in range(4):
                    for tt in range(TT):
                        x = X[:, tt, c * PW:(c + 1) * PW]
                        f(x, x, ACT.Identity, bias=nmr[:, tt:tt + 1], scale=hrs[:, tt:tt + 1]).then_inc(hat, 1)
                    if c and part:
                        split_piece(part, c - 1)

            def split_piece(part, c):
                og_split(part, 2 * c, 2 * c + 2, lambda u: x2[0][:, 2 * u:2 * u + 2, :])

            def u_evac(g):
                return lambda tt: copy(U[:, tt, g * PW:(g + 1) * PW], PS[:, tt, :])

            for g in range(4):
                panel_act(ST["pool_in"], g, evac=u_evac(g))
                if g:
                    og_split("band", 2 * g - 2, 2 * g, lambda u: pT[0][:, 2 * u:2 * u + 2, :])
            og_split("band", 6, 8, lambda u: pT[0][:, 2 * u:2 * u + 2, :])
            for g in range(4):
                panel_act(ST["pool_group"], 0, q=g)
                if g:
                    og_split("py", 2 * g - 2, 2 * g, lambda u: yT[0][:, 2 * u:2 * u + 2, :])
            og_split("py", 6, 8, lambda u: yT[0][:, 2 * u:2 * u + 2, :])
            load(lnB[:], a["ln"][0], ln_in)
            load(ndm[:], a["ndm"], ndm_in)
            each(act, 0, 4, lambda i: panel_act(ST["pool_out"], i))

            def mlp(layer):
                for half in range(2):
                    up, down = ST[f"up{layer}{half}"], ST[f"down{layer}{half}"]

                    def relu(tt):
                        return f(HS[:, tt, :], PS[:, tt, :], ACT.Relu)

                    def split_panel(i, k):
                        if k == 2:
                            for u in range(2):
                                split(TB[up.name] + i, u, hw[0][:, bass.ds(4 * i + 2 * u, 2), :] if not isinstance(i, int)
                                      else hw[0][:, 4 * i + 2 * u:4 * i + 2 * u + 2, :])

                    if half == 0:
                        normed_x(f"ln{2 * layer}", 2 * layer)
                    panel_act(up, 0, evac=relu,
                              slot=lambda k: split_piece(f"ln{2 * layer}", 3) if half == 0 and k == 1 else None)
                    each(act, 1, 8, lambda i: panel_act(up, i, evac=relu, slot=lambda k: split_panel(i - 1, k)))
                    if half == 0:
                        for tt in range(TT):
                            act.wait_ge(x_ready[tt], 4 * (2 * layer + 1))
                        load(lnB[:], a["ln"][2 * layer + 1], ln_in)
                    panel_act(down, 0, slot=lambda k: split_panel(7, k))
                    last = layer == 1 and half == 1
                    each(act, 1, 3 if last else 4, lambda i: panel_act(down, i))
                    if last:
                        panel_act(down, 3, final=True)

            mlp(0)

            normed_x("ln1", 1)
            for tt in range(TT):
                act.wait_ge(x_ready[tt], 4 * 2)
            load(lnB[:], a["ln"][2], ln_in)
            st = ST["qkv"]
            for hf in range(2):
                def take_qk(K, dst, g):
                    for u in range(2):
                        take(K, u, dst[:, bass.ds(4 * g + 2 * u, 2), :], PS[:, 4 + u, :].rearrange("p (h t) -> p h t", h=2))

                def stage(tt):
                    return copy(HS[:, tt, :], PS[:, tt, :])

                def group(g, first=False):
                    i = 9 * hf + 3 * g
                    K = TB[f"qk{hf}"] + 2 * g
                    panel_act(st, i, evac=stage, slot=lambda k: split_piece("ln1", 3) if first and k == 1 else None)
                    panel_act(st, i + 1, evac=stage, slot=lambda k: take_qk(K, qA, g) if k == 1 else None)
                    panel_act(st, i + 2, evac=lambda tt: copy(VA[:, tt, col(g, PW)], PS[:, tt, :]),
                              slot=lambda k: take_qk(K + 1, kA, g) if k == 1 else None)

                if hf == 0:
                    group(0, True)
                each(act, 1 - hf, N_GROUPS, group)
                K = TB[f"att{hf}"]
                for m in range(9):
                    n = 8 * hf + m
                    if m < 8:
                        b, nk = m % 2, KEYS[m % 2]
                        s = SA[:, b, :].rearrange("p (g t) -> p g t", g=N_GROUPS)[:, :, 0:nk]
                        act.wait_ge(dil["m_ready"], n + 1)
                        f(s, s, ACT.Exp, bias=nm[:, b:b + 1], scale=SWA_SCALE,
                          accum_out=rs[:, m % 4:m % 4 + 1]).then_inc(dil["p_ready"], 1)
                    if m:
                        u = m - 1
                        need(act, dil["o_full"], n - 1)
                        at_ = 0
                        for j, part in enumerate(dil_parts(u % 2)):
                            nb = len(part)
                            take(K + u, j, PTa[:, at_:at_ + nb, :],
                                 PS[:, 4 + j, 0:nb * P].rearrange("p (c t) -> p c t", c=nb))
                            at_ += nb
            og_split("ao", 0, 4, lambda u: oT[0][:, 2 * u:2 * u + 2, :])

            def out_body(b):
                for q in range(2):
                    panel_act(ST["attn_out"], b, q)

            each(act, 0, 2, out_body)
            mlp(1)
            normed_x(None, 3)

        @block.vector
        def _(dve):
            v = nc.vector
            C = Chain(dve, dve_chain)

            def rest(I, j, w, n):
                dve.wait_ge(hi_done, n)
                w = width(I, j, w)
                v.tensor_tensor(wlo[:, j % 2, 0:w], raw[:, j, 0:w], whi[:, j % 2, 0:w],
                                ALU.subtract).then_inc(lo_done, 1)

            def panel_dve(st, b, q=0, evac=None, slot=None, final=False, ks=None, after=None):
                n = panel(st, b, q)
                for k in ks or range(st.tpp):
                    if slot:
                        slot(k)
                    if evac and k == st.tpp - 1:
                        for tt in range(st.na):
                            dve.wait_ge(acc_full, st.acc + n * st.na + tt + 1)
                            evac(tt).then_inc(acc_free, 1)
                    if after and k == st.tpp - 1:
                        after()
                    if st.direct(k):
                        continue
                    I, j = two_ahead(st, b, q, k)
                    w = (4 * QBW, 2 * PW)[k] if st.name == "mla_pair" else TW
                    if not (final and k >= st.tpp - 2):
                        rest(I, j, w, st.split(*tile_at(st, b, q, k)) + 2)

            def lower(part, u, hi, lo, first=None):
                K, j = TB[part] + u // 2, u % 2
                dve.wait_ge(split_hi, HB[part] + u + 1)
                n = hi.shape[-1] * (hi.shape[1] if len(hi.shape) == 3 else 1)
                src = PS[:, 4 + j, 0:n]
                if len(hi.shape) == 3:
                    src = src.rearrange("p (c t) -> p c t", c=hi.shape[1])
                v.tensor_tensor(lo, src, hi, ALU.subtract).then_inc(tr_free[j], 1)

            def rsqrt(*terms):
                for c, src, n, eps in terms:
                    C(v.tensor_scalar(ms[:, c], src, 1.0 / n, eps, ALU.mult, ALU.add))
                c = slice(terms[0][0].start, terms[-1][0].stop)
                x, y, t = ms[:, c], hrs[:, c], nt[:, c]
                C(v.tensor_scalar(t.bitcast(I32), x.bitcast(I32), 1, None, ALU.logical_shift_right))
                C(v.tensor_scalar(y.bitcast(I32), t.bitcast(I32), -1.0, float(0x5F3759DF), ALU.mult, ALU.add))
                for _ in range(3):
                    C(v.scalar_tensor_tensor(t, x, -0.5, y, ALU.mult, ALU.mult))
                    C(v.tensor_tensor(t, t, y, ALU.mult))
                    C(v.scalar_tensor_tensor(y, t, 1.5, y, ALU.add, ALU.mult))

            def place_cond():
                c4 = condL[:, :, 0:4].rearrange("p k (j s) -> p j k s", s=2)
                C(v.memset(condL[:].bitcast(F32), 0.0))
                C.tick(v.tensor_copy(c4[:, :, :, 0], condh[:]))
                v.tensor_tensor(c4[:, :, :, 1], cond[:], condh[:], ALU.subtract).then_inc(cond_ready, 1)

            dve.wait_ge(cond_hi, 1)
            C(v.memset(ms[:], 1.0))
            place_cond()
            C.wait()
            rest(0, 0, TW, 1)
            rest(0, 1, TW, 2)
            dve.wait_ge(consts_in, 16 * (len(CONSTS) - 1))
            C(v.memset(zero[:], 0.0))
            C(v.tensor_scalar(nsink[:], sink[:], -1.0, None, ALU.mult))

            def normed(layer, dst):
                dve.wait_ge(ss_ready, (4, 20)[layer])
                if layer:
                    C(v.tensor_reduce(ssq[:], ssq1[:], AX, ALU.add))
                rsqrt((slice(0, 4), ssq[:], D, EPS))
                for tt in range(4):
                    v.tensor_scalar(dst(tt), X[:, tt, :], hrs[:, tt:tt + 1], None, ALU.mult).then_inc(xn_ready, 1)

            def modulated(layer, part):
                dve.wait_ge(cols_full, layer + 1)
                cols = PS[:, 7, 0:4 * KC].rearrange("p (s c j) -> p s j c", s=2, j=2)
                g = normg[:, layer:layer + 1, :].broadcast_to([P, 2, KC])
                C(v.tensor_scalar(modA[:], cols[:, 1], 1.0, None, ALU.add))
                C.tick(v.tensor_tensor(modA[:], modA[:], g, ALU.mult))
                C(v.tensor_copy(modB[:], cols[:, 0]))
                v.tensor_copy(gaterow[:], adarow[:, 2 * D:3 * D]).then_inc(gate_kept, 1)
                dve.wait_ge(gate_kept, layer + 1)
                for c in range(KC + 1):
                    if c < KC:
                        K, j = TB[part] + c // 2, c % 2
                        dve.wait_ge(tr_full[j], K + 1)
                        need(dve, mod_lo, KC * layer + c - 1)
                        for s in range(2):
                            last = v.tensor_scalar(tmod[:, j, s * TOK:(s + 1) * TOK], PS[:, 4 + j, s * TOK:(s + 1) * TOK],
                                                   modA[:, s, c:c + 1], modB[:, s, c:c + 1], ALU.mult, ALU.add)
                        last.then_inc(tr_free[j], 1)
                    if c:
                        dve.wait_ge(split_hi, HB[part] + c)
                        v.tensor_tensor(h4[1][:, c - 1, :], tmod[:, (c - 1) % 2, :], h4[0][:, c - 1, :],
                                        ALU.subtract).then_inc(mod_lo, 1)

            def ada(layer, b, ks=None):
                for st in ADA[layer]:
                    panel_dve(st, b, ks=ks)

            ada(0, 0)
            normed(0, lambda tt: X[:, tt, :])
            each(dve, 1, 4, lambda b: ada(0, b))
            modulated(0, "mod0")
            dve.wait_ge(swa_in_, 16 * 4)
            for w in range(2):
                for s in range(2):
                    C.tick(v.tensor_tensor(tabs[:, w, :, s, :], tabs[:, w, :, s, :],
                                           gqk[:, w, s:s + 1, :].broadcast_to([P, TT, HD]), ALU.mult))
            C.wait()

            def heads(t):
                return t.rearrange("p (h e) -> p h e", h=4)

            def head_norm(acc, w, tt, done):
                x = heads(QS[:, tt, :])
                q4 = heads(SQ[:])
                dve.wait_ge(acc_free, acc + tt + 1)
                need(dve, qk_ready, done + tt)
                C(v.tensor_tensor(SQ[:], QS[:, tt, :], QS[:, tt, :], ALU.mult))
                C(v.tensor_reduce(hss[:, 0:4], q4, AX, ALU.add))
                rsqrt((slice(0, 4), hss[:, 0:4], HD, EPS))
                C(v.tensor_tensor(x, x, hrs[:, 0:4].unsqueeze(2).broadcast_to([P, 4, HD]), ALU.mult))
                if tt < TT:
                    xs = QS[:, tt, :].rearrange("p (h s e) -> p h s e", s=2, e=32)
                    qs = SQ[:].rearrange("p (h s e) -> p h s e", s=2, e=32)
                    sn = tabs[:, w, tt, 1, :].rearrange("p (a s e) -> p a s e", s=2, e=32)
                    for s in range(2):
                        for h in range(4):
                            C.tick(v.tensor_tensor(qs[:, 2 * h:2 * h + 2, s, :], xs[:, 2 * h:2 * h + 2, 1 - s, :],
                                                   sn[:, :, s, :], ALU.mult))
                    C.wait()
                    C(v.tensor_tensor(x, x, tabs[:, w, tt, 0:1, :].broadcast_to([P, 4, HD]), ALU.mult))
                    last = v.tensor_tensor(QS[:, tt, :], QS[:, tt, :], SQ[:], ALU.add)
                else:
                    last = v.tensor_tensor(x, x, gqk[:, w, 0:1, :].broadcast_to([P, 4, HD]), ALU.mult)
                last.then_inc(qk_ready, 1)

            st = ST["swa_kv"]
            panel_dve(st, 0)

            def norm_heads(k, acc, w, done):
                for tt in ((0, 1), (2,), (3,), ())[k]:
                    head_norm(acc, w, tt, done)

            panel_dve(st, 1, slot=lambda k: norm_heads(k, ST["swa_kv"].acc, 1, 0))
            st = ST["swa_qg"]

            def swa_step(g, n):
                if n < 16:
                    h, tt, b = n // 4, n % 4, n % 2
                    nk = 512 if tt < TT else 256
                    m0 = (3 * P, 0, P, P)[tt]
                    dve.wait_ge(swa["s_full"], 16 * g + n + 1)
                    v.memset(waited[:], 0.0)
                    v.tensor_tensor_reduce(Sb[:, b, 0:nk], PS[:, 6, 0:nk], masks[:, m0:m0 + nk], 1.0, -3e38,
                                           ALU.add, ALU.max, mx[:, b:b + 1]).then_inc(swa["s_free"], 1)
                    dve.wait_ge(swa["s_free"], 16 * g + n + 1)
                    v.tensor_scalar(nm[:, b:b + 1], mx[:, b:b + 1], -SWA_SCALE, nsink[:, col(4 * g + h, 1, 1)],
                                    ALU.mult, ALU.min).then_inc(swa["m_ready"], 1)
                if n >= 2:
                    u = n - 2
                    h, tt, b = u // 4, u % 4, u % 2
                    dve.wait_ge(swa["p_ready"], 16 * g + u + 1)
                    C(v.tensor_tensor(den[:, b:b + 1], rs[:, u % 4:u % 4 + 1], es[:, u % 4:u % 4 + 1], ALU.add))
                    C(v.reciprocal(rden[:, b:b + 1], den[:, b:b + 1]))
                    dve.wait_ge(swa["o_full"], 16 * g + u + 1)
                    gate = G0[:, tt, col(4 * g + h, HD, HD)]
                    v.scalar_tensor_tensor(gate, PS[:, 7, 0:HD], rden[:, b:b + 1], gate, ALU.mult,
                                           ALU.mult).then_inc(swa["o_free"], 1)

            panel_dve(st, 0)
            panel_dve(st, 1, slot=lambda k: norm_heads(k, st.acc, 0, 4))

            def swa_group(i):
                def slot(k):
                    for tt in range(4):
                        swa_step(i - 1, 4 * k + tt)

                panel_dve(st, 2 * i, slot=slot)

                def heads_slot(k):
                    for n in (16, 17) if k == 0 else ():
                        swa_step(i - 1, n)
                    norm_heads(k, st.acc + 8 * i, 0, 4 + 4 * i)

                panel_dve(st, 2 * i + 1, slot=heads_slot)

            counted_loop(dve, (C,), 1, 4, swa_group, (110,))
            for n in range(18):
                swa_step(3, n)
            for u in range(KC):
                lower("og0", u, h4[0][:, u, :], h4[1][:, u, :])

            def residual(st, i, gate, tts, ks=None):
                def evac(tt):
                    dve.wait_ge(acc_free, st.acc + st.na * i + tt)
                    C(v.tensor_tensor(rtmp[:], PS[:, tt, :], gate(tt, col(i, PW)), ALU.mult))
                    return v.tensor_tensor(X[:, tt, col(i, PW)], X[:, tt, col(i, PW)], rtmp[:], ALU.add)
                panel_dve(st, i, evac=evac, ks=ks)

            place_cond()
            for j in range(2):
                dve.wait_ge(tr_free[j], TB["gate0"] + 4)
            dve.wait_ge(x_again, 16)

            def out_ada(i):
                for k in range(4):
                    residual(ST["swa_out"], i, lambda tt, c: gateB[:, tt // TT, c], 4, ks=(k,))
                    ada(1, i, (k,))

            counted_loop(dve, (C,), 0, 4, out_ada, (4,))

            normed(1, lambda tt: (XN if tt < TT else X)[:, tt, :])
            modulated(1, "mod1")
            panel_dve(ST["mla_cq"], 0)

            def latents(k):
                if k == 0:
                    dve.wait_ge(mla_in_, 16 * 6)
                    for w in range(2):
                        for s in range(2):
                            C.tick(v.tensor_tensor(rtab[:, w, :, s, :], rtab[:, w, :, s, :],
                                                   gpe[:, w, s:s + 1, :].broadcast_to([P, TT, 64]), ALU.mult))
                    C(v.tensor_tensor(gprod[:], gnope[:, 0, :], gnope[:, 1, :], ALU.mult))
                    dve.wait_ge(acc_free, ST["mla_cq"].acc + 2)
                if k < TT:
                    x = cqS[:, k, :]
                    C(v.tensor_tensor(sqS[:], x, x, ALU.mult))
                    C(v.tensor_reduce(hss[:, 0:1], sqS[:], AX, ALU.add))
                    rsqrt((slice(0, 1), hss[:, 0:1], 512, EPS))
                    v.scalar_tensor_tensor(x, x, hrs[:, 0:1], gqa[:], ALU.mult, ALU.mult).then_inc(lat_ready, 1)

            panel_dve(ST["mla_ckv"], 0, slot=latents)

            def rope64(x, w, tts, heads_, sq):
                xs = x.rearrange("p t h (a s e) -> p t h a s e", s=2, e=16)
                qs = sq.rearrange("p t h (a s e) -> p t h a s e", s=2, e=16)
                for tt in tts:
                    sn = rtab[:, w, tt, 1, :].rearrange("p (a s e) -> p a s e", s=2, e=16)
                    for h in range(heads_):
                        for s in range(2):
                            C.tick(v.tensor_tensor(qs[:, tt, h, :, s, :], xs[:, tt, h, :, 1 - s, :], sn[:, :, s, :], ALU.mult))
                C.wait()
                for tt in tts:
                    C.tick(v.tensor_tensor(x[:, tt], x[:, tt], rtab[:, w, tt, 0:1, :].broadcast_to([P, heads_, 64]), ALU.mult))
                C.wait()

            def latents_kv(tt):
                dve.wait_ge(acc_free, ST["mla_ckv"].acc + 4)
                x, y = ckvS[:, tt, 0:256], ckvS[:, tt, 256:320]
                C(v.tensor_tensor(sqS[:, 0:MLA_KVW], ckvS[:, tt, :], ckvS[:, tt, :], ALU.mult))
                C.tick(v.tensor_reduce(hss[:, 0:1], sqS[:, 0:256], AX, ALU.add))
                C(v.tensor_reduce(hss[:, 1:2], sqS[:, 256:320], AX, ALU.add))
                rsqrt((slice(0, 1), hss[:, 0:1], 256, EPS), (slice(1, 2), hss[:, 1:2], 64, EPS))
                C(v.scalar_tensor_tensor(x, x, hrs[:, 0:1], gkva[:], ALU.mult, ALU.mult))
                if tt < TT:
                    C(v.tensor_scalar(y, y, hrs[:, 1:2], None, ALU.mult))
                else:
                    C(v.scalar_tensor_tensor(y, y, hrs[:, 1:2], gpe[:, 1, 0, :], ALU.mult, ALU.mult))

            def rope_keys(k):
                if k != 0:
                    return
                y = ckvS[:, 0:TT, 256:320].unsqueeze(2)
                s = sqS[:, 0:TT * 64].rearrange("p (t h e) -> p t h e", t=TT, h=1)
                rope64(y, 1, range(TT), 1, s)
                v.tensor_tensor(y, y, s, ALU.add).then_inc(lat_ready, 1)

            st = ST["mla_gate"]
            panel_dve(st, 0, slot=latents_kv)
            panel_dve(st, 1, slot=rope_keys)
            for u in range(2):
                lower("cq", u, *(t[:, 2 * u:2 * u + 2, :] for t in cqT))
            for u in range(2):
                lower("ckv", u, *(t[:, u, :] for t in ckvT))
            for i in range(2, 4):
                panel_dve(st, i)
            st = ST["mla_pair"]

            def pair_norm(p, q, part):
                kn = KL[:, q].rearrange("p t (h e) -> p t h e", h=2)
                x = QP[:, q].rearrange("p t (h e) -> p t h e", h=2)
                xn, xp = x[:, :, :, 0:P], x[:, :, :, P:192]
                if part == 0:
                    dve.wait_ge(acc_free, st.acc + 6 * p + 6)
                    need(dve, pair_ready, p)
                    C(v.tensor_tensor(SQm[:].rearrange("p (t h e) -> p t h e", t=4, h=2), kn, kn, ALU.mult))
                    C(v.tensor_reduce(hss[:, 0:8], SQm[:].rearrange("p (n e) -> p n e", e=P), AX, ALU.add))
                if part == 1:
                    rsqrt((slice(0, 8), hss[:, 0:8], HD, EPS))
                if part == 2:
                    r8 = hrs[:, 0:8].rearrange("p (t h) -> p t h", h=2).unsqueeze(3).broadcast_to([P, 4, 2, P])
                    C.tick(v.tensor_tensor(kn, kn, r8, ALU.mult))
                    sx = SQm[:, 0:TT * QBW].rearrange("p (t h e) -> p t h e", t=TT, h=2)
                    q1 = QP[:, q].rearrange("p t e -> p (t e)")
                    C(v.tensor_tensor(SQm[:, 0:TT * QBW], q1, q1, ALU.mult))
                    C.tick(v.tensor_reduce(hss[:, 0:4], sx[:, :, :, 0:P], AX, ALU.add))
                    C(v.tensor_reduce(hss[:, 8:12], sx[:, :, :, P:192], AX, ALU.add))
                if part == 3:
                    rsqrt((slice(0, 4), hss[:, 0:4], HD, EPS), (slice(8, 12), hss[:, 8:12], 64, EPS))
                if part == 4:
                    r4 = hrs[:, 0:4].rearrange("p (t h) -> p t h", h=2).unsqueeze(3).broadcast_to([P, TT, 2, P])
                    C.tick(v.tensor_tensor(xn, xn, r4, ALU.mult))
                    rp = hrs[:, 8:12].rearrange("p (t h) -> p t h", h=2).unsqueeze(3).broadcast_to([P, TT, 2, 64])
                    C(v.tensor_tensor(xp, xp, rp, ALU.mult))
                    C.tick(v.tensor_tensor(xn, xn, gprod[:].unsqueeze(1).unsqueeze(1).broadcast_to([P, TT, 2, P]), ALU.mult))
                if part == 5:
                    s4 = SQm[:, 0:TT * 2 * 64].rearrange("p (t h e) -> p t h e", t=TT, h=2)
                    rope64(xp, 0, range(TT), 2, s4)
                    v.tensor_tensor(xp, xp, s4, ALU.add).then_inc(pair_ready, 1)

            def mla_step(p, m):
                if m < 4:
                    b = m % 2
                    dve.wait_ge(mla["s_full"], 4 * p + m + 1)
                    v.memset(waited[:], 0.0)
                    v.tensor_tensor_reduce(Sm[:, b, :], PS[:, 6, :], zero[:].broadcast_to([P, 512]), 1.0, -3e38,
                                           ALU.add, ALU.max, mx[:, b:b + 1]).then_inc(mla["s_free"], 1)
                    dve.wait_ge(mla["s_free"], 4 * p + m + 1)
                    v.tensor_scalar(nm[:, b:b + 1], mx[:, b:b + 1], -MLA_SCALE, None,
                                    ALU.mult).then_inc(mla["m_ready"], 1)
                if m >= 2:
                    u = m - 2
                    h, tt, b = u // 2, u % 2, u % 2
                    dve.wait_ge(mla["p_ready"], 4 * p + u + 1)
                    C(v.reciprocal(rden[:, b:b + 1], rs[:, u % 4:u % 4 + 1]))
                    dve.wait_ge(mla["o_full"], 4 * p + u + 1)
                    gate = G1[:, tt, col(2 * p + h, HD, HD)]
                    v.scalar_tensor_tensor(gate, PS[:, 7, 0:HD], rden[:, b:b + 1], gate, ALU.mult,
                                           ALU.mult).then_inc(mla["o_free"], 1)

            def mla_body(b):
                for q in range(2):
                    p = 2 * b + q - 2
                    pair_norm(p + 1, 1 - q, 0)
                    panel_dve(st, b, q, ks=(0,))
                    pair_norm(p + 1, 1 - q, 1)
                    for m in range(6):
                        mla_step(p, m)
                        if m < 4:
                            pair_norm(p + 1, 1 - q, m + 2)
                        if m == 4:
                            panel_dve(st, b, q, ks=(1,))

            panel_dve(st, 0, 0)
            for part in range(6):
                pair_norm(0, 0, part)
                if part in (1, 3):
                    panel_dve(st, 0, 1, ks=(part // 2,))
            counted_loop(dve, (C,), 1, 3, mla_body, (96,))
            mla_body(3)
            for part in range(6):
                pair_norm(7, 1, part)
            for p in range(6, 8):
                for m in range(6):
                    mla_step(p, m)
            for u in range(8):
                lower("og1", u, *(t[:, 2 * u:2 * u + 2, :] for t in og1))
            for j in range(2):
                dve.wait_ge(tr_free[j], TB["gate1"] + 2)
            counted_loop(dve, (C,), 0, 4, lambda i: residual(ST["mla_out"], i, lambda tt, c: gateB1[:, c], 2), (2,))

            def lower_x(part):
                for u in range(8):
                    lower(part, u, *(t[:, 2 * u:2 * u + 2, :] for t in x2))

            lower_x("pool")
            for g in range(4):
                panel_dve(ST["pool_in"], g)
                if g:
                    for u in range(2 * g - 2, 2 * g):
                        lower("band", u, *(t[:, 2 * u:2 * u + 2, :] for t in pT))
            for u in range(6, 8):
                lower("band", u, *(t[:, 2 * u:2 * u + 2, :] for t in pT))
            dve.wait_ge(pool_in_, 32)
            for g in range(4):
                c = slice(g * PW, (g + 1) * PW)
                panel_dve(ST["pool_group"], 0, q=g, evac=lambda tt: v.tensor_tensor(U[:, tt, c], PS[:, tt, :], scaleB[:, c], ALU.mult))
                if g:
                    for u in range(2 * g - 2, 2 * g):
                        lower("py", u, *(t[:, 2 * u:2 * u + 2, :] for t in yT))
            for u in range(6, 8):
                lower("py", u, *(t[:, 2 * u:2 * u + 2, :] for t in yT))

            def part_bn(st, n):
                for tt in range(TT):
                    dve.wait_ge(acc_free, st.acc + 2 * n + tt + 1)
                    v.bn_stats(bn[:, tt, col(n, 1, 1), :].rearrange("p a s -> p (a s)"),
                               X[:, tt, col(n, PW)]).then_inc(part_stats, 1)

            def add_to_x(st, b, factor, q=0):
                n = panel(st, b, q)

                def evac(tt):
                    x = X[:, tt, col(n, PW)]
                    return v.scalar_tensor_tensor(x, x, factor, PS[:, tt, :], ALU.mult, ALU.add)

                panel_dve(st, b, q, evac=evac, after=lambda: part_bn(st, n))

            def layer_norm(part, number):
                dve.wait_ge(part_stats, 8 * (number + 1))
                for tt in range(TT):
                    C.tick(v.bn_aggr(mv[:, tt, :], bn[:, tt]))
                C.wait()
                rsqrt((slice(0, TT), mv[:, :, 1], 1, LN_EPS))
                v.scalar_tensor_tensor(nmr[:], mv[:, :, 0], -1.0, hrs[:, 0:TT], ALU.mult, ALU.mult).then_inc(row_stats, 1)
                for c in range(4):
                    gain_bias(dve, v, 0, number, c)
                    if c and part:
                        lower_piece(part, c - 1)

            def lower_piece(part, c):
                for u in range(2 * c, 2 * c + 2):
                    lower(part, u, *(t[:, 2 * u:2 * u + 2, :] for t in x2))

            each(dve, 0, 4, lambda i: add_to_x(ST["pool_out"], i, ALPHA))

            def mlp(layer, last):
                for half in range(2):
                    up, down = ST[f"up{layer}{half}"], ST[f"down{layer}{half}"]

                    def square(i, k):
                        if k == 0:
                            for tt in range(TT):
                                dve.wait_ge(acc_free, up.acc + 2 * i + tt + 1)
                                v.tensor_tensor(HS[:, tt, :], HS[:, tt, :], HS[:, tt, :], ALU.mult).then_inc(sq_ready, 1)
                        if k == 2:
                            for u in range(2):
                                K = TB[up.name] + i
                                dve.wait_ge(split_hi, HB[up.name] + 2 * i + u + 1)
                                c = slice(4 * i + 2 * u, 4 * i + 2 * u + 2) if isinstance(i, int) else bass.ds(4 * i + 2 * u, 2)
                                v.tensor_tensor(hw[1][:, c, :], PS[:, 4 + u, :].rearrange("p (c t) -> p c t", c=2),
                                                hw[0][:, c, :], ALU.subtract).then_inc(tr_free[u], 1)

                    if half == 0:
                        layer_norm(f"ln{2 * layer}", 2 * layer)
                    panel_dve(up, 0, slot=lambda k: lower_piece(f"ln{2 * layer}", 3) if half == 0 and k == 1 else None)
                    each(dve, 1, 8, lambda i: panel_dve(up, i, slot=lambda k: square(i - 1, k)))
                    factor = ALPHA if half == 0 else 1.0
                    end = last and half == 1

                    def down_panel(i, slot=None, final=False):
                        def evac(tt):
                            x = X[:, tt, col(i, PW)]
                            return v.scalar_tensor_tensor(x, x, factor, PS[:, tt, :], ALU.mult, ALU.add)
                        panel_dve(down, i, evac=evac, slot=slot, final=final,
                                  after=(lambda: part_bn(down, i)) if half == 1 else None)

                    down_panel(0, slot=lambda k: square(7, k))
                    each(dve, 1, 3 if end else 4, down_panel)
                    if end:
                        down_panel(3, final=True)

            mlp(0, False)
            layer_norm("ln1", 1)
            st = ST["qkv"]
            dve.wait_ge(ndm_in, 16)
            for hf in range(2):
                if hf == 0:
                    panel_dve(st, 0, slot=lambda k: lower_piece("ln1", 3) if k == 1 else None)
                each(dve, 9 * hf + 1 - hf, 9 * hf + 9, lambda i: panel_dve(st, i))
                for m in range(10):
                    n = 8 * hf + m
                    if m < 8:
                        s, tt, b = m // 2, m % 2, m % 2
                        nk, k0 = KEYS[tt], (0, KEYS[0])[tt]
                        dve.wait_ge(dil["s_full"], n + 1)
                        for g in range(N_GROUPS):
                            slope = 2.0 ** (-8.0 * (g * N_SLOTS + 4 * hf + s + 1) / (N_GROUPS * N_SLOTS))
                            last = v.scalar_tensor_tensor(
                                SA[:, b, g * TOK:g * TOK + nk], ndm[:, g, k0:k0 + nk], slope / SWA_SCALE,
                                PS[:, 2 + g // 2, g % 2 * TOK:g % 2 * TOK + nk], ALU.mult, ALU.add)
                            if g < 2:
                                C.tick(last)
                        last.then_inc(dil["s_free"], 1)
                        dve.wait_ge(dil["s_free"], n + 1)
                        C.wait()
                        sv = SA[:, b, :].rearrange("p (g t) -> p g t", g=N_GROUPS)[:, :, 0:nk]
                        C(v.tensor_reduce(mx[:, b:b + 1], sv, mybir.AxisListType.XY, ALU.max))
                        v.tensor_scalar(nm[:, b:b + 1], mx[:, b:b + 1], -SWA_SCALE, None, ALU.mult).then_inc(dil["m_ready"], 1)
                    if m >= 2:
                        u = m - 2
                        s, tt, b = u // 2, u % 2, u % 2
                        dve.wait_ge(dil["p_ready"], 8 * hf + u + 1)
                        C(v.reciprocal(rden[:, b:b + 1], rs[:, u % 4:u % 4 + 1]))
                        dve.wait_ge(dil["o_full"], 8 * hf + u + 1)
                        f0 = (4 * hf + s) * HD
                        v.tensor_scalar(OA[:, tt, f0:f0 + HD], PS[:, 7, 0:HD], rden[:, b:b + 1], None,
                                        ALU.mult).then_inc(dil["o_free"], 1)
            for u in range(4):
                lower("ao", u, *(t[:, 2 * u:2 * u + 2, :] for t in oT))

            def out_body(b):
                for q in range(2):
                    add_to_x(ST["attn_out"], b, ALPHA, q)

            each(dve, 0, 2, out_body)
            mlp(1, True)
            layer_norm(None, 3)


def tiles(w):
    k, n = w.shape
    return w.reshape(k // 512, 4, P, n // PW, PW).transpose(3, 0, 2, 1, 4).reshape(-1, P, TW)


def padded(t):
    out = np.zeros((t.shape[0], P, TW), t.dtype)
    out[:, :, :t.shape[2] * t.shape[3]] = t.reshape(t.shape[0], P, -1)
    return out


def weight_stream(i):
    q, kv, hd = D, 512, PW
    w = i["swa_w_in"][0]
    parts = [tiles(i["ada_w"][0]), tiles(w[:, q:q + 2 * kv])]
    for g in range(4):
        parts += [tiles(w[:, g * PW:(g + 1) * PW]), tiles(w[:, q + 2 * kv + g * PW:q + 2 * kv + (g + 1) * PW])]
    out, ada = tiles(i["swa_w_out"][0]), tiles(i["ada_w"][1])
    for p in range(4):
        both = [out[4 * p:4 * p + 4]] + [ada[q:q + 4] for q in range(12 * p, 12 * p + 12, 4)]
        parts.append(np.stack(both, 1).reshape(-1, P, TW))
    w = i["mla_w_in"][0]
    parts.append(tiles(w[:, 0:512]))
    parts.append(padded(w[:, 512:832].reshape(4, 4, P, MLA_KVW).transpose(0, 2, 1, 3)))
    parts.append(tiles(w[:, 832:]))
    qb, kvb = i["mla_w_qb"][0], i["mla_w_kvb"][0]
    for p in range(8):
        parts.append(padded(qb[:, p * QBW:(p + 1) * QBW].reshape(1, 4, P, QBW).transpose(0, 2, 1, 3)))
        parts.append(padded(kvb[:, p * PW:(p + 1) * PW].reshape(1, 2, P, PW).transpose(0, 2, 1, 3)))
    parts.append(tiles(i["mla_w_out"][0]))
    parts.append(tiles(i["pool_w_in_2"][0]))
    parts += [tiles(i["pool_w_group_2"][0, g]) for g in range(4)]
    parts.append(tiles(i["pool_w_out_2"][0]))

    def mlp(l):
        up, down = i["mlp_w_up_2"][l], i["mlp_w_down_2"][l]
        return [tiles(up[:, :4096]), tiles(down[:4096]), tiles(up[:, 4096:]), tiles(down[4096:])]

    parts += mlp(0)
    w = i["attn_w_qkv_2"][0].reshape(D, 3, N_GROUPS, 2, PW)
    parts += [tiles(w[:, k, g, hf]) for hf in range(2) for g in range(N_GROUPS) for k in range(3)]
    parts.append(tiles(i["attn_w_out_2"][0]))
    parts += mlp(1)
    return np.concatenate(parts)


def rope(rot):
    half = rot // 2
    pos = np.arange(TOK)
    inv = (1.0 / (np.float32(10000.0) ** (np.arange(0, half, 2, dtype=np.float32) / np.float32(half)))).astype(np.float32)
    ar, ac = ((x.astype(np.float32)[:, None] * inv).astype(np.float32) for x in (pos // 64, pos % 64))
    ang = np.concatenate([ar, ar, ac, ac], -1).astype(np.float64)
    sign = np.repeat(np.array([-1.0, 1.0, -1.0, 1.0]), half // 2)
    t = np.stack([np.cos(ang), np.sin(ang) * sign], 1).astype(np.float32)
    return t.reshape(TT, P, 2, rot).transpose(1, 0, 2, 3).copy()


def swap(g):
    n = g.shape[-1] // 4
    return np.concatenate([g[..., n:2 * n], g[..., :n], g[..., 3 * n:], g[..., 2 * n:3 * n]], -1)


def over(v):
    return np.broadcast_to(v, (P,) + v.shape).copy()


def constants():
    f = np.float32
    qi, ki = np.arange(P)[:, None], np.arange(P)[None, :]
    zero = np.zeros((P, P), f)
    upper = np.where(ki >= qi, 0, NEG).astype(f)
    lower = np.where(ki <= qi, 0, NEG).astype(f)
    masks = np.concatenate([upper, zero, zero, zero, lower, zero, zero], 1)
    s, t = np.arange(TOK)[:, None], np.arange(TOK)[None, :]
    bands = np.zeros((TOK, 4, TOK), f)
    for g, w in enumerate(POOL_WINDOWS):
        inside = (s <= t) & (s > t - w)
        bands[:, g] = np.where(inside, 1.0 / np.minimum(t + 1, w), 0.0) - (s == t)
    bands = bands.reshape(TT, P, 4, TOK).transpose(1, 2, 0, 3).copy()
    ndm = np.zeros((P, N_GROUPS, 3 * P), f)
    for g, (w, d) in enumerate(((128, 1), (512, 4), (2048, 16))):
        dist = np.arange(TOK)[:, None] - np.arange(TOK)[None, :]
        ok = (dist >= 0) & (dist % d == 0) & (dist // d <= w // d)
        m = np.where(ok, -dist, NEG).astype(f)
        ndm[:, g, :P] = m[:P, :P]
        ndm[:, g, P:] = m[P:]
    selrow = np.zeros((5, 2, P), f)
    selrow[0:2, 0] = selrow[2:4, 1] = selrow[4] = 1
    return {"ident": np.eye(P, dtype=f), "masks": masks, "bands": bands, "ndm": ndm, "selrow": selrow,
            "selcol": selrow[:, :, 0].copy(), "rope128": rope(HD), "rope64": rope(64)}


def kernel(**inputs):
    import concourse.bacc as bacc
    from concourse.bass_utils import run_bass_kernel_spmd

    i = {k: np.asarray(v) for k, v in inputs.items()}
    pair = lambda q, k: over(np.stack([np.stack([q, swap(q)]), np.stack([k, swap(k)])]))
    cols = lambda v: v.reshape(KC, P).T
    tok = lambda v: v.reshape(TT, P, D).transpose(1, 0, 2)
    ln = np.stack([i["ln_mix_g_2"], i["ln_mix_b_2"], i["ln_mlp_g_2"], i["ln_mlp_b_2"]], 1).reshape(2, 2, 2, D).reshape(4, 1, 2, D)
    arrays = {
        "weights": weight_stream(i),
        "x": np.concatenate([tok(i["x"][0]), tok(i["ctx"][0])], 1),
        "cond": np.stack([cols(i["c"][0]), cols(i["c_ctx"])], 1),
        "normg": np.stack([cols(i["norm_g"][0]), cols(i["norm_g"][1])], 1),
        "ada_b": i["ada_b"][:, None, :],
        "sink": over(i["swa_sink"][0]),
        "gqk": pair(i["swa_q_g"][0], i["swa_k_g"][0]),
        "gpe": pair(i["mla_qn_pe_g"][0], i["mla_kn_pe_g"][0]),
        "gqa": over(i["mla_qa_g"][0]),
        "gkva": over(i["mla_kva_g"][0]),
        "gnope": over(np.stack([i["mla_qn_nope_g"][0], i["mla_kn_nope_g"][0]])),
        "pool_scale": over(i["pool_scale_2"][0]),
        "ln": np.broadcast_to(ln, (4, P, 2, D)),
        **constants(),
    }
    nc = bacc.Bacc("TRN2", target_bir_lowering=False, num_devices=1, dynamic_dma_scratch_size=1024)
    sent, a = {}, {}
    for name, x in arrays.items():
        x = np.ascontiguousarray(x)
        sent[f"in_{name}"] = x
        a[name] = nc.dram_tensor(f"in_{name}", x.shape, mybir.dt.from_np(x.dtype), kind="ExternalInput").ap()
    out = nc.dram_tensor("out_x", (P, TT, D), F32, kind="ExternalOutput").ap()
    program(nc, a, out)
    r = run_bass_kernel_spmd(nc, [sent], core_ids=[0])
    return r.results[0]["out_x"].transpose(1, 0, 2).reshape(1, TOK, D)
```
